# Optimizing a Trainium2 kernel written in Bass

```python
import jax, jax.numpy as jnp
from jax import lax
import numpy as np

D_MODEL = 1024
BATCH = 1
SEQ = 1024
DEPTH = 2
DEC_BATCH = 8
DEC_SEQ = 4
PAST_LEN = 8192
PAGE_SIZE = 128

N_META = 16
N_A_LAYERS = (DEPTH + 1) // 2
N_C_LAYERS = DEPTH // 2
EPS = 1e-6

M_HEADS = 4
M_DK = 256
M_DV = 256
M_WIDTH = M_HEADS * M_DV
M_CHUNK = 64
LRU_WIDTH = 1024
LRU_BLOCKS = 8
LRU_BS = LRU_WIDTH // LRU_BLOCKS
CONV_W = 4
LRU_C = 8.0
G_HEADS = 4
G_DK = 256
G_DV = 512
G_KW = G_HEADS * G_DK
G_VW = G_HEADS * G_DV
G_RANK = 16
G_TAU = 16.0
G_CHUNK = 64

EVEN_SPLITS = (M_HEADS * M_DK, M_HEADS * M_DK, M_WIDTH, M_WIDTH, M_HEADS, M_HEADS, M_WIDTH, LRU_WIDTH, LRU_WIDTH)
EVEN_IN = sum(EVEN_SPLITS)
EVEN_OUT = M_WIDTH + LRU_WIDTH
ODD_SPLITS = (G_KW, G_KW, G_VW, G_VW, G_RANK)
ODD_IN = sum(ODD_SPLITS)

kernel_name = 'hybrid_mlstm_rglru_gla_step'

F32 = jnp.float32

def _split(a, sizes):
    idx = [int(i) for i in np.cumsum(sizes)[:-1]]
    return jnp.split(a, idx, axis=-1)

def _rmsnorm(x, g):
    xf = x.astype(F32)
    y = xf * lax.rsqrt(jnp.mean(xf * xf, axis=-1, keepdims=True) + EPS)
    return y * g.astype(F32)

def _head_norm(h, g, nh):
    B, L, W = h.shape
    hh = h.reshape(B, L, nh, W // nh)
    hh = hh * lax.rsqrt(jnp.mean(hh * hh, axis=-1, keepdims=True) + EPS)
    return hh.reshape(B, L, W) * g.astype(F32)

def _heads(a, nh):
    B, L, W = a.shape
    return a.reshape(B, L, nh, W // nh).transpose(0, 2, 1, 3)

def _chunk_len(L, c):
    return c if L % c == 0 else L

def _to_chunks(a, T):
    B, H, L = a.shape[:3]
    a = a.reshape((B, H, L // T, T) + a.shape[3:])
    return jnp.moveaxis(a, 2, 0)

def _from_chunks(a):
    NC, B, H, T = a.shape[:4]
    return jnp.moveaxis(a, 0, 2).reshape((B, H, NC * T) + a.shape[4:])

def _mlstm_segment(q, k, v, li, lf, C, n, m):
    L = q.shape[2]
    T = _chunk_len(L, M_CHUNK)
    causal = jnp.tril(jnp.ones((T, T), dtype=bool))

    def step(carry, xs):
        C, n, m = carry
        qc, kc, vc, ic, fc = xs
        b = jnp.cumsum(fc, axis=-1)
        inter = b + m[..., None]
        D = b[..., :, None] - b[..., None, :] + ic[..., None, :]
        D = jnp.where(causal, D, -jnp.inf)
        mt = jnp.maximum(inter, jnp.max(D, axis=-1))
        w_inter = jnp.exp(inter - mt)
        s = jnp.einsum('bhtd,bhjd->bhtj', qc, kc) * jnp.exp(D - mt[..., None])
        num = w_inter[..., None] * jnp.einsum('bhvd,bhtd->bhtv', C, qc) + jnp.einsum('bhtj,bhjv->bhtv', s, vc)
        den = w_inter * jnp.einsum('bhd,bhtd->bht', n, qc) + jnp.sum(s, axis=-1)
        h = num / jnp.maximum(jnp.abs(den), jnp.exp(-mt))[..., None]
        m_new = mt[..., -1]
        wC = jnp.exp(inter[..., -1] - m_new)
        wk = jnp.exp(b[..., -1:] - b + ic - m_new[..., None])
        C_new = wC[..., None, None] * C + jnp.einsum('bhjv,bhjd->bhvd', vc * wk[..., None], kc)
        n_new = wC[..., None] * n + jnp.einsum('bhj,bhjd->bhd', wk, kc)
        return (C_new, n_new, m_new), h

    xs = (_to_chunks(q, T), _to_chunks(k, T), _to_chunks(v, T), _to_chunks(li, T), _to_chunks(lf, T))
    (C, n, m), h = lax.scan(step, (C, n, m), xs)
    return _from_chunks(h), (C, n, m)

def _gla_segment(q, k, v, lg, S):
    L = q.shape[2]
    T = _chunk_len(L, G_CHUNK)
    causal = jnp.tril(jnp.ones((T, T), dtype=bool))

    def step(S, xs):
        qc, kc, vc, gc = xs
        b = jnp.cumsum(gc, axis=2)
        bL = b[:, :, -1:]
        qd = qc * jnp.exp(b)
        A = jnp.einsum('bhtd,bhjd->bhtj', qd, kc * jnp.exp(-b))
        A = jnp.where(causal, A, 0.0)
        o = jnp.einsum('bhtd,bhdv->bhtv', qd, S) + jnp.einsum('bhtj,bhjv->bhtv', A, vc)
        S_new = jnp.exp(bL)[:, :, 0, :, None] * S + jnp.einsum('bhjd,bhjv->bhdv', kc * jnp.exp(bL - b), vc)
        return S_new, o

    xs = (_to_chunks(q, T), _to_chunks(k, T), _to_chunks(v, T), _to_chunks(lg, T))
    S, o = lax.scan(step, S, xs)
    return _from_chunks(o), S

def _causal_conv(x, buf, w, b):
    L = x.shape[1]
    xp = jnp.concatenate([buf.astype(F32), x], axis=1)
    wf = w.astype(F32)
    y = b.astype(F32) + wf[0] * xp[:, 0:L]
    for j in range(1, CONV_W):
        y = y + wf[j] * xp[:, j:j + L]
    return y, xp[:, -(CONV_W - 1):]

def _rglru(xc, h0, wa, ba, wx, bx, lam):
    B, L, W = xc.shape
    xb = xc.reshape(B, L, LRU_BLOCKS, LRU_BS)
    r = jax.nn.sigmoid(jnp.einsum('blni,nij->blnj', xb, wa.astype(F32)).reshape(B, L, W) + ba.astype(F32))
    i = jax.nn.sigmoid(jnp.einsum('blni,nij->blnj', xb, wx.astype(F32)).reshape(B, L, W) + bx.astype(F32))
    log_a = -LRU_C * r * jax.nn.softplus(-lam.astype(F32))
    a = jnp.exp(log_a)
    u = jnp.sqrt(-jnp.expm1(2.0 * log_a)) * (i * xc)
    u = u.at[:, 0].add(a[:, 0] * h0.astype(F32))

    def comb(lhs, rhs):
        al, bl = lhs
        ar, br = rhs
        return al * ar, ar * bl + br

    _, h = lax.associative_scan(comb, (a, u), axis=1)
    return h, h[:, -1]

def _even_layer(x, segs, C0, n0, m0, h0, conv0, pre_g, post_g, w_in, w_out, b_i, b_f, m_norm_g,
                conv_w, conv_b, wa, ba, wx, bx, lam):
    B, L, _ = x.shape
    hn = _rmsnorm(x, pre_g).astype(x.dtype)
    proj = jnp.einsum('bld,de->ble', hn, w_in).astype(F32)
    q, k, v, og, ig, fg, z, xr, gr = _split(proj, EVEN_SPLITS)
    qh = _heads(q, M_HEADS)
    kh = _heads(k, M_HEADS) * (M_DK ** -0.5)
    vh = _heads(v, M_HEADS)
    li = (ig + b_i.astype(F32)).transpose(0, 2, 1)
    lf = jax.nn.log_sigmoid(fg + b_f.astype(F32)).transpose(0, 2, 1)
    mstate = (C0.astype(F32), n0.astype(F32), m0.astype(F32))
    hs = []
    off = 0
    for sl in segs:
        idx = slice(off, off + sl)
        hseg, mstate = _mlstm_segment(qh[:, :, idx], kh[:, :, idx], vh[:, :, idx], li[:, :, idx], lf[:, :, idx], *mstate)
        hs.append(hseg)
        off += sl
    hm = jnp.concatenate(hs, axis=2).transpose(0, 2, 1, 3).reshape(B, L, M_WIDTH)
    hm = jax.nn.sigmoid(og) * hm
    hm = _head_norm(hm, m_norm_g, M_HEADS) * jax.nn.silu(z)
    xc, conv_new = _causal_conv(xr, conv0, conv_w, conv_b)
    hl, h_new = _rglru(xc, h0, wa, ba, wx, bx, lam)
    hl = hl * jax.nn.silu(gr)
    mix = jnp.concatenate([hm, hl], axis=-1).astype(x.dtype)
    out = jnp.einsum('ble,ed->bld', mix, w_out)
    y = x + _rmsnorm(out, post_g).astype(x.dtype)
    return y, (mstate[0], mstate[1], mstate[2], h_new, conv_new)

def _odd_layer(x, segs, S0, pre_g, post_g, w_in, w_out, a_up, a_b, g_norm_g):
    B, L, _ = x.shape
    hn = _rmsnorm(x, pre_g).astype(x.dtype)
    proj = jnp.einsum('bld,de->ble', hn, w_in).astype(F32)
    q, k, v, r, alow = _split(proj, ODD_SPLITS)
    qh = _heads(q, G_HEADS) * (G_DK ** -0.5)
    kh = _heads(k, G_HEADS)
    vh = _heads(v, G_HEADS)
    lg = jax.nn.log_sigmoid(jnp.einsum('blr,rk->blk', alow, a_up.astype(F32)) + a_b.astype(F32)) / G_TAU
    gh = _heads(lg, G_HEADS)
    S = S0.astype(F32)
    os_ = []
    off = 0
    for sl in segs:
        idx = slice(off, off + sl)
        oseg, S = _gla_segment(qh[:, :, idx], kh[:, :, idx], vh[:, :, idx], gh[:, :, idx], S)
        os_.append(oseg)
        off += sl
    o = jnp.concatenate(os_, axis=2).transpose(0, 2, 1, 3).reshape(B, L, G_VW)
    o = (_head_norm(o, g_norm_g, G_HEADS) * jax.nn.silu(r)).astype(x.dtype)
    out = jnp.einsum('ble,ed->bld', o, w_out)
    y = x + _rmsnorm(out, post_g).astype(x.dtype)
    return y, S

def setup_inputs(seed: int = 0) -> dict:
    key = jax.random.key(seed)
    ks = jax.random.split(key, 32)
    NA, NC = N_A_LAYERS, N_C_LAYERS

    def nrm(i, shape, scale=1.0):
        return scale * jax.random.normal(ks[i], shape, F32)

    u = jax.random.uniform(ks[20], (NA, LRU_WIDTH), F32, 0.9, 0.999)
    s = u ** (1.0 / LRU_C)
    lam = jnp.log(s) - jnp.log1p(-s)
    return {
        'x_prompt': nrm(0, (BATCH, SEQ, D_MODEL)),
        'x_sample': nrm(1, (DEC_BATCH, DEC_SEQ, D_MODEL)),
        'state_mlstm_C': nrm(2, (NA, DEC_BATCH, M_HEADS, M_DV, M_DK), 0.05),
        'state_mlstm_n': nrm(3, (NA, DEC_BATCH, M_HEADS, M_DK), 0.05),
        'state_mlstm_m': jax.random.uniform(ks[4], (NA, DEC_BATCH, M_HEADS), F32, 0.0, 3.0),
        'state_rglru_h': nrm(5, (NA, DEC_BATCH, LRU_WIDTH), 0.5),
        'state_rglru_conv': nrm(6, (NA, DEC_BATCH, CONV_W - 1, LRU_WIDTH)),
        'state_gla_S': nrm(7, (NC, DEC_BATCH, G_HEADS, G_DK, G_DV), 0.05),
        'meta_tokens': nrm(8, (N_META, D_MODEL)),
        'pre_norm_a': 1.0 + nrm(9, (NA, D_MODEL), 0.05),
        'post_norm_a': 1.0 + nrm(10, (NA, D_MODEL), 0.05),
        'w_in_a': nrm(11, (NA, D_MODEL, EVEN_IN), D_MODEL ** -0.5),
        'w_out_a': nrm(12, (NA, EVEN_OUT, D_MODEL), EVEN_OUT ** -0.5),
        'mlstm_b_i': nrm(13, (NA, M_HEADS), 0.1),
        'mlstm_b_f': jnp.linspace(3.0, 6.0, M_HEADS, dtype=F32)[None] + nrm(14, (NA, M_HEADS), 0.1),
        'mlstm_norm': 1.0 + nrm(15, (NA, M_WIDTH), 0.05),
        'conv_w': nrm(16, (NA, CONV_W, LRU_WIDTH), CONV_W ** -0.5),
        'conv_b': nrm(17, (NA, LRU_WIDTH), 0.02),
        'lru_w_a': nrm(18, (NA, LRU_BLOCKS, LRU_BS, LRU_BS), LRU_BS ** -0.5),
        'lru_b_a': nrm(19, (NA, LRU_WIDTH), 0.02),
        'lru_w_x': nrm(21, (NA, LRU_BLOCKS, LRU_BS, LRU_BS), LRU_BS ** -0.5),
        'lru_b_x': nrm(22, (NA, LRU_WIDTH), 0.02),
        'lru_lambda': lam,
        'pre_norm_c': 1.0 + nrm(23, (NC, D_MODEL), 0.05),
        'post_norm_c': 1.0 + nrm(24, (NC, D_MODEL), 0.05),
        'w_in_c': nrm(25, (NC, D_MODEL, ODD_IN), D_MODEL ** -0.5),
        'w_out_c': nrm(26, (NC, G_VW, D_MODEL), G_VW ** -0.5),
        'gla_alpha_up': nrm(27, (NC, G_RANK, G_KW), G_RANK ** -0.5),
        'gla_alpha_b': 2.0 + nrm(28, (NC, G_KW), 0.1),
        'gla_norm': 1.0 + nrm(29, (NC, G_VW), 0.05),
    }

def reference(x_prompt, x_sample, state_mlstm_C, state_mlstm_n, state_mlstm_m, state_rglru_h, state_rglru_conv,
              state_gla_S, meta_tokens, pre_norm_a, post_norm_a, w_in_a, w_out_a, mlstm_b_i, mlstm_b_f, mlstm_norm,
              conv_w, conv_b, lru_w_a, lru_b_a, lru_w_x, lru_b_x, lru_lambda, pre_norm_c, post_norm_c, w_in_c,
              w_out_c, gla_alpha_up, gla_alpha_b, gla_norm):
    B = x_prompt.shape[0]
    meta = jnp.broadcast_to(meta_tokens[None].astype(x_prompt.dtype), (B, N_META, D_MODEL))
    xp = jnp.concatenate([meta, x_prompt], axis=1)
    segs_p = (N_META, x_prompt.shape[1])
    xs = x_sample
    segs_s = (x_sample.shape[1],)

    pC, pn, pm, ph, pconv, pS = [], [], [], [], [], []
    sC, sn, sm, sh, sconv, sS = [], [], [], [], [], []
    for layer in range(DEPTH):
        j = layer // 2
        if layer % 2 == 0:
            wts = (pre_norm_a[j], post_norm_a[j], w_in_a[j], w_out_a[j], mlstm_b_i[j], mlstm_b_f[j], mlstm_norm[j],
                   conv_w[j], conv_b[j], lru_w_a[j], lru_b_a[j], lru_w_x[j], lru_b_x[j], lru_lambda[j])
            zC = jnp.zeros((B, M_HEADS, M_DV, M_DK), F32)
            zn = jnp.zeros((B, M_HEADS, M_DK), F32)
            zm = jnp.zeros((B, M_HEADS), F32)
            zh = jnp.zeros((B, LRU_WIDTH), F32)
            zconv = jnp.zeros((B, CONV_W - 1, LRU_WIDTH), F32)
            xp, st = _even_layer(xp, segs_p, zC, zn, zm, zh, zconv, *wts)
            pC.append(st[0]); pn.append(st[1]); pm.append(st[2]); ph.append(st[3]); pconv.append(st[4])
            xs, st = _even_layer(xs, segs_s, state_mlstm_C[j], state_mlstm_n[j], state_mlstm_m[j],
                                 state_rglru_h[j], state_rglru_conv[j], *wts)
            sC.append(st[0]); sn.append(st[1]); sm.append(st[2]); sh.append(st[3]); sconv.append(st[4])
        else:
            wts = (pre_norm_c[j], post_norm_c[j], w_in_c[j], w_out_c[j], gla_alpha_up[j], gla_alpha_b[j], gla_norm[j])
            zS = jnp.zeros((B, G_HEADS, G_DK, G_DV), F32)
            xp, S = _odd_layer(xp, segs_p, zS, *wts)
            pS.append(S)
            xs, S = _odd_layer(xs, segs_s, state_gla_S[j], *wts)
            sS.append(S)

    y_prompt = xp[:, N_META:]
    return (y_prompt, xs,
            jnp.stack(pC), jnp.stack(pn), jnp.stack(pm), jnp.stack(ph), jnp.stack(pconv), jnp.stack(pS),
            jnp.stack(sC), jnp.stack(sn), jnp.stack(sm), jnp.stack(sh), jnp.stack(sconv), jnp.stack(sS))


_drawn_inputs = setup_inputs


def setup_inputs(seed=0):
    import zlib

    import numpy as np

    out = dict(_drawn_inputs(seed))
    spreads = {}
    factors = {'lru_b_a': 8.0, 'lru_b_x': 8.0}
    for name, (base, spread) in spreads.items():
        noise = np.random.default_rng([zlib.crc32(name.encode()), seed]).standard_normal(out[name].shape)
        drawn = base * np.exp(spread * noise) if base else spread * noise
        out[name] = __import__('jax').numpy.asarray(drawn.astype(out[name].dtype))
    for name, factor in factors.items():
        out[name] = (out[name] * factor).astype(out[name].dtype)
    return out
```

```python
from contextlib import ExitStack

import concourse.bass as bass
from concourse import mybir

P = 128
D = 1024
KT = D // P
NP_TOK = 1040
NSEQ, SLEN = 8, 4
T = NP_TOK + NSEQ * SLEN
NC = 9
LAST = T - 8 * P
TAIL = NP_TOK - 8 * P
NG = 1 + NSEQ
TC = 358
TP = 3 * TC
H = 4
DK = 256
MV = 257
GV = 512
EPS = 1e-6
NEG = -1e30

A_PAIR0 = 1
A_QKV0 = 17
A_TILES = 57
C_PAIR0 = 1
C_V0 = 17
C_TILES = 49
AF = 10
CF = 12

V_PRE_A, V_PRE_C = 0, 8
V_CONVW, V_CONVB = 16, 48
V_BA, V_BX, V_LAM = 56, 64, 72
V_MNORM, V_GNORM = 80, 88
V_ALPHAB = 104
V_GATEB = 112
NVEC = 113

F32 = mybir.dt.float32
F32R = mybir.dt.float32r
ALU = mybir.AluOpType
ACT = mybir.ActivationFunctionType


class Names:
    pass


def make_alloc(nc, ctx):
    a = Names()
    a.sb = lambda name, shape, dt=F32: ctx.enter_context(nc.sbuf_tensor(name, shape, dt))
    a.ps = lambda name, shape: ctx.enter_context(nc.psum_tensor(name, shape, F32))
    a.sems = []

    def sem(name):
        a.sems.append(nc.alloc_semaphore(name=name))
        return a.sems[-1]
    a.sem = sem
    return a


def clear_semaphores(nc, a):
    nc.clear_and_free_semaphores(a.sems)
    a.sems.clear()
    nc.all_engine_barrier()


def linker(eng, sem, base=0):
    k = [0]

    def link(ins):
        k[0] += 1
        ins.then_inc(sem, 1)
        eng.wait_ge(sem, base + k[0])
    link.count = lambda: k[0]
    return link


def stage_constants(nc, S, vecs_d):
    made = S.a.sem("const_made")
    loaded = S.a.sem("const_loaded")
    with nc.Block() as block:
        @block.sync
        def _(sp):
            sp.dma_start(S.vecs[:], vecs_d).then_inc(loaded, 16)
            sp.wait_ge(loaded, 16)

        @block.gpsimd
        def _(pool):
            link = linker(pool, made)
            link(pool.memset(S.ident[:], 0.0))
            link(pool.affine_select(out=S.ident[:], in_=S.ident[:], compare_op=ALU.not_equal, fill=1.0,
                                    base=0, pattern=[[-1, P]], channel_multiplier=1))
            link(pool.memset(S.sel[:], 0.0))
            link(pool.affine_select(out=S.sel[:], in_=S.sel[:], compare_op=ALU.not_equal, fill=1.0,
                                    base=0, pattern=[[-1, H], [0, P]], channel_multiplier=1))
            link(pool.memset(S.reset[:], 1.0))
            link(pool.memset(S.reset[:, 0:8 * P].rearrange("p (c t) -> p c t", t=P)[:, :, 0:1], 0.0))
            link(pool.memset(S.reset[:, 8 * P:8 * P + 1], 0.0))
            link(pool.memset(S.reset[:, NP_TOK:T].rearrange("p (s t) -> p s t", t=SLEN)[:, :, 0:1], 0.0))
            for m, seen, hidden in ((S.mask_add, 0.0, NEG), (S.mask_add8, 0.0, NEG), (S.mask_one, 1.0, 0.0), (S.mask_one8, 1.0, 0.0)):
                w = m.shape[1]
                link(pool.memset(m[:], seen))
                link(pool.affine_select(out=m[:], in_=m[:], compare_op=ALU.is_ge, fill=hidden,
                                        base=0, pattern=[[1, w]], channel_multiplier=-1))
                if w == LAST:
                    part = m[:, TAIL:LAST].rearrange("p (s t) -> p s t", t=SLEN)
                    link(pool.affine_select(out=part, in_=part, compare_op=ALU.is_ge, fill=hidden,
                                            base=-TAIL, pattern=[[-SLEN, NSEQ], [0, SLEN]], channel_multiplier=1))
            link(pool.memset(S.seq_mask[:], 1.0))
            link(pool.affine_select(out=S.seq_mask[:], in_=S.seq_mask[:], compare_op=ALU.is_ge, fill=0.0,
                                    base=-TAIL, pattern=[[-SLEN, NSEQ]], channel_multiplier=1))
            link(pool.affine_select(out=S.seq_mask[:], in_=S.seq_mask[:], compare_op=ALU.is_ge, fill=0.0,
                                    base=TAIL + SLEN - 1, pattern=[[SLEN, NSEQ]], channel_multiplier=-1))
            link(pool.memset(S.tail_mask[:], 1.0))
            link(pool.affine_select(out=S.tail_mask[:], in_=S.tail_mask[:], compare_op=ALU.is_ge, fill=0.0,
                                    base=TAIL - 1, pattern=[[0, 1]], channel_multiplier=-1))

def stage_norm(nc, S, name, x_d, gcol):
    with ExitStack() as ctx:
        a = make_alloc(nc, ctx)
        xin = [a.sb(f"{name}_xin{s}", [P, D]) for s in range(2)]
        junk = a.sb(f"{name}_junk", [P, D])
        xn = [a.sb(f"{name}_xn{s}", [P, D]) for s in range(2)]
        stat = [a.sb(f"{name}_stat{s}", [P, 4]) for s in range(2)]
        ps = a.ps(f"{name}_ps", [P, 4, 512])
        loaded = [S.a.sem(f"{name}_x_loaded{s}") for s in range(2)]
        rstd_ready = S.a.sem(f"{name}_rstd_ready")
        act_chain = S.a.sem(f"{name}_act_chain")
        xn_ready = S.a.sem(f"{name}_xn_ready")
        turned = S.a.sem(f"{name}_turned")
        hi_ready = S.a.sem(f"{name}_hi_ready")
        lo_ready = S.a.sem(f"{name}_lo_ready")

        def cols(c, rows):
            return bass.ds(c * P, rows)

        with nc.Block() as block:
            @block.sync
            def _(sp):
                def load(c, u, rows, first):
                    if not first:
                        sp.wait_ge(xn_ready, c - 1)
                    sp.dma_start(xin[u][0:rows, :], x_d[bass.ds(c * P, rows), :]).then_inc(loaded[u], 16)
                load(0, 0, P, True)
                load(1, 1, P, True)
                with sp.Fori(1, 4) as i:
                    load(2 * i, 0, P, False)
                    load(2 * i + 1, 1, P, False)
                load(8, 0, LAST, False)

            @block.scalar
            def _(act):
                act.preload_act_table_set('natural_log_exp_and_others')
                link_base = [0]

                def tile(i, u, c, rows, done):
                    st = stat[u]
                    act.wait_ge(loaded[u], 16 * i + 16)
                    base = c * 3
                    act.activation(junk[0:rows, :], xin[u][0:rows, :], ACT.Square,
                                   accum_out=st[0:rows, 0:1]).then_inc(act_chain, 1)
                    act.wait_ge(act_chain, base + 1)
                    act.activation(st[0:rows, 1:2], st[0:rows, 0:1], ACT.Ln, scale=1.0 / D,
                                   bias=S.eps[0:rows, :]).then_inc(act_chain, 1)
                    act.wait_ge(act_chain, base + 2)
                    act.activation(st[0:rows, 2:3], st[0:rows, 1:2], ACT.Exp, scale=-0.5).then_inc(rstd_ready, 1)
                    act.wait_ge(rstd_ready, c + 1)
                    act.activation(st[0:rows, 3:4], st[0:rows, 2:3], ACT.Copy).then_inc(act_chain, 1)
                    act.wait_ge(turned, c + 1)
                    for k in range(KT):
                        ins = act.activation(S.XT_hi[:, k, cols(c, rows)], ps[:, 2 * u + k // 4, bass.ds(k % 4 * P, rows)],
                                             ACT.Copy, scale=S.vecs[:, gcol + k:gcol + k + 1])
                    ins.then_inc(hi_ready, 1)
                with act.Fori(0, 4) as i:
                    tile(i, 0, 2 * i, P, None)
                    tile(i, 1, 2 * i + 1, P, None)
                tile(4, 0, 8, LAST, None)

            @block.vector
            def _(dve):
                def tile(u, c, rows):
                    dve.wait_ge(rstd_ready, c + 1)
                    if not isinstance(c, int) or c >= 2:
                        pass
                    dve.tensor_scalar(xn[u][0:rows, :], xin[u][0:rows, :], stat[u][0:rows, 2:3], None,
                                      ALU.mult).then_inc(xn_ready, 1)
                    dve.wait_ge(hi_ready, c + 1)
                    for k in range(KT):
                        ins = dve.scalar_tensor_tensor(
                            out=S.XT_lo[:, k, cols(c, rows)], in0=ps[:, 2 * u + k // 4, bass.ds(k % 4 * P, rows)],
                            scalar=S.vecs[:, gcol + k:gcol + k + 1],
                            in1=S.XT_hi[:, k, cols(c, rows)].bitcast(F32), op0=ALU.mult, op1=ALU.subtract)
                    ins.then_inc(lo_ready, 1)
                with dve.Fori(0, 4) as i:
                    tile(0, 2 * i, P)
                    tile(1, 2 * i + 1, P)
                tile(0, 8, LAST)
                for t in (S.XT_hi, S.XT_lo):
                    dve.memset(t[:, :, T:TP].bitcast(F32), 0.0)

            @block.tensor
            def _(pe):
                def tile(u, c, rows, first):
                    pe.wait_ge(xn_ready, c + 1)
                    if not first:
                        pe.wait_ge(lo_ready, c - 1)
                    for k in range(KT):
                        ins = pe.transpose(ps[:, 2 * u + k // 4, bass.ds(k % 4 * P, rows)],
                                           xn[u][0:rows, k * P:(k + 1) * P], S.ident[0:rows, 0:rows])
                    ins.then_inc(turned, 1)
                tile(0, 0, P, True)
                tile(1, 1, P, True)
                with pe.Fori(1, 4) as i:
                    tile(0, 2 * i, P, False)
                    tile(1, 2 * i + 1, P, False)
                tile(0, 8, LAST, False)


class Projection:

    def __init__(self, nc, S, a, name, w_d, tiles):
        self.S, self.w_d, self.tiles, self.name = S, w_d, tiles, name
        self.raw = [a.sb(f"{name}_w_raw{s}", [P, KT, P]) for s in range(2)]
        self.hi = [a.sb(f"{name}_w_hi{s}", [P, KT, P], F32R) for s in range(2)]
        self.lo = [a.sb(f"{name}_w_lo{s}", [P, KT, P], F32R) for s in range(2)]
        self.ps = a.ps(f"{name}_ps", [P, 8, 512])
        self.w_loaded = [S.a.sem(f"{name}_w_loaded{s}") for s in range(2)]
        self.w_hi_ready = S.a.sem(f"{name}_w_hi_ready")
        self.w_lo_ready = S.a.sem(f"{name}_w_lo_ready")
        self.gemm_done = S.a.sem(f"{name}_gemm_done")
        self.psum_free = [S.a.sem(f"{name}_psum_free{s}") for s in range(2)]

    def bank(self, s):
        return self.ps[:, 3 * s:3 * s + 3, 0:TC]

    def load(self, sp, n, s):
        if not (isinstance(n, int) and n < 2):
            sp.wait_ge(self.w_lo_ready, n - 1)
        sp.dma_start(self.raw[s][:], self.w_d[bass.ds(n, 1), :, :, :].rearrange("o p k f -> p (o k) f")
                     ).then_inc(self.w_loaded[s], 16)

    def split_hi(self, act, n, s, half):
        act.wait_ge(self.w_loaded[s], 16 * half + 16)
        if not (isinstance(n, int) and n < 2):
            act.wait_ge(self.gemm_done, n - 1)
        act.activation(self.hi[s][:], self.raw[s][:], ACT.Copy).then_inc(self.w_hi_ready, 1)

    def split_lo(self, dve, n, s):
        dve.wait_ge(self.w_hi_ready, n + 1)
        dve.tensor_tensor(self.lo[s][:], self.raw[s][:], self.hi[s][:].bitcast(F32), ALU.subtract
                          ).then_inc(self.w_lo_ready, 1)

    def products(self, pe, n, s, half, hooks={}):
        pe.wait_ge(self.w_lo_ready, n + 1)
        if not (isinstance(n, int) and n < 2):
            pe.wait_ge(self.psum_free[s], half)
        S = self.S
        passes = ((self.hi[s], S.XT_hi), (self.hi[s], S.XT_lo), (self.lo[s], S.XT_hi))
        for k in range(KT):
            if k in hooks:
                hooks[k]()
            for j, (w, x) in enumerate(passes):
                for t in range(3):
                    ins = pe.matmul(self.ps[:, 3 * s + t, 0:TC], w[:, k, :], x[:, k, t * TC:(t + 1) * TC],
                                    start=(k == 0 and j == 0), stop=(k == KT - 1 and j == 2))
        ins.then_inc(self.gemm_done, 1)


def stage_vectors(nc, S):
    chain_a = S.a.sem("vec_act_chain")
    chain_d = S.a.sem("vec_dve_chain")
    lam_abs = S.a.sem("lam_exp_ready")
    with ExitStack() as ctx:
        a = make_alloc(nc, ctx)
        e, w, z, z2, p, m = (a.sb(f"vec_{n}", [P, 8]) for n in ("e", "w", "z", "z2", "p", "m"))
        lam = S.vecs[:, V_LAM:V_LAM + 8]
        with nc.Block() as block:
            @block.scalar
            def _(act):
                act.preload_act_table_set('natural_log_exp_and_others')
                link = linker(act, chain_a)
                link(act.activation(w[:], lam, ACT.Abs))
                act.activation(e[:], w[:], ACT.Exp, scale=-1.0).then_inc(lam_abs, 1)

            @block.vector
            def _(dve):
                link = linker(dve, chain_d)
                dve.memset(S.eps[:], EPS)
                dve.memset(S.tiny[:], 1e-18)
                link(dve.tensor_scalar(m[:], lam, -1.0, 0.0, ALU.mult, ALU.max))
                dve.wait_ge(lam_abs, 1)
                link(dve.tensor_scalar(z[:], e[:], 2.0, None, ALU.add))
                link(dve.reciprocal(p[:], z[:]))
                link(dve.tensor_tensor(z[:], e[:], p[:], ALU.mult))
                link(dve.tensor_tensor(z2[:], z[:], z[:], ALU.mult))
                link(dve.tensor_scalar(p[:], z2[:], 1.0 / 15, 1.0 / 13, ALU.mult, ALU.add))
                for n in (11, 9, 7, 5, 3, 1):
                    link(dve.tensor_tensor(p[:], p[:], z2[:], ALU.mult))
                    link(dve.tensor_scalar(p[:], p[:], 1.0 / n, None, ALU.add))
                link(dve.tensor_tensor(p[:], p[:], z[:], ALU.mult))
                link(dve.scalar_tensor_tensor(out=z[:], in0=p[:], scalar=2.0, in1=m[:], op0=ALU.mult, op1=ALU.add))
                dve.tensor_scalar(S.derived[:, 0, :], z[:], 8.0, None, ALU.mult)
                dve.tensor_scalar(S.derived[:, 1, :], z[:], -8.0, None, ALU.mult)


def stage_project_a(nc, S, w_d, lru_w_d, conv0_d, h0_d, scr_d, lru_d, m0_d, out_conv_p, out_conv_s, out_h_p, out_h_s, out_m):
    with ExitStack() as ctx:
        a = make_alloc(nc, ctx)
        G = Projection(nc, S, a, "pa", w_d, A_TILES)
        stage = [a.sb(f"pa_stage{s}", [P, 3, TC]) for s in range(2)]
        flat = [s[:].rearrange("p a b -> p (a b)") for s in stage]
        xe_p = a.sb("pa_xe_p", [P, 3 + NP_TOK])
        xe_s = a.sb("pa_xe_s", [P, NSEQ, 3 + SLEN])
        xc = a.sb("pa_xc", [P, TP])
        gr_e = a.sb("pa_gate_r", [P, TP])
        gi_e = a.sb("pa_gate_i", [P, TP])
        av = a.sb("pa_decay", [P, T])
        tv = a.sb("pa_tanh", [P, T])
        lv = a.sb("pa_log", [P, T])
        hv = a.sb("pa_h", [P, T])
        silu = a.sb("pa_silu", [P, 3, TC])
        silu_f = silu[:].rearrange("p a b -> p (a b)")
        lout = a.sb("pa_lru_out", [P, T])
        lru_w = a.sb("pa_lru_w", [P, 2, P])
        conv0 = a.sb("pa_conv0", [P, 8, NSEQ, 3])
        h0 = a.sb("pa_h0", [P, 8, NSEQ])
        cp_out = a.sb("pa_conv_p_out", [P, 8, 3])
        cs_out = a.sb("pa_conv_s_out", [P, 8, NSEQ, 3])
        hp_out = a.sb("pa_h_p_out", [P, 8])
        hs_out = a.sb("pa_h_s_out", [P, 8, NSEQ])
        tmp8 = a.sb("pa_tmp8", [P, NSEQ])
        gates = a.sb("pa_gates", [P, TP])
        par = a.sb("pa_scalars", [P, 4])
        rows = a.sb("pa_rows", [P, T])
        m0 = a.sb("pa_m0", [4, NSEQ])
        m_prev = a.sb("pa_m_prev", [4, 17])
        m_out = a.sb("pa_m_out", [4, 9])
        e_last = a.sb("pa_e_last", [4, 17])

        sem = S.a.sem
        small_in = sem("pa_small_in")
        lru_w_in = sem("pa_lru_w_in")
        gates_out = sem("pa_gates_out")
        xr_ready = sem("pa_xr_ready")
        conv_ready = sem("pa_conv_ready")
        lru_gemm = sem("pa_lru_gemm_done")
        gates_ready = sem("pa_gates_ready")
        tanh_ready = sem("pa_tanh_ready")
        decay_ready = sem("pa_decay_ready")
        logs_ready = sem("pa_logs_ready")
        root_log = sem("pa_root_log_ready")
        root_ready = sem("pa_root_ready")
        silu_ready = sem("pa_silu_ready")
        dve_chain = sem("pa_dve_chain")
        scan_done = sem("pa_scan_done")
        lru_out_ready = sem("pa_lru_out_ready")
        lru_spilled = sem("pa_lru_spilled")
        ixc_ready = sem("pa_ixc_ready")
        stage_ready = sem("pa_stage_ready")
        z_ready = sem("pa_z_ready")
        sigmoid_ready = sem("pa_sigmoid_ready")
        spilled = [sem(f"pa_spilled{s}") for s in range(2)]
        finished = sem("pa_outputs_stored")
        row_act = sem("pa_rows_act")
        row_dve = sem("pa_rows_dve")
        rows_ready = sem("pa_rows_ready")
        rows_turned = sem("pa_rows_turned")
        tok_ready = sem("pa_tok_ready")

        PROMPT = slice(0, NP_TOK)
        STARTS = (NP_TOK, SLEN)

        def seq_cols(buf, off):
            return buf[:, NP_TOK:NP_TOK + NSEQ * SLEN].rearrange("p (s t) -> p s t", t=SLEN)[:, :, off]

        def seqs4(row, off):
            return seqs(row)[:, :, off]

        def seqs(buf):
            return buf[:, NP_TOK:NP_TOK + NSEQ * SLEN].rearrange("p (s t) -> p s t", t=SLEN)

        groups = ("q", "k", "v", "og", "z")

        xf, ab, lf, bb, mm = (x[0:4, 0:T] for x in (gr_e, gi_e, av, tv, lv))
        li = gates[0:4, 0:T]

        def chunked(row):
            return row[:, 0:8 * P].rearrange("p (c t) -> p c t", t=P)

        def gate_rows_act(act):
            act.wait_ge(lru_out_ready, 8)
            act.activation(xf, gates[32:36, 0:T], ACT.Copy).then_inc(row_act, 1)
            act.activation(ab, gates[32:36, 0:T], ACT.Abs).then_inc(row_act, 1)
            act.wait_ge(row_act, 2)
            act.activation(ab, ab, ACT.Exp, scale=-1.0).then_inc(row_act, 1)
            act.wait_ge(row_act, 3)
            act.activation(ab, ab, ACT.Ln, bias=1.0).then_inc(row_act, 1)

        def gate_rows_act_out(act):
            act.wait_ge(rows_turned, 1)
            act.activation(S.wc[:], G.ps[:, 6, 0:4 * 17].rearrange("p (h g) -> p h g", g=17), ACT.Exp)
            for bank, off, c0, n in ((6, 80, 0, 5), (7, 0, 5, 4)):
                turned = G.ps[:, bank, off:off + 68 * n].rearrange("p (c r) -> p c r", r=68)
                act.activation(S.tok[:, c0:c0 + n, 0, :], turned[:, :, 0:4], ACT.Copy)
                act.activation(S.tok[:, c0:c0 + n, 1, :], turned[:, :, 32:36], ACT.Exp)
                ins = act.activation(S.tok[:, c0:c0 + n, 2, :], turned[:, :, 64:68], ACT.Exp)
            ins.then_inc(tok_ready, 1)

        def gate_rows_dve(dve):
            link = linker(dve, row_dve)
            link(dve.memset(rows[:], 0.0))
            link(dve.memset(m_prev[:], 0.0))
            dve.wait_ge(row_act, 4)
            link(dve.scalar_tensor_tensor(out=lf, in0=xf, scalar=0.0, in1=ab, op0=ALU.min, op1=ALU.subtract))
            link(dve.tensor_tensor_scan(bb, S.reset[0:4, :], lf, 0.0, ALU.mult, ALU.add))
            link(dve.tensor_tensor_scan(mm[:, PROMPT], lf[:, PROMPT], li[:, PROMPT], 0.0, ALU.add, ALU.max))
            link(dve.tensor_copy(m_prev[:, 9:17], m0[:]))
            for t in range(SLEN):
                before = m_prev[:, 9:17] if t == 0 else seqs4(mm, t - 1)
                link(dve.tensor_tensor(seqs4(mm, t), before, seqs4(lf, t), ALU.add))
                link(dve.tensor_tensor(seqs4(mm, t), seqs4(mm, t), seqs4(li, t), ALU.max))
            link(dve.tensor_copy(m_prev[:, 1:9], chunked(mm)[:, :, P - 1]))
            link(dve.tensor_copy(m_out[:, 0:1], mm[:, NP_TOK - 1:NP_TOK]))
            link(dve.tensor_copy(m_out[:, 1:9], seqs4(mm, SLEN - 1)))
            link(dve.tensor_tensor(S.rrow[:], bb, mm, ALU.subtract))
            dve.tensor_tensor(rows[0:4, :], li, bb, ALU.subtract)
            dve.tensor_tensor(chunked(rows[32:36, :]), chunked(S.rrow[:]),
                              m_prev[:, 0:8].unsqueeze(2).to_broadcast([4, 8, P]), ALU.add)
            dve.tensor_scalar(rows[32:36, 8 * P:NP_TOK], S.rrow[:, 8 * P:NP_TOK], m_prev[:, 8:9], None, ALU.add)
            dve.tensor_tensor(seqs(rows[32:36, :]), seqs(S.rrow[:]),
                              m_prev[:, 9:17].unsqueeze(2).to_broadcast([4, NSEQ, SLEN]), ALU.add)
            dve.tensor_scalar(rows[64:68, :], mm, -1.0, None, ALU.mult)
            dve.tensor_tensor(e_last[:, 0:8], chunked(S.rrow[:])[:, :, P - 1], m_prev[:, 0:8], ALU.add)
            dve.tensor_tensor(e_last[:, 8:9], S.rrow[:, NP_TOK - 1:NP_TOK], m_prev[:, 8:9], ALU.add)
            dve.tensor_tensor(e_last[:, 9:17], seqs4(S.rrow[:], SLEN - 1), m_prev[:, 9:17], ALU.add).then_inc(rows_ready, 1)

        def gate_rows_pe(pe):
            pe.wait_ge(rows_ready, 1)
            pe.wait_ge(gates_ready, 24)
            for h in range(H):
                pe.matmul(G.ps[:, 6, 17 * h:17 * h + 17], S.sel[:, h, :], e_last[:], start=True, stop=True)
            for c in range(NC):
                w = P if c < 8 else LAST
                bank, off = (6, 80 + 68 * c) if c < 5 else (7, 68 * (c - 5))
                ins = pe.transpose(G.ps[0:w, bank, off:off + 68], rows[0:68, c * P:c * P + w], S.ident[0:68, 0:68])
            ins.then_inc(rows_turned, 1)

        with nc.Block() as block:
            @block.sync
            def _(sp):
                sp.dma_start(m0[:], m0_d).then_inc(small_in, 16)
                sp.dma_start(conv0[:], conv0_d).then_inc(small_in, 16)
                sp.dma_start(h0[:], h0_d).then_inc(small_in, 16)
                G.load(sp, 0, 0)
                G.load(sp, 1, 1)
                G.load(sp, 2, 0)

                def pair(i, first):
                    if not first:
                        sp.wait_ge(lru_gemm, 3 * i)
                    sp.dma_start(lru_w[:], lru_w_d[bass.ds(i, 1), :, :, :].rearrange("o i m j -> i (o m) j")
                                 ).then_inc(lru_w_in, 16)
                    G.load(sp, 2 * i + 3, 1)
                    G.load(sp, 2 * i + 4, 0)
                    sp.wait_ge(lru_out_ready, i + 1)
                    dst = lru_d[0:8, :, bass.ds(i, 1), :].rearrange("c p o t -> p c (o t)")
                    sp.dma_start(dst, lout[:, 0:8 * P].rearrange("p (c t) -> p c t", t=P)).then_inc(lru_spilled, 16)
                    sp.dma_start(lru_d[8, :, bass.ds(i, 1), 0:LAST].rearrange("p o t -> p (o t)"),
                                 lout[:, 8 * P:T]).then_inc(lru_spilled, 16)
                pair(0, True)
                with sp.Fori(1, 8) as i:
                    pair(i, False)
                sp.wait_ge(scan_done, 8)
                sp.dma_start(out_conv_p, cp_out[:]).then_inc(finished, 16)
                sp.dma_start(out_conv_s, cs_out[:]).then_inc(finished, 16)
                sp.dma_start(out_h_p, hp_out[:]).then_inc(finished, 16)
                sp.dma_start(out_h_s, hs_out[:]).then_inc(finished, 16)

                def spill(n, s, head, slot_in_head, m):
                    sp.wait_ge(z_ready if slot_in_head >= 8 else stage_ready, m + 1)
                    dst = scr_d[0:8, bass.ds(head, 1), :, slot_in_head, :].rearrange("c o p t -> p (o c) t")
                    sp.dma_start(dst, flat[s][:, 0:8 * P].rearrange("p (c t) -> p c t", t=P)).then_inc(spilled[s], 16)
                    sp.dma_start(scr_d[8, bass.ds(head, 1), :, slot_in_head, 0:LAST].rearrange("o p t -> (o p) t"),
                                 flat[s][:, 8 * P:T]).then_inc(spilled[s], 16)

                def group(g):
                    last = g == len(groups) - 1

                    def two(h, tail):
                        for d in range(2):
                            n = A_QKV0 + 8 * g + 2 * h + d
                            if not tail:
                                G.load(sp, n + 2, (1 + d) % 2)
                            spill(n, (1 + d) % 2, h, 2 * g + d, (0 if last else 8 * g) + 2 * h + d)
                    if last:
                        with sp.Fori(0, 3) as h:
                            two(h, False)
                        two(3, True)
                    else:
                        with sp.Fori(0, 4) as h:
                            two(h, False)
                for g in range(len(groups)):
                    group(g)
                    if g == 0:
                        sp.wait_ge(rows_ready, 1)
                        sp.dma_start(out_m, m_out[:]).then_inc(finished, 16)
                sp.wait_ge(lru_spilled, 16 * 2 * 8)
                for s in range(2):
                    sp.wait_ge(spilled[s], 16 * 2 * 20)
                sp.wait_ge(finished, 80)

            @block.scalar
            def _(act):
                act.preload_act_table_set('natural_log_exp_and_others')
                G.split_hi(act, 0, 0, 0)
                G.split_hi(act, 1, 1, 0)
                act.wait_ge(G.gemm_done, 1)
                for t in range(3):
                    w = TC if t < 2 else T - 2 * TC
                    ins = act.activation(gates[:, t * TC:t * TC + w], G.ps[:, t, 0:w], ACT.Identity,
                                         bias=S.vecs[:, V_GATEB:V_GATEB + 1])
                ins.then_inc(G.psum_free[0], 1)
                G.split_hi(act, 2, 0, 1)

                def pair(i, first):
                    n = 2 * i + 1
                    act.wait_ge(G.gemm_done, n + 1)
                    if not first:
                        act.wait_ge(conv_ready, i)
                    act.activation(xe_p[:, 3:3 + 2 * TC].rearrange("p (a b) -> p a b", b=TC), G.ps[:, 3:5, 0:TC], ACT.Copy)
                    act.activation(xe_p[:, 3 + 2 * TC:3 + NP_TOK], G.ps[:, 5, 0:NP_TOK - 2 * TC], ACT.Copy)
                    act.activation(xe_s[:, :, 3:], G.ps[:, 5, NP_TOK - 2 * TC:T - 2 * TC].rearrange(
                        "p (s t) -> p s t", t=SLEN), ACT.Copy).then_inc(xr_ready, 1)
                    G.split_hi(act, n + 2, 1, i + 1)
                    act.preload_act_table_set('sigmoid_and_others')
                    for t in range(3):
                        act.wait_ge(lru_gemm, 3 * i + t + 1)
                        if t == 0 and not first:
                            act.wait_ge(scan_done, i)
                        act.activation(gr_e[:, t * TC:(t + 1) * TC], G.ps[:, 6, 0:TC], ACT.Sigmoid,
                                       bias=par[:, 0:1])
                        act.activation(gi_e[:, t * TC:(t + 1) * TC], G.ps[:, 7, 0:TC], ACT.Sigmoid,
                                       bias=par[:, 1:2]).then_inc(gates_ready, 1)
                    act.wait_ge(G.gemm_done, n + 2)
                    if not first:
                        act.wait_ge(lru_out_ready, i)
                    act.activation(silu[:], G.bank(0), ACT.Sigmoid).then_inc(silu_ready, 1)
                    G.split_hi(act, n + 3, 0, i + 2)
                    act.wait_ge(gates_ready, 3 * i + 3)
                    act.activation(tv[:], gr_e[:, 0:T], ACT.Tanh, scale=par[:, 2:3]).then_inc(tanh_ready, 1)
                    act.preload_act_table_set('natural_log_exp_and_others')
                    act.activation(av[:], gr_e[:, 0:T], ACT.Exp, scale=par[:, 3:4]).then_inc(decay_ready, 1)
                    act.wait_ge(tanh_ready, i + 1)
                    act.activation(lv[:], tv[:], ACT.Ln, scale=2.0, bias=S.tiny[:])
                    act.wait_ge(decay_ready, i + 1)
                    act.activation(gr_e[:, 0:T], tv[:], ACT.Ln, bias=1.0).then_inc(logs_ready, 1)
                    act.wait_ge(root_log, i + 1)
                    act.activation(lv[:], lv[:], ACT.Exp, scale=0.5).then_inc(root_ready, 1)

                pair(0, True)
                with act.Fori(1, 8) as i:
                    pair(i, False)

                gate_rows_act(act)

                def tile(g, h, d, tail, first):
                    s = (1 + d) % 2
                    n = A_QKV0 + 8 * g + 2 * h + d
                    kind = groups[g]
                    act.wait_ge(G.gemm_done, n + 1)
                    if not first:
                        act.wait_ge(spilled[s], 32 * (4 * g + h))
                    if kind in ("q", "k", "v"):
                        act.activation(stage[s][:], G.bank(s), ACT.Copy, scale=0.0625 if kind == "k" else 1.0
                                       ).then_inc(stage_ready, 1)
                        act.wait_ge(stage_ready, 8 * g + 2 * h + d + 1)
                        act.sem_inc(G.psum_free[s], 1)
                    else:
                        if kind == "og":
                            act.activation(stage[s][:], G.bank(s), ACT.Sigmoid).then_inc(stage_ready, 1)
                            act.wait_ge(stage_ready, 8 * g + 2 * h + d + 1)
                            act.sem_inc(G.psum_free[s], 1)
                        else:
                            act.activation(stage[s][:], G.bank(s), ACT.Sigmoid).then_inc(sigmoid_ready, 1)
                    if not tail:
                        G.split_hi(act, n + 2, s, (A_QKV0 + 8 * g + d) // 2 + 1 + h)

                for g in range(len(groups)):
                    last = g == len(groups) - 1
                    if g == 0:
                        for d in range(2):
                            tile(g, 0, d, False, True)
                    with act.Fori(1 if g == 0 else 0, 3 if last else 4) as h:
                        for d in range(2):
                            tile(g, h, d, False, False)
                    if last:
                        for d in range(2):
                            tile(g, 3, d, True, False)
                    if g == 1:
                        gate_rows_act_out(act)

            @block.vector
            def _(dve):
                dve.memset(xe_p[:, 0:3], 0.0)
                dve.memset(xc[:, T:TP], 0.0)
                G.split_lo(dve, 0, 0)
                G.split_lo(dve, 1, 1)
                G.split_lo(dve, 2, 0)
                dve.wait_ge(small_in, 48)

                def pair(i, first):
                    n = 2 * i + 1
                    K = LRU_DVE_STEPS
                    link = linker(dve, dve_chain, i * K)
                    cw = [S.vecs[:, bass.ds(V_CONVW + j * 8 + i, 1)] for j in range(4)]
                    cb = S.vecs[:, bass.ds(V_CONVB + i, 1)]
                    dve.tensor_copy(xe_s[:, :, 0:3], conv0[:, bass.ds(i, 1), :, :].rearrange("p o s j -> p (o s) j"))
                    dve.wait_ge(xr_ready, i + 1)
                    dve.sem_inc(G.psum_free[1], 1)
                    dve.tensor_copy(par[:, 0:2], S.vecs[:, V_BA:V_BA + 16].rearrange("p (m i) -> p m i", i=8)[:, :, bass.ds(i, 1)]
                                    .rearrange("p m o -> p (m o)"))
                    dve.tensor_copy(par[:, 2:4], S.derived[:, :, bass.ds(i, 1)].rearrange("p m o -> p (m o)"))
                    link(dve.tensor_scalar(xc[:, 0:NP_TOK], xe_p[:, 0:NP_TOK], cw[0], cb, ALU.mult, ALU.add))
                    link(dve.tensor_scalar(seqs(xc), xe_s[:, :, 0:SLEN], cw[0], cb, ALU.mult, ALU.add))
                    for j in range(1, 4):
                        link(dve.scalar_tensor_tensor(out=xc[:, 0:NP_TOK], in0=xe_p[:, j:j + NP_TOK], scalar=cw[j],
                                                      in1=xc[:, 0:NP_TOK], op0=ALU.mult, op1=ALU.add))
                        link(dve.scalar_tensor_tensor(out=seqs(xc), in0=xe_s[:, :, j:j + SLEN], scalar=cw[j],
                                                      in1=seqs(xc), op0=ALU.mult, op1=ALU.add))
                    dve.tensor_copy(cp_out[:, bass.ds(i, 1), :].rearrange("p o j -> p (o j)"), xe_p[:, NP_TOK:NP_TOK + 3])
                    dve.tensor_copy(cs_out[:, bass.ds(i, 1), :, :].rearrange("p o s j -> p (o s) j"),
                                    xe_s[:, :, SLEN:SLEN + 3]).then_inc(conv_ready, 1)
                    G.split_lo(dve, n + 2, 1)
                    dve.wait_ge(silu_ready, i + 1)
                    dve.tensor_tensor(silu[:], G.bank(0), silu[:], ALU.mult).then_inc(G.psum_free[0], 1)
                    G.split_lo(dve, n + 3, 0)
                    dve.wait_ge(logs_ready, i + 1)
                    dve.tensor_tensor(lv[:], lv[:], gr_e[:, 0:T], ALU.subtract).then_inc(root_log, 1)
                    dve.wait_ge(ixc_ready, i + 1)
                    dve.wait_ge(root_ready, i + 1)
                    link(dve.tensor_tensor(lv[:], lv[:], gi_e[:, 0:T], ALU.mult))
                    dve.wait_ge(decay_ready, i + 1)
                    link(dve.tensor_tensor(tmp8[:], seq_cols(av, 0), h0[:, bass.ds(i, 1), :].rearrange("p o s -> p (o s)"), ALU.mult))
                    link(dve.tensor_tensor(seq_cols(lv, 0), seq_cols(lv, 0), tmp8[:], ALU.add))
                    link(dve.memset(seq_cols(av, 0), 0.0))
                    link(dve.tensor_tensor_scan(hv[:], av[:], lv[:], 0.0, ALU.mult, ALU.add))
                    dve.tensor_copy(hp_out[:, bass.ds(i, 1)], hv[:, NP_TOK - 1:NP_TOK])
                    dve.tensor_copy(hs_out[:, bass.ds(i, 1), :].rearrange("p o s -> p (o s)"),
                                    seq_cols(hv, SLEN - 1)).then_inc(scan_done, 1)
                    if not first:
                        dve.wait_ge(lru_spilled, 32 * i)
                    dve.tensor_tensor(lout[:], hv[:], silu_f[:, 0:T], ALU.mult).then_inc(lru_out_ready, 1)
                    assert link.count() == K, link.count()

                pair(0, True)
                with dve.Fori(1, 8) as i:
                    pair(i, False)

                gate_rows_dve(dve)

                def tile(g, h, d, tail):
                    s = (1 + d) % 2
                    n = A_QKV0 + 8 * g + 2 * h + d
                    kind = groups[g]
                    if kind == "z":
                        dve.wait_ge(sigmoid_ready, 2 * h + d + 1)
                        dve.scalar_tensor_tensor(out=stage[s][:], in0=G.bank(s), scalar=S.vecs[:, bass.ds(V_MNORM + 2 * h + d, 1)],
                                                     in1=stage[s][:], op0=ALU.mult, op1=ALU.mult).then_inc(z_ready, 1)
                        dve.wait_ge(z_ready, 2 * h + d + 1)
                        dve.sem_inc(G.psum_free[s], 1)
                    if not tail:
                        G.split_lo(dve, n + 2, s)
                for g in range(len(groups)):
                    last = g == len(groups) - 1
                    with dve.Fori(0, 3 if last else 4) as h:
                        for d in range(2):
                            tile(g, h, d, False)
                    if last:
                        for d in range(2):
                            tile(g, 3, d, True)

            @block.gpsimd
            def _(pool):
                with pool.Fori(0, 8) as i:
                    pool.wait_ge(gates_ready, 3 * i + 3)
                    pool.tensor_tensor(gi_e[:, 0:T], gi_e[:, 0:T], xc[:, 0:T], ALU.mult).then_inc(ixc_ready, 1)

            @block.tensor
            def _(pe):
                G.products(pe, 0, 0, 0)

                def gate_round(i, t):
                    def go():
                        if t == 0:
                            pe.wait_ge(conv_ready, i + 1)
                            pe.wait_ge(lru_w_in, 16 * i + 16)
                        if not (isinstance(i, int) and i == 0 and t == 0):
                            pe.wait_ge(gates_ready, 3 * i + t)
                        for m in range(2):
                            ins = pe.matmul(G.ps[:, 6 + m, 0:TC], lru_w[:, m, :], xc[:, t * TC:(t + 1) * TC],
                                            start=True, stop=True)
                        ins.then_inc(lru_gemm, 1)
                    return go

                def pair(i):
                    G.products(pe, 2 * i + 1, 1, i)
                    G.products(pe, 2 * i + 2, 0, i + 1, {5: gate_round(i, 0), 6: gate_round(i, 1), 7: gate_round(i, 2)})
                pair(0)
                with pe.Fori(1, 8) as i:
                    pair(i)

                for g in range(len(groups)):
                    if g == 1:
                        gate_rows_pe(pe)
                    with pe.Fori(0, 4) as h:
                        for d in range(2):
                            G.products(pe, A_QKV0 + 8 * g + 2 * h + d, (1 + d) % 2, (A_QKV0 + 8 * g + d) // 2 + h)


LRU_DVE_STEPS = 13


class OutProjection:

    def __init__(self, S, a, name, w_d, layer, x_d, y_d):
        self.S, self.w_d, self.x_d, self.y_d = S, w_d, x_d, y_d
        self.w_hi = a.sb(f"{name}_wout_hi", [P, 16, D], F32R)
        self.w_lo = a.sb(f"{name}_wout_lo", [P, 16, D], F32R)
        self.m_hi = a.sb(f"{name}_mix_hi", [P, 16, P], F32R)
        self.m_lo = a.sb(f"{name}_mix_lo", [P, 16, P], F32R)
        self.xres = a.sb(f"{name}_xres", [P, D])
        self.yb = a.sb(f"{name}_yb", [P, D])
        self.raw = [self.xres, self.yb]
        self.post = a.sb(f"{name}_post", [P, D])
        self.stat = a.sb(f"{name}_post_stat", [P, 6])
        self.layer = layer
        sem = S.a.sem
        self.w_in = [sem(f"{name}_wout_in{s}") for s in range(2)]
        self.w_hi_ready = sem(f"{name}_wout_hi_ready")
        self.w_ready = sem(f"{name}_wout_ready")
        self.post_in = sem(f"{name}_post_in")
        self.x_in = sem(f"{name}_xres_in")
        self.out_done = sem(f"{name}_out_done")
        self.squares = sem(f"{name}_squares")
        self.sq_sum = sem(f"{name}_square_sum")
        self.post_ln = sem(f"{name}_post_ln")
        self.post_rstd = sem(f"{name}_post_rstd")
        self.out_read = sem(f"{name}_out_read")
        self.y_ready = sem(f"{name}_y_ready")
        self.y_stored = sem(f"{name}_y_stored")

    def load_w(self, sp, e, s):
        if not (isinstance(e, int) and e < 2):
            sp.wait_ge(self.w_ready, e - 1)
        sp.dma_start(self.raw[s][:], self.w_d[:, bass.ds(e, 1), :].rearrange("p e n -> p (e n)")).then_inc(self.w_in[s], 16)

    def split_w_hi(self, act, i, s):
        act.wait_ge(self.w_in[s], 16 * i + 16)
        act.activation(self.w_hi[:, bass.ds(2 * i + s, 1), :].rearrange("p e n -> p (e n)"), self.raw[s][:], ACT.Copy
                       ).then_inc(self.w_hi_ready, 1)

    def split_w_lo(self, dve, i, s):
        dve.wait_ge(self.w_hi_ready, 2 * i + s + 1)
        e = bass.ds(2 * i + s, 1)
        dve.tensor_tensor(self.w_lo[:, e, :].rearrange("p e n -> p (e n)"), self.raw[s][:],
                          self.w_hi[:, e, :].bitcast(F32).rearrange("p e n -> p (e n)"), ALU.subtract).then_inc(self.w_ready, 1)

    def products(self, pe, ps, e, first, last):
        for half in range(2):
            cols = slice(half * 512, half * 512 + 512)
            for j, (m, w) in enumerate(((self.m_hi, self.w_hi), (self.m_hi, self.w_lo), (self.m_lo, self.w_hi))):
                ins = pe.matmul(ps[:, 6 + half, :], m[:, e, :], w[:, e, cols], start=first and j == 0, stop=last and j == 2)
        if last:
            ins.then_inc(self.out_done, 1)

    def post_act(self, act, ps, c, rows):
        st = self.stat
        act.wait_ge(self.out_done, c + 1)
        for half in range(2):
            ins = act.activation(self.junk[0:rows, :], ps[0:rows, 6 + half, :], ACT.Square,
                                 accum_out=st[0:rows, half:half + 1])
            ins.then_inc(self.squares, 1)
            act.wait_ge(self.squares, 2 * c + half + 1)
        act.wait_ge(self.sq_sum, c + 1)
        act.activation(st[0:rows, 3:4], st[0:rows, 2:3], ACT.Ln, scale=1.0 / D, bias=self.S.eps[0:rows, :]).then_inc(self.post_ln, 1)
        act.wait_ge(self.post_ln, c + 1)
        act.activation(st[0:rows, 4:5], st[0:rows, 3:4], ACT.Exp, scale=-0.5).then_inc(self.post_rstd, 1)

    def post_dve(self, dve, ps, c, rows, first):
        st = self.stat
        dve.wait_ge(self.squares, 2 * c + 2)
        dve.tensor_tensor(st[0:rows, 2:3], st[0:rows, 0:1], st[0:rows, 1:2], ALU.add).then_inc(self.sq_sum, 1)
        if first:
            dve.wait_ge(self.post_in, 16)
        else:
            dve.wait_ge(self.y_stored, 16 * c)
        dve.wait_ge(self.post_rstd, c + 1)
        for half in range(2):
            cols = slice(half * 512, half * 512 + 512)
            ins = dve.scalar_tensor_tensor(out=self.yb[0:rows, cols], in0=ps[0:rows, 6 + half, :], scalar=st[0:rows, 4:5],
                                           in1=self.post[0:rows, cols], op0=ALU.mult, op1=ALU.mult)
        ins.then_inc(self.out_read, 1)

    def post_pool(self, pool, c, rows):
        pool.wait_ge(self.out_read, c + 1)
        pool.wait_ge(self.x_in, 16 * c + 16)
        pool.tensor_tensor(self.yb[0:rows, :], self.yb[0:rows, :], self.xres[0:rows, :], ALU.add).then_inc(self.y_ready, 1)

    def load_x(self, sp, c, rows, first):
        if first:
            sp.wait_ge(self.w_ready, 16)
        else:
            sp.wait_ge(self.y_ready, c)
        sp.dma_start(self.xres[0:rows, :], self.x_d[bass.ds(c * P, rows), :]).then_inc(self.x_in, 16)

    def store_y(self, sp, c, rows):
        sp.wait_ge(self.y_ready, c + 1)
        sp.dma_start(self.y_d[bass.ds(c * P, rows), :], self.yb[0:rows, :]).then_inc(self.y_stored, 16)


NRING = 4


def stage_mix_a(nc, S, scr_d, lru_d, w_d, post_d, x_d, y_d, c0_d, out_cp, out_cs):
    with ExitStack() as ctx:
        a = make_alloc(nc, ctx)
        sem = S.a.sem
        O = OutProjection(S, a, "ma", w_d, 0, x_d, y_d)
        hin = [a.sb(f"ma_hin{s}", [P, AF, P]) for s in range(2)]
        hl = a.sb("ma_hl", [P, 8, P])
        cst = a.sb("ma_state", [P, H, 2, MV])
        vv = [a.sb(f"ma_v{s}", [P, MV + 3]) for s in range(2)]
        og = [a.sb(f"ma_og{s}", [P, 256]) for s in range(2)]
        kw = [a.sb(f"ma_kw{s}", [P, 256]) for s in range(2)]
        ei = a.sb("ma_exponent", [P, P])
        ee = [a.sb(f"ma_decay{s}", [P, P]) for s in range(2)]
        sc = [a.sb(f"ma_scores{s}", [P, P]) for s in range(2)]
        inter = a.sb("ma_inter", [P, MV])
        num = a.sb("ma_num", [P, MV])
        gg = a.sb("ma_gated", [P, 256])
        gn = a.sb("ma_normed", [P, 256])
        mp = a.sb("ma_mix_plain", [P, 256])
        sm = a.sb("ma_small", [P, 8])
        O.junk = a.sb("ma_junk", [P, 512])
        kw8 = a.sb("ma_kw8", [LAST, 2, 256])
        qm = a.sb("ma_q_masked", [P, 2, 480])
        cs = [a.sb(f"ma_sample_state{r}", [P, 2, MV]) for r in range(NRING)]
        ps = a.ps("ma_ps", [P, 8, 512])

        hin_in = [sem(f"ma_hin_in{s}") for s in range(2)]
        hl_in = sem("ma_hl_in")
        hl_hi = sem("ma_hl_hi_ready")
        hl_ready = sem("ma_hl_ready")
        init_done = sem("ma_init_done")
        turned = sem("ma_turned")
        v_ready = sem("ma_v_ready")
        ei_ready = sem("ma_exponent_ready")
        e_ready = sem("ma_decay_ready")
        kw_ready = sem("ma_kw_ready")
        sc_ready = sem("ma_scores_ready")
        b_done = sem("ma_products_done")
        inter_ready = sem("ma_inter_ready")
        num_ready = sem("ma_num_ready")
        state_ready = sem("ma_state_ready")
        den_chain = sem("ma_den_chain")
        gated_ready = sem("ma_gated_ready")
        sq_chain = sem("ma_square_chain")
        rstd_ready = sem("ma_rstd_ready")
        gn_ready = sem("ma_normed_ready")
        c_done = sem("ma_head_turned")
        mp_ready = sem("ma_mix_plain_ready")
        mhi_ready = sem("ma_mix_hi_ready")
        mix_ready = sem("ma_mix_ready")
        qm_ready = sem("ma_q_masked_ready")
        s_in = [sem(f"ma_sample_in{r}") for r in range(NRING)]
        s_out = [sem(f"ma_sample_out{r}") for r in range(NRING)]
        upd_done = sem("ma_update_done")
        kw8_ready = sem("ma_group_keys_ready")
        s_ready = sem("ma_sample_ready")
        s_read = sem("ma_update_read")
        p_stored = sem("ma_prompt_state_stored")
        pool_chain = sem("ma_pool_chain")

        BQ, BK, BV, BO, BZ = (slice(2 * j, 2 * j + 2) for j in range(5))
        LASTS = [TAIL - 1] + [TAIL + SLEN * b + SLEN - 1 for b in range(NSEQ)]

        def not_first(n, least=1):
            return not (isinstance(n, int) and n < least)

        with nc.Block() as block:
            @block.sync
            def _(sp):
                def load_head(n, c, h, s, rows):
                    if not_first(n, 2):
                        sp.wait_ge(mix_ready, n - 1)
                    sp.dma_start(hin[s][:, :, 0:rows], scr_d[bass.ds(c, 1), h, :, :, 0:rows].rearrange("o p f t -> (o p) f t")
                                 ).then_inc(hin_in[s], 16)

                def load_hl(c, rows):
                    if not_first(c):
                        sp.wait_ge(hl_ready, c)
                    sp.dma_start(hl[:, :, 0:rows], lru_d[bass.ds(c, 1), :, :, 0:rows].rearrange("o p f t -> (o p) f t")
                                 ).then_inc(hl_in, 16)
                load_head(0, 0, 0, 0, P)
                load_head(1, 0, 1, 1, P)
                load_hl(0, P)
                for s in range(2):
                    O.load_w(sp, s, s)
                with sp.Fori(1, 8) as i:
                    for s in range(2):
                        O.load_w(sp, 2 * i + s, s)
                sp.dma_start(O.post[:], post_d[:, O.layer, :]).then_inc(O.post_in, 16)
                load_head(2, 0, 2, 0, P)
                load_head(3, 0, 3, 1, P)
                O.load_x(sp, 0, P, True)

                with sp.Fori(1, 8) as c:
                    load_hl(c, P)
                    load_head(4 * c, c, 0, 0, P)
                    load_head(4 * c + 1, c, 1, 1, P)
                    O.store_y(sp, c - 1, P)
                    O.load_x(sp, c, P, False)
                    load_head(4 * c + 2, c, 2, 0, P)
                    load_head(4 * c + 3, c, 3, 1, P)
                load_hl(8, LAST)
                load_head(32, 8, 0, 0, LAST)
                load_head(33, 8, 1, 1, LAST)
                O.store_y(sp, 7, P)
                O.load_x(sp, 8, LAST, False)

                def load_state(m):
                    r = m % NRING
                    if m >= NRING:
                        sp.wait_ge(s_out[r], 16 * (m // NRING))
                    sp.dma_start(cs[r][:], c0_d[m % NSEQ, m // NSEQ]).then_inc(s_in[r], 16)

                def store_state(m):
                    r = m % NRING
                    sp.wait_ge(s_ready, m + 1)
                    sp.dma_start(out_cs[m % NSEQ, m // NSEQ], cs[r][:]).then_inc(s_out[r], 16)
                for m in range(NRING):
                    load_state(m)
                for h in range(H):
                    for b in range(NSEQ):
                        m = h * NSEQ + b
                        store_state(m)
                        if m + NRING < H * NSEQ:
                            load_state(m + NRING)
                    sp.wait_ge(state_ready, 32 + h + 1)
                    sp.dma_start(out_cp[h], cst[:, h, :, :]).then_inc(p_stored, 16)
                    if h < 2:
                        load_head(34 + h, 8, 2 + h, h % 2, LAST)
                O.store_y(sp, 8, LAST)
                sp.wait_ge(O.y_stored, 16 * NC)
                sp.wait_ge(p_stored, 16 * H)
                for r in range(NRING):
                    sp.wait_ge(s_out[r], 16 * (H * NSEQ // NRING))

            @block.tensor
            def _(pe):
                def part_a(n, c, h, s, rows):
                    pe.wait_ge(hin_in[s], 16 * (2 * c + h // 2) + 16)
                    t = hin[s]
                    for d in range(2):
                        pe.transpose(ps[0:rows, 1, 256 + d * P:256 + (d + 1) * P], t[:, 2 + d, 0:rows], S.ident[:])
                        pe.transpose(ps[0:rows, 1, d * P:(d + 1) * P], t[:, 4 + d, 0:rows], S.ident[:])
                        pe.transpose(ps[0:rows, 0, 256 + d * P:256 + (d + 1) * P], t[:, 6 + d, 0:rows], S.ident[:])
                    pe.matmul(ps[0:rows, 0, 128:128 + rows], S.sel[:, h, 0:rows], S.rrow[:, bass.ds(c * P, rows)],
                              start=True, stop=True)
                    for d in range(2):
                        ins = pe.matmul(ps[0:rows, 0, 0:rows], t[:, 2 + d, 0:rows], t[:, d, 0:rows], start=(d == 0), stop=(d == 1))
                    ins.then_inc(turned, 1)

                def part_b(n, c, h, s):
                    if not_first(n):
                        pe.wait_ge(num_ready, n)
                        pe.wait_ge(state_ready, n)
                    else:
                        pe.wait_ge(init_done, 1)
                    for d in range(2):
                        pe.matmul(ps[:, 2, 0:MV], hin[s][:, d, :], cst[:, h, d, :], start=(d == 0), stop=(d == 1))
                    pe.wait_ge(v_ready, n + 1)
                    pe.wait_ge(sc_ready, n + 1)
                    pe.matmul(ps[:, 3, 0:MV], sc[s][:], vv[s][:, 0:MV], start=True, stop=True)
                    pe.wait_ge(kw_ready, n + 1)
                    if not_first(n):
                        pe.wait_ge(mp_ready, n)
                    for d in range(2):
                        ins = pe.matmul(ps[:, 4 + d, 0:MV], kw[s][:, d * P:(d + 1) * P], vv[s][:, 0:MV], start=True, stop=True)
                    ins.then_inc(b_done, 1)

                def part_c(n, s, rows):
                    pe.wait_ge(gn_ready, n + 1)
                    for d in range(2):
                        ins = pe.transpose(ps[:, 4 + d, 384:384 + rows], gn[0:rows, d * P:(d + 1) * P], S.ident[0:rows, 0:rows])
                    ins.then_inc(c_done, 1)

                def out(c, *tiles, waits=()):
                    for e in tiles:
                        if e == 8:
                            pe.wait_ge(hl_ready, c + 1)
                            if not_first(c):
                                pe.wait_ge(O.out_read, c)
                            else:
                                pe.wait_ge(O.w_ready, 16)
                        if e < 8 and e % 2 == 0:
                            pe.wait_ge(mix_ready, 4 * c + e // 2 + 1)
                        O.products(pe, ps, e, e == 8, e == 7)

                def chunk(c):
                    n = 4 * c
                    part_a(n, c, 0, 0, P)
                    part_b(n, c, 0, 0)
                    part_a(n + 1, c, 1, 1, P)
                    out(c, 8, 9)
                    part_c(n, 0, P)
                    out(c, 10)
                    part_b(n + 1, c, 1, 1)
                    out(c, 11)
                    part_a(n + 2, c, 2, 0, P)
                    out(c, 12)
                    part_c(n + 1, 1, P)
                    out(c, 13)
                    part_b(n + 2, c, 2, 0)
                    out(c, 14)
                    part_a(n + 3, c, 3, 1, P)
                    out(c, 15)
                    part_c(n + 2, 0, P)
                    out(c, 0, 1)
                    part_b(n + 3, c, 3, 1)
                    out(c, 2, 3, 4, 5)
                    part_c(n + 3, 1, P)
                    out(c, 6, 7)
                chunk(0)
                with pe.Fori(1, 8) as c:
                    chunk(c)

                pe.wait_ge(O.out_read, 8)
                for h in range(H):
                    n, s = 32 + h, h % 2
                    part_a(n, 8, h, s, LAST)
                    pe.wait_ge(num_ready, n)
                    pe.wait_ge(state_ready, n)
                    pe.wait_ge(mp_ready, n)
                    pe.wait_ge(qm_ready, h + 1)
                    pe.wait_ge(v_ready, n + 1)
                    for g in range(NG):
                        m = h * NSEQ + g - 1
                        r = m % NRING
                        if g:
                            pe.wait_ge(s_in[r], 16 * (m // NRING) + 16)
                        for d in range(2):
                            st = cst[:, h, d, :] if g == 0 else cs[r][:, d, :]
                            pe.matmul(ps[0:LAST, 2, 0:MV], qm[:, d, g * LAST:(g + 1) * LAST], st,
                                      start=(g == 0 and d == 0), stop=(g == NG - 1 and d == 1))
                        u = h * NG + g
                        if u >= 2:
                            pe.wait_ge(s_read, u - 1)
                        pe.wait_ge(kw8_ready, u + 1)
                        for d in range(2):
                            ins = pe.matmul(ps[:, 4 + 2 * (u % 2) + d, 0:MV], kw8[:, u % 2, d * P:(d + 1) * P],
                                            vv[s][0:LAST, 0:MV], start=True, stop=True)
                        ins.then_inc(upd_done, 1)
                    pe.wait_ge(sc_ready, n + 1)
                    pe.matmul(ps[0:LAST, 3, 0:MV], sc[s][0:LAST, 0:LAST], vv[s][0:LAST, 0:MV], start=True, stop=True).then_inc(b_done, 1)
                    part_c(n, s, LAST)
                pe.wait_ge(s_read, H * NG)
                out(8, 8, 9, 10, 11, 12, 13, 14, 15, 0, 1, 2, 3, 4, 5, 6, 7)

            @block.scalar
            def _(act):
                act.preload_act_table_set('natural_log_exp_and_others')
                with act.Fori(0, 8) as i:
                    for s in range(2):
                        O.split_w_hi(act, i, s)

                def hl_split(c, rows):
                    act.wait_ge(hl_in, 16 * c + 16)
                    if not_first(c):
                        act.wait_ge(O.out_done, c)
                    act.activation(O.m_hi[:, 8:16, 0:rows], hl[:, :, 0:rows], ACT.Copy).then_inc(hl_hi, 1)

                def copies(n, s, rows):
                    act.wait_ge(turned, n + 1)
                    if not_first(n, 2):
                        act.wait_ge(b_done, n - 1)
                    act.activation(vv[s][0:rows, 0:256], ps[0:rows, 1, 0:256], ACT.Copy).then_inc(v_ready, 1)
                    act.wait_ge(ei_ready, n + 1)
                    act.activation(ee[s][0:rows, 0:rows], ei[0:rows, 0:rows], ACT.Exp).then_inc(e_ready, 1)
                    act.wait_ge(e_ready, n + 1)

                def part_a(n, s):
                    copies(n, s, P)
                    act.activation(kw[s][:], ps[:, 1, 256:512], ACT.Copy, scale=ee[s][:, P - 1:P]).then_inc(kw_ready, 1)

                def part_b(n, c, h, rows):
                    act.wait_ge(b_done, n + 1)
                    w = S.tok[0:rows, bass.ds(c, 1), 1, h]
                    act.activation(inter[0:rows, :], ps[0:rows, 2, 0:MV], ACT.Copy, scale=w).then_inc(inter_ready, 1)

                def part_c(n, rows):
                    act.wait_ge(gated_ready, n + 1)
                    act.activation(O.junk[0:rows, 0:256], gg[0:rows, :], ACT.Square, accum_out=sm[0:rows, 4:5]).then_inc(sq_chain, 1)
                    act.wait_ge(sq_chain, 2 * n + 1)
                    act.activation(sm[0:rows, 5:6], sm[0:rows, 4:5], ACT.Ln, scale=1.0 / 256, bias=S.eps[0:rows, :]).then_inc(sq_chain, 1)
                    act.wait_ge(sq_chain, 2 * n + 2)
                    act.activation(sm[0:rows, 6:7], sm[0:rows, 5:6], ACT.Exp, scale=-0.5).then_inc(rstd_ready, 1)

                def part_m(n, c, h, rows):
                    act.wait_ge(mp_ready, n + 1)
                    if h == 0 and not_first(c):
                        act.wait_ge(O.out_done, c)
                    act.activation(O.m_hi[:, 2 * h:2 * h + 2, 0:rows], mp[:].rearrange("p (d t) -> p d t", d=2)[:, :, 0:rows], ACT.Copy
                                   ).then_inc(mhi_ready, 1)

                def chunk(c):
                    n = 4 * c
                    hl_split(c, P)
                    part_a(n, 0)
                    part_b(n, c, 0, P)
                    for h in range(1, 4):
                        part_a(n + h, h % 2)
                        part_c(n + h - 1, P)
                        part_m(n + h - 1, c, h - 1, P)
                        part_b(n + h, c, h, P)
                    part_c(n + 3, P)
                    part_m(n + 3, c, 3, P)
                    O.post_act(act, ps, c, P)
                chunk(0)
                with act.Fori(1, 8) as c:
                    chunk(c)
                hl_split(8, LAST)
                for h in range(H):
                    n, s = 32 + h, h % 2
                    copies(n, s, LAST)
                    for g in range(NG):
                        u = h * NG + g
                        if u >= 2:
                            act.wait_ge(upd_done, u - 1)
                        act.activation(kw8[:, u % 2, :], ps[0:LAST, 1, 256:512], ACT.Copy,
                                       scale=ee[s][0:LAST, LASTS[g]:LASTS[g] + 1]).then_inc(kw8_ready, 1)
                    part_b(n, 8, h, LAST)
                    part_c(n, LAST)
                    part_m(n, 8, h, LAST)
                O.post_act(act, ps, 8, LAST)

            @block.vector
            def _(dve):
                for s in range(2):
                    dve.memset(vv[s][:, 256:257], 1.0)
                dve.memset(cst[:], 0.0).then_inc(init_done, 1)
                with dve.Fori(0, 8) as i:
                    for s in range(2):
                        O.split_w_lo(dve, i, s)

                def part_a(n, c, h, s, rows, mask):
                    dve.wait_ge(turned, n + 1)
                    if not_first(n):
                        dve.wait_ge(e_ready, n)
                    dve.scalar_tensor_tensor(out=ei[0:rows, 0:rows], in0=ps[0:rows, 0, 128:128 + rows],
                                             scalar=S.tok[0:rows, bass.ds(c, 1), 0, h], in1=mask[:],
                                             op0=ALU.add, op1=ALU.add).then_inc(ei_ready, 1)
                    dve.tensor_copy(og[s][0:rows, :], ps[0:rows, 0, 256:512])
                    dve.wait_ge(e_ready, n + 1)
                    if not_first(n, 2):
                        dve.wait_ge(b_done, n - 1)
                    dve.tensor_tensor(sc[s][0:rows, 0:rows], ps[0:rows, 0, 0:rows], ee[s][0:rows, 0:rows], ALU.mult).then_inc(sc_ready, 1)

                def part_num(n, rows):
                    dve.wait_ge(inter_ready, n + 1)
                    dve.tensor_tensor(num[0:rows, :], inter[0:rows, :], ps[0:rows, 3, 0:MV], ALU.add).then_inc(num_ready, 1)

                def update(dst, scale, bank):
                    for d in range(2):
                        ins = dve.scalar_tensor_tensor(out=dst[:, d, :], in0=dst[:, d, :], scalar=scale,
                                                       in1=ps[:, bank + d, 0:MV], op0=ALU.mult, op1=ALU.add)
                    return ins

                def part_den(n, c, h, s, rows):
                    link = linker(dve, den_chain, 3 * n)
                    dve.wait_ge(num_ready, n + 1)
                    link(dve.scalar_tensor_tensor(out=sm[0:rows, 0:1], in0=num[0:rows, 256:257], scalar=-1.0,
                                                  in1=num[0:rows, 256:257], op0=ALU.mult, op1=ALU.max))
                    link(dve.tensor_tensor(sm[0:rows, 1:2], sm[0:rows, 0:1], S.tok[0:rows, bass.ds(c, 1), 2, h], ALU.max))
                    link(dve.reciprocal(sm[0:rows, 2:3], sm[0:rows, 1:2]))
                    dve.scalar_tensor_tensor(out=gg[0:rows, :], in0=num[0:rows, 0:256], scalar=sm[0:rows, 2:3],
                                             in1=og[s][0:rows, :], op0=ALU.mult, op1=ALU.mult).then_inc(gated_ready, 1)

                def part_c(n, s, rows):
                    dve.wait_ge(rstd_ready, n + 1)
                    dve.tensor_scalar(gn[0:rows, :], gg[0:rows, :], sm[0:rows, 6:7], None, ALU.mult).then_inc(gn_ready, 1)
                    dve.wait_ge(c_done, n + 1)
                    if not_first(n):
                        dve.wait_ge(mix_ready, n)
                    for d in range(2):
                        ins = dve.tensor_tensor(mp[:, d * P:d * P + rows], ps[:, 4 + d, 384:384 + rows], hin[s][:, 8 + d, 0:rows], ALU.mult)
                    ins.then_inc(mp_ready, 1)

                def part_b(n, c, h, s):
                    part_num(n, P)
                    update(cst[:, h, :, :], S.wc[:, h, bass.ds(c, 1)], 4).then_inc(state_ready, 1)
                    part_den(n, c, h, s, P)

                def chunk(c, first):
                    n = 4 * c
                    part_a(n, c, 0, 0, P, S.mask_add)
                    part_b(n, c, 0, 0)
                    for h in range(1, 4):
                        part_a(n + h, c, h, h % 2, P, S.mask_add)
                        part_c(n + h - 1, (h - 1) % 2, P)
                        part_b(n + h, c, h, h % 2)
                    part_c(n + 3, 1, P)
                    O.post_dve(dve, ps, c, P, first)
                chunk(0, True)
                with dve.Fori(1, 8) as c:
                    chunk(c, False)
                for h in range(H):
                    n, s = 32 + h, h % 2
                    part_a(n, 8, h, s, LAST, S.mask_add8)
                    for g in range(NG):
                        u = h * NG + g
                        dve.wait_ge(upd_done, u + 1)
                        bank = 4 + 2 * (u % 2)
                        if g == 0:
                            update(cst[:, h, :, :], S.wc[:, h, 8:9], bank).then_inc(state_ready, 1)
                            dve.wait_ge(state_ready, n + 1)
                        else:
                            m = u - h - 1
                            update(cs[m % NRING][:], S.wc[:, h, 8 + g:9 + g], bank).then_inc(s_ready, 1)
                            dve.wait_ge(s_ready, m + 1)
                        dve.sem_inc(s_read, 1)
                    part_num(n, LAST)
                    part_den(n, 8, h, s, LAST)
                    part_c(n, s, LAST)
                O.post_dve(dve, ps, 8, LAST, False)

            @block.gpsimd
            def _(pool):
                link = linker(pool, pool_chain)
                link(pool.memset(qm[:], 0.0))

                def lo(c, tiles, plain, rows):
                    return pool.tensor_tensor(O.m_lo[:, tiles, 0:rows], plain, O.m_hi[:, tiles, 0:rows].bitcast(F32), ALU.subtract)

                def chunk(c, rows):
                    pool.wait_ge(hl_hi, c + 1)
                    lo(c, slice(8, 16), hl[:, :, 0:rows], rows).then_inc(hl_ready, 1)
                    for h in range(H):
                        if rows == LAST:
                            pool.wait_ge(hin_in[h % 2], 16 * (16 + h // 2) + 16)
                            if h:
                                pool.wait_ge(upd_done, NG * h)
                            for d in range(2):
                                q = hin[h % 2][:, d, :]
                                pool.tensor_copy(qm[:, d, 0:TAIL], q[:, 0:TAIL])
                                ins = pool.tensor_copy(qm[:, d, 64:480].rearrange("p (s r) -> p s r", r=LAST + SLEN)[:, :, 0:SLEN],
                                                       q[:, TAIL:LAST].rearrange("p (s t) -> p s t", t=SLEN))
                            ins.then_inc(qm_ready, 1)
                        pool.wait_ge(mhi_ready, 4 * c + h + 1)
                        lo(c, slice(2 * h, 2 * h + 2), mp[:].rearrange("p (d t) -> p d t", d=2)[:, :, 0:rows], rows).then_inc(mix_ready, 1)
                    O.post_pool(pool, c, rows)
                with pool.Fori(0, 8) as c:
                    chunk(c, P)
                chunk(8, LAST)


def stage_project_c(nc, S, w_d, a_up_d, scr_d):
    with ExitStack() as ctx:
        a = make_alloc(nc, ctx)
        G = Projection(nc, S, a, "pc", w_d, C_TILES)
        stage = [a.sb(f"pc_stage{s}", [P, 3, TC]) for s in range(2)]
        flat = [s[:].rearrange("p a b -> p (a b)") for s in stage]
        alow = a.sb("pc_alow", [16, TP])
        a_up = a.sb("pc_a_up", [16, P])
        xg = a.sb("pc_gate", [P, TP])
        ab = a.sb("pc_gate_abs", [P, TP])
        bsum = a.sb("pc_decay_sum", [P, T])
        eq = a.sb("pc_exp_q", [P, 3, TC])
        ek = a.sb("pc_exp_k", [P, 3, TC])
        eqf, ekf = (e[:].rearrange("p a b -> p (a b)") for e in (eq, ek))
        gt = a.sb("pc_group_sum", [P, 17])
        par = a.sb("pc_bias", [P, 1])
        mid = a.sb("pc_mid", [P, 8])

        sem = S.a.sem
        alow_ready = sem("pc_alow_ready")
        a_up_in = sem("pc_a_up_in")
        lg_done = sem("pc_log_gate_done")
        lg_read = sem("pc_log_gate_read")
        act_chain = sem("pc_act_chain")
        soft_ready = sem("pc_softplus_ready")
        par_ready = sem("pc_bias_ready")
        dve_chain = sem("pc_dve_chain")
        cent_ready = sem("pc_centred_ready")
        exps_ready = sem("pc_exps_ready")
        qk_ready = sem("pc_qk_ready")
        v_ready = sem("pc_v_ready")
        r_ready = sem("pc_r_ready")
        sigmoid_ready = sem("pc_sigmoid_ready")
        spilled = [sem(f"pc_spilled{s}") for s in range(2)]

        def n_slot(d):
            return (C_V0 + d) % 2

        def seqs(buf):
            return buf[:, NP_TOK:T].rearrange("p (s t) -> p s t", t=SLEN)

        def chunked(buf):
            return buf[:, 0:8 * P].rearrange("p (c t) -> p c t", t=P)

        with nc.Block() as block:
            @block.sync
            def _(sp):
                def spill(ready, m, s, head, f):
                    sp.wait_ge(ready, m + 1)
                    dst = scr_d[0:8, bass.ds(head, 1), :, f, :].rearrange("c o p t -> p (o c) t")
                    sp.dma_start(dst, flat[s][:, 0:8 * P].rearrange("p (c t) -> p c t", t=P)).then_inc(spilled[s], 16)
                    sp.dma_start(scr_d[8, bass.ds(head, 1), :, f, 0:LAST].rearrange("o p t -> (o p) t"),
                                 flat[s][:, 8 * P:T]).then_inc(spilled[s], 16)
                for n in range(3):
                    G.load(sp, n, n % 2)
                with sp.Fori(0, 4) as hh:
                    for d in range(2):
                        i = 2 * hh + d
                        n = 2 * i + 1
                        sp.wait_ge(lg_done, 3 * i)
                        sp.dma_start(a_up[:], a_up_d[:, bass.ds(i, 1), :].rearrange("r o k -> r (o k)")).then_inc(a_up_in, 16)
                        G.load(sp, n + 2, 1)
                        G.load(sp, n + 3, 0)
                        spill(qk_ready, 2 * i, 1, hh, d)
                        spill(qk_ready, 2 * i + 1, 0, hh, 2 + d)

                def two(g, h, d, tail):
                    n = C_V0 + 16 * g + 4 * h + d
                    if not tail:
                        G.load(sp, n + 2, n_slot(d))
                    spill((v_ready, r_ready)[g], 4 * h + d, n_slot(d), h, 4 + 4 * g + d)
                for g in range(2):
                    with sp.Fori(0, 4 - g) as h:
                        for d in range(4):
                            two(g, h, d, False)
                for d in range(4):
                    two(1, 3, d, d >= 2)
                for s in range(2):
                    sp.wait_ge(spilled[s], 32 * 24)

            @block.scalar
            def _(act):
                act.preload_act_table_set('natural_log_exp_and_others')
                G.split_hi(act, 0, 0, 0)
                G.split_hi(act, 1, 1, 0)
                act.wait_ge(G.gemm_done, 1)
                for t in range(3):
                    ins = act.activation(alow[:, t * TC:(t + 1) * TC], G.ps[0:16, t, 0:TC], ACT.Copy)
                ins.then_inc(alow_ready, 1)
                G.split_hi(act, 2, 0, 1)
                with act.Fori(0, 4) as hh:
                    for d in range(2):
                        i = 2 * hh + d
                        n = 2 * i + 1
                        link = linker(act, act_chain, i)
                        ba = par[:]
                        act.wait_ge(par_ready, i + 1)
                        for t in range(3):
                            act.wait_ge(lg_done, 3 * i + t + 1)
                            act.activation(ab[:, t * TC:(t + 1) * TC], G.ps[:, 6 + t % 2, 0:TC], ACT.Abs, bias=ba)
                            act.activation(xg[:, t * TC:(t + 1) * TC], G.ps[:, 6 + t % 2, 0:TC], ACT.Identity, bias=ba
                                           ).then_inc(lg_read, 1)
                        act.wait_ge(lg_read, 3 * i + 3)
                        link(act.activation(ab[:], ab[:], ACT.Exp, scale=-1.0))
                        act.activation(ab[:], ab[:], ACT.Ln, bias=1.0).then_inc(soft_ready, 1)
                        G.split_hi(act, n + 2, 1, i + 1)
                        act.wait_ge(cent_ready, i + 1)
                        act.wait_ge(qk_ready, 2 * i)
                        act.activation(eqf[:, 0:T], bsum[:], ACT.Exp, scale=1.0 / 16)
                        act.activation(S.gf[:, bass.ds(i, 1), :].rearrange("p o g -> p (o g)"), gt[:], ACT.Exp, scale=1.0 / 16)
                        act.activation(ekf[:, 0:T], bsum[:], ACT.Exp, scale=-1.0 / 16).then_inc(exps_ready, 1)
                        G.split_hi(act, n + 3, 0, i + 2)
                act.preload_act_table_set('sigmoid_and_others')

                def tile(g, h, d, tail):
                    s = n_slot(d)
                    n = C_V0 + 16 * g + 4 * h + d
                    act.wait_ge(G.gemm_done, n + 1)
                    act.wait_ge(spilled[s], 32 * (8 + 8 * g + 2 * h + d // 2))
                    if g == 0:
                        act.activation(stage[s][:], G.bank(s), ACT.Copy).then_inc(v_ready, 1)
                        act.wait_ge(v_ready, 4 * h + d + 1)
                        act.sem_inc(G.psum_free[s], 1)
                    else:
                        act.activation(stage[s][:], G.bank(s), ACT.Sigmoid).then_inc(sigmoid_ready, 1)
                    if not tail:
                        G.split_hi(act, n + 2, s, (C_V0 + 16 * g + d) // 2 + 1 + 2 * h)
                for g in range(2):
                    with act.Fori(0, 4 - g) as h:
                        for d in range(4):
                            tile(g, h, d, False)
                for d in range(4):
                    tile(1, 3, d, d >= 2)

            @block.vector
            def _(dve):
                dve.memset(eqf[:, T:TP], 0.0)
                dve.memset(ekf[:, T:TP], 0.0)
                G.split_lo(dve, 0, 0)
                G.split_lo(dve, 1, 1)
                dve.wait_ge(alow_ready, 1)
                dve.sem_inc(G.psum_free[0], 1)
                G.split_lo(dve, 2, 0)
                dve.tensor_copy(par[:], S.vecs[:, V_ALPHAB:V_ALPHAB + 1]).then_inc(par_ready, 1)
                K = 5
                with dve.Fori(0, 4) as hh:
                    for d in range(2):
                        i = 2 * hh + d
                        n = 2 * i + 1
                        link = linker(dve, dve_chain, K * i)
                        dve.wait_ge(soft_ready, i + 1)
                        link(dve.scalar_tensor_tensor(out=xg[:, 0:T], in0=xg[:, 0:T], scalar=0.0, in1=ab[:, 0:T],
                                                      op0=ALU.min, op1=ALU.subtract))
                        dve.wait_ge(exps_ready, i)
                        link(dve.tensor_tensor_scan(bsum[:], S.reset[:], xg[:, 0:T], 0.0, ALU.mult, ALU.add))
                        link(dve.tensor_tensor(gt[:, 0:8], chunked(bsum)[:, :, P - 1], chunked(bsum)[:, :, P // 2 - 1], ALU.subtract))
                        link(dve.tensor_tensor(gt[:, 0:7], gt[:, 0:7], chunked(bsum)[:, 1:8, P // 2 - 1], ALU.add))
                        dve.tensor_copy(gt[:, 8:9], bsum[:, NP_TOK - 1:NP_TOK])
                        dve.tensor_copy(gt[:, 9:17], seqs(bsum)[:, :, SLEN - 1])
                        link(dve.tensor_copy(mid[:], chunked(bsum)[:, :, P // 2 - 1]))
                        assert link.count() == K
                        dve.tensor_tensor(chunked(bsum), chunked(bsum), mid[:].unsqueeze(2).to_broadcast([P, 8, P]), ALU.subtract
                                          ).then_inc(cent_ready, 1)
                        dve.tensor_copy(par[:], S.vecs[:, bass.ds(V_ALPHAB + 1 + i, 1)]).then_inc(par_ready, 1)
                        G.split_lo(dve, n + 2, 1)
                        dve.wait_ge(exps_ready, i + 1)
                        dve.wait_ge(spilled[1], 32 * i)
                        dve.scalar_tensor_tensor(out=stage[1][:], in0=G.bank(1), scalar=DK ** -0.5, in1=eq[:],
                                                 op0=ALU.mult, op1=ALU.mult).then_inc(qk_ready, 1)
                        dve.wait_ge(qk_ready, 2 * i + 1)
                        dve.sem_inc(G.psum_free[1], 1)
                        dve.wait_ge(G.gemm_done, n + 2)
                        dve.wait_ge(spilled[0], 32 * i)
                        dve.tensor_tensor(stage[0][:], G.bank(0), ek[:], ALU.mult).then_inc(qk_ready, 1)
                        dve.wait_ge(qk_ready, 2 * i + 2)
                        dve.sem_inc(G.psum_free[0], 1)
                        G.split_lo(dve, n + 3, 0)

                def tile(g, h, d, tail):
                    s = n_slot(d)
                    n = C_V0 + 16 * g + 4 * h + d
                    if g == 1:
                        dve.wait_ge(sigmoid_ready, 4 * h + d + 1)
                        dve.scalar_tensor_tensor(out=stage[s][:], in0=G.bank(s), scalar=S.vecs[:, bass.ds(V_GNORM + 4 * h + d, 1)],
                                                 in1=stage[s][:], op0=ALU.mult, op1=ALU.mult).then_inc(r_ready, 1)
                        dve.wait_ge(r_ready, 4 * h + d + 1)
                        dve.sem_inc(G.psum_free[s], 1)
                    if not tail:
                        G.split_lo(dve, n + 2, s)
                for g in range(2):
                    with dve.Fori(0, 4 - g) as h:
                        for d in range(4):
                            tile(g, h, d, False)
                for d in range(4):
                    tile(1, 3, d, d >= 2)

            @block.tensor
            def _(pe):
                G.products(pe, 0, 0, 0)

                def gate_round(i, t):
                    def go():
                        if t == 0:
                            pe.wait_ge(alow_ready, 1)
                            pe.wait_ge(a_up_in, 16 * i + 16)
                            pe.wait_ge(lg_read, 3 * i)
                        if t == 2:
                            pe.wait_ge(lg_read, 3 * i + 1)
                        pe.matmul(G.ps[:, 6 + t % 2, 0:TC], a_up[:], alow[:, t * TC:(t + 1) * TC], start=True, stop=True
                                  ).then_inc(lg_done, 1)
                    return go
                with pe.Fori(0, 4) as hh:
                    for d in range(2):
                        i = 2 * hh + d
                        G.products(pe, 2 * i + 1, 1, i, {1: gate_round(i, 0), 2: gate_round(i, 1), 3: gate_round(i, 2)})
                        G.products(pe, 2 * i + 2, 0, i + 1)
                with pe.Fori(0, 8) as h:
                    for d in range(4):
                        G.products(pe, C_V0 + 4 * h + d, n_slot(d), (C_V0 + d) // 2 + 2 * h)


def stage_mix_c(nc, S, scr_d, w_d, post_d, x_d, y_d, s0_d, out_sp, out_ss):
    with ExitStack() as ctx:
        a = make_alloc(nc, ctx)
        sem = S.a.sem
        O = OutProjection(S, a, "mc", w_d, 1, x_d, y_d)
        hin = [a.sb(f"mc_hin{s}", [P, CF, P]) for s in range(2)]
        cst = a.sb("mc_state", [P, H, 2, GV])
        vv = [a.sb(f"mc_v{s}", [P, GV]) for s in range(2)]
        kk = [a.sb(f"mc_k{s}", [P, 256]) for s in range(2)]
        sc = [a.sb(f"mc_scores{s}", [P, P]) for s in range(2)]
        sc8 = a.sb("mc_scores_last", [LAST, LAST])
        gn = a.sb("mc_normed", [P, GV])
        mp = a.sb("mc_mix_plain", [P, GV])
        sm = a.sb("mc_small", [P, 4])
        gfc = a.sb("mc_factors", [P, 8])
        O.junk = mp
        kw8 = a.sb("mc_group_keys", [LAST, 2, 256])
        qm = a.sb("mc_q_masked", [P, 2, 480])
        cs = [a.sb(f"mc_sample_state{r}", [P, 2, GV]) for r in range(CRING)]
        ps = a.ps("mc_ps", [P, 8, 512])

        hin_in = [sem(f"mc_hin_in{s}") for s in range(2)]
        init_done = sem("mc_init_done")
        turned = sem("mc_turned")
        v_ready = sem("mc_v_ready")
        k_ready = sem("mc_k_ready")
        sc_ready = sem("mc_scores_ready")
        b_done = sem("mc_products_done")
        added = sem("mc_state_added")
        gfc_ready = sem("mc_factors_ready")
        state_ready = sem("mc_state_ready")
        sq_chain = sem("mc_square_chain")
        gn_ready = sem("mc_normed_ready")
        c_done = sem("mc_head_turned")
        mp_ready = sem("mc_mix_plain_ready")
        mhi_ready = sem("mc_mix_hi_ready")
        mix_ready = sem("mc_mix_ready")
        head_out = sem("mc_head_out_done")
        qm_ready = sem("mc_q_masked_ready")
        s_in = [sem(f"mc_sample_in{r}") for r in range(CRING)]
        s_out = [sem(f"mc_sample_out{r}") for r in range(CRING)]
        upd_done = sem("mc_update_done")
        s_added = sem("mc_sample_added")
        s_ready = sem("mc_sample_ready")
        p_stored = sem("mc_prompt_state_stored")
        pool_chain = sem("mc_pool_chain")
        kw8_ready = sem("mc_group_keys_ready")

        with nc.Block() as block:
            @block.sync
            def _(sp):
                def load_head(n, c, h, rows, first=False):
                    if not first:
                        sp.wait_ge(mp_ready, n - 1)
                    sp.dma_start(hin[h % 2][:, :, 0:rows], scr_d[bass.ds(c, 1), h, :, :, 0:rows].rearrange("o p f t -> (o p) f t")
                                 ).then_inc(hin_in[h % 2], 16)
                load_head(0, 0, 0, P, True)
                load_head(1, 0, 1, P, True)
                for s in range(2):
                    O.load_w(sp, s, s)
                with sp.Fori(1, 8) as i:
                    for s in range(2):
                        O.load_w(sp, 2 * i + s, s)
                sp.dma_start(O.post[:], post_d[:, O.layer, :]).then_inc(O.post_in, 16)
                load_head(2, 0, 2, P)
                O.load_x(sp, 0, P, True)
                load_head(3, 0, 3, P)

                def rest(c, rows):
                    load_head(4 * c, c, 0, rows)
                    load_head(4 * c + 1, c, 1, rows)
                    O.store_y(sp, c - 1, P)
                    O.load_x(sp, c, rows, False)
                with sp.Fori(1, 8) as c:
                    rest(c, P)
                    load_head(4 * c + 2, c, 2, P)
                    load_head(4 * c + 3, c, 3, P)
                rest(8, LAST)

                def load_state(m):
                    r = m % CRING
                    if m >= CRING:
                        sp.wait_ge(s_out[r], 16 * (m // CRING))
                    sp.dma_start(cs[r][:], s0_d[m % NSEQ, m // NSEQ]).then_inc(s_in[r], 16)

                def store_state(m):
                    r = m % CRING
                    sp.wait_ge(s_ready, m + 1)
                    sp.dma_start(out_ss[m % NSEQ, m // NSEQ], cs[r][:]).then_inc(s_out[r], 16)
                for m in range(CRING):
                    load_state(m)
                for h in range(H):
                    for b in range(NSEQ):
                        m = h * NSEQ + b
                        store_state(m)
                        if m + CRING < H * NSEQ:
                            load_state(m + CRING)
                    sp.wait_ge(state_ready, 32 + h + 1)
                    sp.dma_start(out_sp[h], cst[:, h, :, :]).then_inc(p_stored, 16)
                    if h < 2:
                        load_head(34 + h, 8, 2 + h, LAST)
                O.store_y(sp, 8, LAST)
                sp.wait_ge(O.y_stored, 16 * NC)
                sp.wait_ge(p_stored, 16 * H)
                for r in range(CRING):
                    sp.wait_ge(s_out[r], 16 * len(range(r, H * NSEQ, CRING)))

            @block.tensor
            def _(pe):
                def part_a(n, c, h, rows):
                    s = h % 2
                    pe.wait_ge(hin_in[s], 16 * (2 * c + h // 2) + 16)
                    t = hin[s]
                    for d in range(2):
                        pe.transpose(ps[0:rows, 0, P + d * P:P + (d + 1) * P], t[:, 2 + d, 0:rows], S.ident[:])
                    for d in range(4):
                        pe.transpose(ps[0:rows, 2, d * P:(d + 1) * P], t[:, 4 + d, 0:rows], S.ident[:])
                    for d in range(2):
                        ins = pe.matmul(ps[0:rows, 0, 0:rows], t[:, 2 + d, 0:rows], t[:, d, 0:rows], start=(d == 0), stop=(d == 1))
                    ins.then_inc(turned, 1)

                def part_b(n, h):
                    s = h % 2
                    pe.wait_ge(gn_ready, n)
                    pe.wait_ge(state_ready, n)
                    for d in range(2):
                        pe.matmul(ps[:, 3, :], hin[s][:, d, :], cst[:, h, d, :], start=(d == 0), stop=False)
                    pe.wait_ge(v_ready, n + 1)
                    pe.wait_ge(sc_ready, n + 1)
                    pe.matmul(ps[:, 3, :], sc[s][:], vv[s][:], start=False, stop=True)
                    for d in range(2):
                        ins = pe.matmul(ps[:, 4 + d, :], kk[s][:, d * P:(d + 1) * P], vv[s][:], start=True, stop=True)
                    ins.then_inc(b_done, 1)

                def part_c(n, rows):
                    pe.wait_ge(gn_ready, n + 1)
                    pe.wait_ge(mp_ready, n)
                    for d in range(4):
                        ins = pe.transpose(ps[:, 1, d * rows:(d + 1) * rows], gn[0:rows, d * P:(d + 1) * P], S.ident[0:rows, 0:rows])
                    ins.then_inc(c_done, 1)

                def out(c, h):
                    if h == 0:
                        pe.wait_ge(O.out_read, c)
                    pe.wait_ge(mix_ready, 4 * c + h + 1)
                    for e in range(4 * h, 4 * h + 4):
                        O.products(pe, ps, e, e == 0, e == 15)

                def chunk(c, first, last):
                    for h in range(H):
                        n = 4 * c + h
                        if not (last and h == 3):
                            part_a(n + 1, c + (h == 3), (h + 1) % H, P)
                        if not (first and h == 0):
                            out(c - (h == 0), (h - 1) % H)
                        part_c(n, P)
                        if not (last and h == 3):
                            part_b(n + 1, (h + 1) % H)
                pe.wait_ge(init_done, 1)
                part_a(0, 0, 0, P)
                part_b(0, 0)
                pe.wait_ge(O.w_ready, 16)
                chunk(0, True, False)
                with pe.Fori(1, 7) as c:
                    chunk(c, False, False)
                chunk(7, False, True)
                out(7, 3)
                pe.wait_ge(O.out_read, 8)
                for h in range(H):
                    n, s = 32 + h, h % 2
                    part_a(n, 8, h, LAST)
                    pe.wait_ge(gn_ready, n)
                    pe.wait_ge(state_ready, n)
                    pe.wait_ge(qm_ready, h + 1)
                    pe.wait_ge(v_ready, n + 1)
                    for g in range(NG):
                        m = h * NSEQ + g - 1
                        r = m % CRING
                        if g:
                            pe.wait_ge(s_in[r], 16 * (m // CRING) + 16)
                        for d in range(2):
                            st = cst[:, h, d, :] if g == 0 else cs[r][:, d, :]
                            pe.matmul(ps[0:LAST, 3, :], qm[:, d, g * LAST:(g + 1) * LAST], st,
                                      start=(g == 0 and d == 0), stop=False)
                        u = h * NG + g
                        if u >= 2:
                            pe.wait_ge(s_added, u - 1)
                        pe.wait_ge(kw8_ready, u + 1)
                        for d in range(2):
                            ins = pe.matmul(ps[:, 4 + 2 * (u % 2) + d, :], kw8[:, u % 2, d * P:(d + 1) * P],
                                            vv[s][0:LAST, :], start=True, stop=True)
                        ins.then_inc(upd_done, 1)
                    pe.wait_ge(sc_ready, n + 1)
                    pe.matmul(ps[0:LAST, 3, :], sc8[:], vv[s][0:LAST, :], start=False, stop=True).then_inc(b_done, 1)
                    part_c(n, LAST)
                pe.wait_ge(s_added, H * NG)
                for h in range(H):
                    out(8, h)

            @block.scalar
            def _(act):
                act.preload_act_table_set('natural_log_exp_and_others')
                with act.Fori(0, 8) as i:
                    for s in range(2):
                        O.split_w_hi(act, i, s)

                def part_a(n, s, rows, first=False):
                    act.wait_ge(turned, n + 1)
                    if not first:
                        act.wait_ge(b_done, n - 1)
                    act.activation(vv[s][0:rows, :], ps[0:rows, 2, :], ACT.Copy).then_inc(v_ready, 1)

                def norm(n, rows):
                    act.wait_ge(b_done, n + 1)
                    act.activation(gn[0:rows, :], ps[0:rows, 3, :], ACT.Square, accum_out=sm[0:rows, 0:1]).then_inc(sq_chain, 1)
                    act.wait_ge(sq_chain, 3 * n + 1)
                    act.activation(sm[0:rows, 1:2], sm[0:rows, 0:1], ACT.Ln, scale=1.0 / GV, bias=S.eps[0:rows, :]).then_inc(sq_chain, 1)
                    act.wait_ge(sq_chain, 3 * n + 2)
                    act.activation(sm[0:rows, 2:3], sm[0:rows, 1:2], ACT.Exp, scale=-0.5).then_inc(sq_chain, 1)
                    act.wait_ge(sq_chain, 3 * n + 3)
                    act.activation(gn[0:rows, :], ps[0:rows, 3, :], ACT.Copy, scale=sm[0:rows, 2:3]).then_inc(gn_ready, 1)

                def part_m(n, c, h, rows):
                    act.wait_ge(mp_ready, n + 1)
                    act.wait_ge(O.out_done, c)
                    act.activation(O.m_hi[:, 4 * h:4 * h + 4, 0:rows], mp[:, 0:4 * rows].rearrange("p (d t) -> p d t", d=4), ACT.Copy
                                   ).then_inc(mhi_ready, 1)

                def chunk(c, first, last):
                    for h in range(H):
                        n = 4 * c + h
                        norm(n, P)
                        if not (last and h == 3):
                            part_a(n + 1, (h + 1) % 2, P, first and h == 0)
                        if h == 0 and not first:
                            O.post_act(act, ps, c - 1, P)
                        part_m(n, c, h, P)
                part_a(0, 0, P, True)
                chunk(0, True, False)
                with act.Fori(1, 7) as c:
                    chunk(c, False, False)
                chunk(7, False, True)
                O.post_act(act, ps, 7, P)
                for h in range(H):
                    n = 32 + h
                    part_a(n, h % 2, LAST)
                    for g in range(1, NG):
                        m = h * NSEQ + g - 1
                        act.wait_ge(s_added, h * NG + g + 1)
                        for d in range(2):
                            ins = act.activation(cs[m % CRING][:, d, :], cs[m % CRING][:, d, :], ACT.Copy,
                                                 scale=S.gf[:, 2 * h + d, 8 + g:9 + g])
                        ins.then_inc(s_ready, 1)
                    norm(n, LAST)
                    part_m(n, 8, h, LAST)
                O.post_act(act, ps, 8, LAST)

            @block.vector
            def _(dve):
                dve.memset(sc[0][:], 0.0)
                dve.memset(sc[1][:], 0.0)
                dve.memset(sc8[:], 0.0)
                dve.memset(cst[:], 0.0).then_inc(init_done, 1)
                with dve.Fori(0, 8) as i:
                    for s in range(2):
                        O.split_w_lo(dve, i, s)

                def part_a(n, s, rows, first=False):
                    dve.wait_ge(turned, n + 1)
                    if not first:
                        dve.wait_ge(b_done, n - 1)
                    dve.tensor_copy(kk[s][0:rows, :], ps[0:rows, 0, P:P + 256])
                    dst, mask = (sc[s], S.mask_one) if rows == P else (sc8, S.mask_one8)
                    dve.copy_predicated(dst[:], mask[:].bitcast(mybir.dt.uint32), ps[0:rows, 0, 0:rows]).then_inc(sc_ready, 1)

                def add_state(dst, bank):
                    for d in range(2):
                        ins = dve.tensor_tensor(dst[:, d, :], ps[:, bank + d, :], dst[:, d, :], ALU.add)
                    return ins

                def part_m(n, s, rows):
                    dve.wait_ge(c_done, n + 1)
                    dve.wait_ge(mix_ready, n)
                    dve.tensor_tensor(mp[:, 0:4 * rows].rearrange("p (d t) -> p d t", d=4),
                                      ps[:, 1, 0:4 * rows].rearrange("p (d t) -> p d t", d=4), hin[s][:, 8:12, 0:rows],
                                      ALU.mult).then_inc(mp_ready, 1)

                def chunk(c, first, last):
                    for h in range(H):
                        n = 4 * c + h
                        dve.wait_ge(b_done, n + 1)
                        add_state(cst[:, h, :, :], 4).then_inc(added, 1)
                        if not (last and h == 3):
                            part_a(n + 1, (h + 1) % 2, P, first and h == 0)
                        if h == 0 and not first:
                            O.post_dve(dve, ps, c - 1, P, False)
                        part_m(n, h % 2, P)
                part_a(0, 0, P, True)
                dve.wait_ge(O.post_in, 16)
                chunk(0, True, False)
                with dve.Fori(1, 7) as c:
                    chunk(c, False, False)
                chunk(7, False, True)
                O.post_dve(dve, ps, 7, P, False)
                for h in range(H):
                    n, s = 32 + h, h % 2
                    part_a(n, s, LAST)
                    for g in range(NG + 1):
                        u = h * NG + g
                        if g < NG:
                            if u >= 2:
                                dve.wait_ge(upd_done, u - 1)
                            mask = S.tail_mask[:] if g == 0 else S.seq_mask[:, g - 1:g]
                            dve.tensor_scalar(kw8[:, u % 2, :], ps[0:LAST, 0, P:P + 256], mask, None, ALU.mult).then_inc(kw8_ready, 1)
                        if g:
                            u -= 1
                            dve.wait_ge(upd_done, u + 1)
                            dst = cst[:, h, :, :] if g == 1 else cs[(h * NSEQ + g - 2) % CRING]
                            add_state(dst, 4 + 2 * (u % 2)).then_inc(s_added, 1)
                    part_m(n, s, LAST)
                O.post_dve(dve, ps, 8, LAST, False)

            @block.gpsimd
            def _(pool):
                link = linker(pool, pool_chain)
                link(pool.memset(qm[:], 0.0))

                def take_factors(c):
                    pool.wait_ge(state_ready, 4 * c)
                    pool.tensor_copy(gfc[:], S.gf[:, :, bass.ds(c, 1)].rearrange("p t o -> p (t o)")).then_inc(gfc_ready, 1)
                    pool.wait_ge(gfc_ready, c + 1)

                def scale_state(h):
                    for d in range(2):
                        factor = gfc[:, 2 * h + d:2 * h + d + 1].to_broadcast([P, GV])
                        ins = pool.tensor_tensor(cst[:, h, d, :], cst[:, h, d, :], factor, ALU.mult)
                    ins.then_inc(state_ready, 1)

                def lo(n, h, rows):
                    pool.wait_ge(mhi_ready, n + 1)
                    tiles = slice(4 * h, 4 * h + 4)
                    pool.tensor_tensor(O.m_lo[:, tiles, 0:rows], mp[:, 0:4 * rows].rearrange("p (d t) -> p d t", d=4),
                                       O.m_hi[:, tiles, 0:rows].bitcast(F32), ALU.subtract).then_inc(mix_ready, 1)

                def chunk(c, first):
                    take_factors(c)
                    for h in range(H):
                        n = 4 * c + h
                        pool.wait_ge(added, n + 1)
                        scale_state(h)
                        if h == 0 and not first:
                            O.post_pool(pool, c - 1, P)
                        lo(n, h, P)
                chunk(0, True)
                with pool.Fori(1, 8) as c:
                    chunk(c, False)
                O.post_pool(pool, 7, P)
                take_factors(8)
                for h in range(H):
                    n, s = 32 + h, h % 2
                    pool.wait_ge(hin_in[s], 16 * (16 + h // 2) + 16)
                    if h:
                        pool.wait_ge(upd_done, NG * h)
                    for d in range(2):
                        q = hin[s][:, d, :]
                        pool.tensor_copy(qm[:, d, 0:TAIL], q[:, 0:TAIL])
                        ins = pool.tensor_copy(qm[:, d, 64:480].rearrange("p (s r) -> p s r", r=LAST + SLEN)[:, :, 0:SLEN],
                                               q[:, TAIL:LAST].rearrange("p (s t) -> p s t", t=SLEN))
                    ins.then_inc(qm_ready, 1)
                    pool.wait_ge(s_added, NG * h + 1)
                    scale_state(h)
                    lo(n, h, LAST)
                O.post_pool(pool, 8, LAST)


CRING = 3


def build_program(nc, io, upto=99):
    with ExitStack() as ctx:
        S = Names()
        S.a = make_alloc(nc, ctx)
        sb = S.a.sb
        S.vecs = sb("vecs", [P, NVEC])
        S.derived = sb("derived", [P, 2, 8])
        S.eps = sb("eps", [P, 1])
        S.tiny = sb("tiny", [P, 1])
        S.ident = sb("ident", [P, P])
        S.sel = sb("sel", [H, H, P])
        S.reset = sb("reset", [P, T])
        S.mask_add = sb("mask_add", [P, P])
        S.mask_one = sb("mask_one", [P, P])
        S.mask_add8 = sb("mask_add8", [LAST, LAST])
        S.mask_one8 = sb("mask_one8", [LAST, LAST])
        S.seq_mask = sb("seq_mask", [LAST, NSEQ])
        S.tail_mask = sb("tail_mask", [LAST, 1])
        stage_constants(nc, S, io["vecs"])
        stage_vectors(nc, S)
        scr_a = nc.dram_tensor("scr_a", [NC, H, P, AF, P], F32, kind="Internal").ap()
        scr_l = nc.dram_tensor("scr_l", [NC, P, 8, P], F32, kind="Internal").ap()
        with ExitStack() as actx:
            la = make_alloc(nc, actx)
            S.wc = la.sb("wc", [P, H, 17])
            S.tok = la.sb("tok", [P, NC, 3, H])
            S.rrow = la.sb("rrow", [H, T])
            with ExitStack() as xctx:
                xa = make_alloc(nc, xctx)
                S.XT_hi = xa.sb("a_XT_hi", [P, KT, TP], F32R)
                S.XT_lo = xa.sb("a_XT_lo", [P, KT, TP], F32R)
                stage_norm(nc, S, "na", io["x"], V_PRE_A)
                stage_project_a(nc, S, io["w_a"], io["lru_w"], io["conv0"], io["h0"], scr_a, scr_l, io["m0"],
                                io["conv_p"], io["conv_s"], io["h_p"], io["h_s"], io["m_out"])
            scr_y = nc.dram_tensor("scr_y", [T, D], F32, kind="Internal").ap()
            stage_mix_a(nc, S, scr_a, scr_l, io["w_oa"], io["post"], io["x"], scr_y, io["c0"], io["c_p"], io["c_s"])
        clear_semaphores(nc, S.a)
        with ExitStack() as cctx:
            lc = make_alloc(nc, cctx)
            S.gf = lc.sb("gf", [P, 8, 17])
            scr_c = nc.dram_tensor("scr_c", [NC, H, P, CF, P], F32, kind="Internal").ap()
            with ExitStack() as xctx:
                xa = make_alloc(nc, xctx)
                S.XT_hi = xa.sb("c_XT_hi", [P, KT, TP], F32R)
                S.XT_lo = xa.sb("c_XT_lo", [P, KT, TP], F32R)
                stage_norm(nc, S, "nc", scr_y, V_PRE_C)
                stage_project_c(nc, S, io["w_c"], io["a_up"], scr_c)
            stage_mix_c(nc, S, scr_c, io["w_oc"], io["post"], scr_y, io["y"], io["s0"], io["s_p"], io["s_s"])


def _features(v, n):
    return v.reshape(n, P).T


def _tiles(w, columns):
    import numpy as np
    wz = np.concatenate([w, np.zeros((w.shape[0], 1), w.dtype)], axis=1)
    t = wz[:, columns].reshape(KT, P, -1, P)
    return t.transpose(2, 1, 0, 3)


def lay_out(i):
    import numpy as np
    r = np.arange
    none = -np.ones(P, np.int64)
    gates = none.copy()
    gates[0:4], gates[32:36] = r(4096, 4100), r(4100, 4104)
    cols = [gates]
    for t in range(8):
        cols += [5128 + P * t + r(P), 6152 + P * t + r(P)]
    cols += [r(0, 4096), r(4104, 5128)]
    alow = none.copy()
    alow[0:16] = r(6144, 6160)
    ccols = [alow]
    for t in range(8):
        ccols += [P * t + r(P), 1024 + P * t + r(P)]
    ccols += [r(2048, 6144)]
    vecs = [_features(i["pre_norm_a"][0], 8), _features(i["pre_norm_c"][0], 8)]
    vecs += [_features(i["conv_w"][0, j], 8) for j in range(4)]
    vecs += [_features(i[k][0], n) for k, n in (("conv_b", 8), ("lru_b_a", 8), ("lru_b_x", 8), ("lru_lambda", 8),
                                                ("mlstm_norm", 8), ("gla_norm", 16), ("gla_alpha_b", 8))]
    gb = np.zeros((P, 1), np.float32)
    gb[0:4, 0], gb[32:36, 0] = i["mlstm_b_i"][0], i["mlstm_b_f"][0]
    vecs.append(gb)
    c = i["state_mlstm_C"][0].transpose(0, 1, 3, 2)
    caug = np.concatenate([c, i["state_mlstm_n"][0][..., None]], axis=-1)
    return {
        "x": np.concatenate([i["meta_tokens"], i["x_prompt"][0], i["x_sample"].reshape(-1, D)], axis=0),
        "vecs": np.concatenate(vecs, axis=1),
        "w_a": _tiles(i["w_in_a"][0], np.concatenate(cols)),
        "w_c": _tiles(i["w_in_c"][0], np.concatenate(ccols)),
        "lru_w": np.stack([i["lru_w_a"][0], i["lru_w_x"][0]], axis=2),
        "conv0": i["state_rglru_conv"][0].reshape(NSEQ, 3, 8, P).transpose(3, 2, 0, 1),
        "h0": i["state_rglru_h"][0].reshape(NSEQ, 8, P).transpose(2, 1, 0),
        "m0": i["state_mlstm_m"][0].T,
        "c0": caug.reshape(NSEQ, H, 2, P, MV).transpose(0, 1, 3, 2, 4),
        "s0": i["state_gla_S"][0].reshape(NSEQ, H, 2, P, GV).transpose(0, 1, 3, 2, 4),
        "w_oa": i["w_out_a"][0].reshape(16, P, D).transpose(1, 0, 2),
        "w_oc": i["w_out_c"][0].reshape(16, P, D).transpose(1, 0, 2),
        "post": np.stack([np.broadcast_to(i["post_norm_a"][0], (P, D)), np.broadcast_to(i["post_norm_c"][0], (P, D))], axis=1),
        "a_up": i["gla_alpha_up"][0].reshape(16, 8, P),
    }


OUTS = {
    "y": (T, D), "conv_p": (P, 8, 3), "conv_s": (P, 8, NSEQ, 3), "h_p": (P, 8), "h_s": (P, 8, NSEQ), "m_out": (H, 9),
    "c_p": (H, P, 2, MV), "c_s": (NSEQ, H, P, 2, MV), "s_p": (H, P, 2, GV), "s_s": (NSEQ, H, P, 2, GV),
}


def take_out(o):
    import numpy as np
    y = o["y"]

    def c_state(c):
        c = np.moveaxis(c, -2, -3)
        c = c.reshape(c.shape[:-3] + (DK, MV))
        return np.ascontiguousarray(np.swapaxes(c[..., 0:DK], -1, -2)), np.ascontiguousarray(c[..., DK])

    def s_state(c):
        c = np.moveaxis(c, -2, -3)
        return c.reshape(c.shape[:-3] + (DK, GV))
    pc, pn = c_state(o["c_p"])
    sc, sn = c_state(o["c_s"])
    con = np.ascontiguousarray
    return (
        con(y[16:NP_TOK][None]), con(y[NP_TOK:].reshape(NSEQ, SLEN, D)),
        pc[None, None], pn[None, None], con(o["m_out"][:, 0][None, None]),
        con(o["h_p"].T.reshape(1, 1, D)), con(o["conv_p"].transpose(2, 1, 0).reshape(1, 1, 3, D)), con(s_state(o["s_p"])[None, None]),
        sc[None], sn[None], con(o["m_out"][:, 1:].T[None]),
        con(o["h_s"].transpose(2, 1, 0).reshape(1, NSEQ, D)), con(o["conv_s"].transpose(2, 3, 1, 0).reshape(1, NSEQ, 3, D)),
        con(s_state(o["s_s"])[None]),
    )


def kernel(**inputs):
    import numpy as _np
    import concourse.bacc as _bacc
    from concourse.bass_utils import run_bass_kernel_spmd as _run

    nc = _bacc.Bacc("TRN2", target_bir_lowering=False, num_devices=1,
                    dynamic_dma_scratch_size=1024)
    arrays = {k: _np.ascontiguousarray(v) for k, v in lay_out({k: _np.asarray(v) for k, v in inputs.items()}).items()}
    io = {k: nc.dram_tensor("in_" + k, v.shape, F32, kind="ExternalInput").ap() for k, v in arrays.items()}
    for k, shape in OUTS.items():
        io[k] = nc.dram_tensor("out_" + k, shape, F32, kind="ExternalOutput").ap()
    build_program(nc, io)
    r = _run(nc, [{"in_" + k: v for k, v in arrays.items()}], core_ids=[0])
    return take_out({k: r.results[0]["out_" + k] for k in OUTS})
```

```python
from contextlib import ExitStack

import concourse.bass as bass
from concourse import mybir

P = 128
D = 1024
KT = D // P
NP_TOK = 1040
NSEQ, SLEN = 8, 4
T = NP_TOK + NSEQ * SLEN
NC = 9
LAST = T - 8 * P
TAIL = NP_TOK - 8 * P
NG = 1 + NSEQ
TC = 358
TP = 3 * TC
H = 4
DK = 256
MV = 257
GV = 512
EPS = 1e-6
NEG = -1e30

A_PAIR0 = 1
A_QKV0 = 17
A_TILES = 57
C_PAIR0 = 1
C_V0 = 17
C_TILES = 49
AF = 10
CF = 12

V_PRE_A, V_PRE_C = 0, 8
V_CONVW, V_CONVB = 16, 48
V_BA, V_BX, V_LAM = 56, 64, 72
V_MNORM, V_GNORM = 80, 88
V_ALPHAB = 104
V_GATEB = 112
NVEC = 113

F32 = mybir.dt.float32
F32R = mybir.dt.float32r
ALU = mybir.AluOpType
ACT = mybir.ActivationFunctionType


class Names:
    pass


def make_alloc(nc, ctx):
    a = Names()
    a.sb = lambda name, shape, dt=F32: ctx.enter_context(nc.sbuf_tensor(name, shape, dt))
    a.ps = lambda name, shape: ctx.enter_context(nc.psum_tensor(name, shape, F32))
    a.sems = []

    def sem(name):
        a.sems.append(nc.alloc_semaphore(name=name))
        return a.sems[-1]
    a.sem = sem
    return a


def clear_semaphores(nc, a):
    nc.clear_and_free_semaphores(a.sems)
    a.sems.clear()
    nc.all_engine_barrier()


def linker(eng, sem, base=0):
    k = [0]

    def link(ins):
        k[0] += 1
        ins.then_inc(sem, 1)
        eng.wait_ge(sem, base + k[0])
    link.count = lambda: k[0]
    return link


def stage_constants(nc, S, vecs_d):
    made = S.a.sem("const_made")
    loaded = S.a.sem("const_loaded")
    with nc.Block() as block:
        @block.sync
        def _(sp):
            sp.dma_start(S.vecs[:], vecs_d).then_inc(loaded, 16)
            sp.wait_ge(loaded, 16)

        @block.gpsimd
        def _(pool):
            link = linker(pool, made)
            link(pool.memset(S.ident[:], 0.0))
            link(pool.affine_select(out=S.ident[:], in_=S.ident[:], compare_op=ALU.not_equal, fill=1.0,
                                    base=0, pattern=[[-1, P]], channel_multiplier=1))
            link(pool.memset(S.sel[:], 0.0))
            link(pool.affine_select(out=S.sel[:], in_=S.sel[:], compare_op=ALU.not_equal, fill=1.0,
                                    base=0, pattern=[[-1, H], [0, P]], channel_multiplier=1))
            link(pool.memset(S.reset[:], 1.0))
            link(pool.memset(S.reset[:, 0:8 * P].rearrange("p (c t) -> p c t", t=P)[:, :, 0:1], 0.0))
            link(pool.memset(S.reset[:, 8 * P:8 * P + 1], 0.0))
            link(pool.memset(S.reset[:, NP_TOK:T].rearrange("p (s t) -> p s t", t=SLEN)[:, :, 0:1], 0.0))
            for m, seen, hidden in ((S.mask_add, 0.0, NEG), (S.mask_add8, 0.0, NEG), (S.mask_one, 1.0, 0.0), (S.mask_one8, 1.0, 0.0)):
                w = m.shape[1]
                link(pool.memset(m[:], seen))
                link(pool.affine_select(out=m[:], in_=m[:], compare_op=ALU.is_ge, fill=hidden,
                                        base=0, pattern=[[1, w]], channel_multiplier=-1))
                if w == LAST:
                    part = m[:, TAIL:LAST].rearrange("p (s t) -> p s t", t=SLEN)
                    link(pool.affine_select(out=part, in_=part, compare_op=ALU.is_ge, fill=hidden,
                                            base=-TAIL, pattern=[[-SLEN, NSEQ], [0, SLEN]], channel_multiplier=1))
            link(pool.memset(S.seq_mask[:], 1.0))
            link(pool.affine_select(out=S.seq_mask[:], in_=S.seq_mask[:], compare_op=ALU.is_ge, fill=0.0,
                                    base=-TAIL, pattern=[[-SLEN, NSEQ]], channel_multiplier=1))
            link(pool.affine_select(out=S.seq_mask[:], in_=S.seq_mask[:], compare_op=ALU.is_ge, fill=0.0,
                                    base=TAIL + SLEN - 1, pattern=[[SLEN, NSEQ]], channel_multiplier=-1))
            link(pool.memset(S.tail_mask[:], 1.0))
            link(pool.affine_select(out=S.tail_mask[:], in_=S.tail_mask[:], compare_op=ALU.is_ge, fill=0.0,
                                    base=TAIL - 1, pattern=[[0, 1]], channel_multiplier=-1))

def stage_norm(nc, S, name, x_d, gcol):
    with ExitStack() as ctx:
        a = make_alloc(nc, ctx)
        xin = [a.sb(f"{name}_xin{s}", [P, D]) for s in range(2)]
        junk = a.sb(f"{name}_junk", [P, D])
        xn = [a.sb(f"{name}_xn{s}", [P, D]) for s in range(2)]
        stat = [a.sb(f"{name}_stat{s}", [P, 4]) for s in range(2)]
        ps = a.ps(f"{name}_ps", [P, 4, 512])
        loaded = [S.a.sem(f"{name}_x_loaded{s}") for s in range(2)]
        rstd_ready = S.a.sem(f"{name}_rstd_ready")
        act_chain = S.a.sem(f"{name}_act_chain")
        xn_ready = S.a.sem(f"{name}_xn_ready")
        turned = S.a.sem(f"{name}_turned")
        hi_ready = S.a.sem(f"{name}_hi_ready")
        lo_ready = S.a.sem(f"{name}_lo_ready")

        def cols(c, rows):
            return bass.ds(c * P, rows)

        with nc.Block() as block:
            @block.sync
            def _(sp):
                def load(c, u, rows, first):
                    if not first:
                        sp.wait_ge(xn_ready, c - 1)
                    sp.dma_start(xin[u][0:rows, :], x_d[bass.ds(c * P, rows), :]).then_inc(loaded[u], 16)
                load(0, 0, P, True)
                load(1, 1, P, True)
                with sp.Fori(1, 4) as i:
                    load(2 * i, 0, P, False)
                    load(2 * i + 1, 1, P, False)
                load(8, 0, LAST, False)

            @block.scalar
            def _(act):
                act.preload_act_table_set('natural_log_exp_and_others')
                link_base = [0]

                def tile(i, u, c, rows, done):
                    st = stat[u]
                    act.wait_ge(loaded[u], 16 * i + 16)
                    base = c * 3
                    act.activation(junk[0:rows, :], xin[u][0:rows, :], ACT.Square,
                                   accum_out=st[0:rows, 0:1]).then_inc(act_chain, 1)
                    act.wait_ge(act_chain, base + 1)
                    act.activation(st[0:rows, 1:2], st[0:rows, 0:1], ACT.Ln, scale=1.0 / D,
                                   bias=S.eps[0:rows, :]).then_inc(act_chain, 1)
                    act.wait_ge(act_chain, base + 2)
                    act.activation(st[0:rows, 2:3], st[0:rows, 1:2], ACT.Exp, scale=-0.5).then_inc(rstd_ready, 1)
                    act.wait_ge(rstd_ready, c + 1)
                    act.activation(st[0:rows, 3:4], st[0:rows, 2:3], ACT.Copy).then_inc(act_chain, 1)
                    act.wait_ge(turned, c + 1)
                    for k in range(KT):
                        ins = act.activation(S.XT_hi[:, k, cols(c, rows)], ps[:, 2 * u + k // 4, bass.ds(k % 4 * P, rows)],
                                             ACT.Copy, scale=S.vecs[:, gcol + k:gcol + k + 1])
                    ins.then_inc(hi_ready, 1)
                with act.Fori(0, 4) as i:
                    tile(i, 0, 2 * i, P, None)
                    tile(i, 1, 2 * i + 1, P, None)
                tile(4, 0, 8, LAST, None)

            @block.vector
            def _(dve):
                def tile(u, c, rows):
                    dve.wait_ge(rstd_ready, c + 1)
                    if not isinstance(c, int) or c >= 2:
                        pass
                    dve.tensor_scalar(xn[u][0:rows, :], xin[u][0:rows, :], stat[u][0:rows, 2:3], None,
                                      ALU.mult).then_inc(xn_ready, 1)
                    dve.wait_ge(hi_ready, c + 1)
                    for k in range(KT):
                        ins = dve.scalar_tensor_tensor(
                            out=S.XT_lo[:, k, cols(c, rows)], in0=ps[:, 2 * u + k // 4, bass.ds(k % 4 * P, rows)],
                            scalar=S.vecs[:, gcol + k:gcol + k + 1],
                            in1=S.XT_hi[:, k, cols(c, rows)].bitcast(F32), op0=ALU.mult, op1=ALU.subtract)
                    ins.then_inc(lo_ready, 1)
                with dve.Fori(0, 4) as i:
                    tile(0, 2 * i, P)
                    tile(1, 2 * i + 1, P)
                tile(0, 8, LAST)
                for t in (S.XT_hi, S.XT_lo):
                    dve.memset(t[:, :, T:TP].bitcast(F32), 0.0)

            @block.tensor
            def _(pe):
                def tile(u, c, rows, first):
                    pe.wait_ge(xn_ready, c + 1)
                    if not first:
                        pe.wait_ge(lo_ready, c - 1)
                    for k in range(KT):
                        ins = pe.transpose(ps[:, 2 * u + k // 4, bass.ds(k % 4 * P, rows)],
                                           xn[u][0:rows, k * P:(k + 1) * P], S.ident[0:rows, 0:rows])
                    ins.then_inc(turned, 1)
                tile(0, 0, P, True)
                tile(1, 1, P, True)
                with pe.Fori(1, 4) as i:
                    tile(0, 2 * i, P, False)
                    tile(1, 2 * i + 1, P, False)
                tile(0, 8, LAST, False)


class Projection:

    def __init__(self, nc, S, a, name, w_d, tiles):
        self.S, self.w_d, self.tiles, self.name = S, w_d, tiles, name
        self.raw = [a.sb(f"{name}_w_raw{s}", [P, KT, P]) for s in range(2)]
        self.hi = [a.sb(f"{name}_w_hi{s}", [P, KT, P], F32R) for s in range(2)]
        self.lo = [a.sb(f"{name}_w_lo{s}", [P, KT, P], F32R) for s in range(2)]
        self.ps = a.ps(f"{name}_ps", [P, 8, 512])
        self.w_loaded = [S.a.sem(f"{name}_w_loaded{s}") for s in range(2)]
        self.w_hi_ready = S.a.sem(f"{name}_w_hi_ready")
        self.w_lo_ready = S.a.sem(f"{name}_w_lo_ready")
        self.gemm_done = S.a.sem(f"{name}_gemm_done")
        self.psum_free = [S.a.sem(f"{name}_psum_free{s}") for s in range(2)]

    def bank(self, s):
        return self.ps[:, 3 * s:3 * s + 3, 0:TC]

    def load(self, sp, n, s):
        if not (isinstance(n, int) and n < 2):
            sp.wait_ge(self.w_lo_ready, n - 1)
        sp.dma_start(self.raw[s][:], self.w_d[bass.ds(n, 1), :, :, :].rearrange("o p k f -> p (o k) f")
                     ).then_inc(self.w_loaded[s], 16)

    def split_hi(self, act, n, s, half):
        act.wait_ge(self.w_loaded[s], 16 * half + 16)
        if not (isinstance(n, int) and n < 2):
            act.wait_ge(self.gemm_done, n - 1)
        act.activation(self.hi[s][:], self.raw[s][:], ACT.Copy).then_inc(self.w_hi_ready, 1)

    def split_lo(self, dve, n, s):
        dve.wait_ge(self.w_hi_ready, n + 1)
        dve.tensor_tensor(self.lo[s][:], self.raw[s][:], self.hi[s][:].bitcast(F32), ALU.subtract
                          ).then_inc(self.w_lo_ready, 1)

    def products(self, pe, n, s, half, hooks={}):
        pe.wait_ge(self.w_lo_ready, n + 1)
        if not (isinstance(n, int) and n < 2):
            pe.wait_ge(self.psum_free[s], half)
        S = self.S
        passes = ((self.hi[s], S.XT_hi), (self.hi[s], S.XT_lo), (self.lo[s], S.XT_hi))
        for k in range(KT):
            if k in hooks:
                hooks[k]()
            for j, (w, x) in enumerate(passes):
                for t in range(3):
                    ins = pe.matmul(self.ps[:, 3 * s + t, 0:TC], w[:, k, :], x[:, k, t * TC:(t + 1) * TC],
                                    start=(k == 0 and j == 0), stop=(k == KT - 1 and j == 2))
        ins.then_inc(self.gemm_done, 1)


def stage_vectors(nc, S):
    chain_a = S.a.sem("vec_act_chain")
    chain_d = S.a.sem("vec_dve_chain")
    lam_abs = S.a.sem("lam_exp_ready")
    with ExitStack() as ctx:
        a = make_alloc(nc, ctx)
        e, w, z, z2, p, m = (a.sb(f"vec_{n}", [P, 8]) for n in ("e", "w", "z", "z2", "p", "m"))
        lam = S.vecs[:, V_LAM:V_LAM + 8]
        with nc.Block() as block:
            @block.scalar
            def _(act):
                act.preload_act_table_set('natural_log_exp_and_others')
                link = linker(act, chain_a)
                link(act.activation(w[:], lam, ACT.Abs))
                act.activation(e[:], w[:], ACT.Exp, scale=-1.0).then_inc(lam_abs, 1)

            @block.vector
            def _(dve):
                link = linker(dve, chain_d)
                dve.memset(S.eps[:], EPS)
                dve.memset(S.tiny[:], 1e-18)
                link(dve.tensor_scalar(m[:], lam, -1.0, 0.0, ALU.mult, ALU.max))
                dve.wait_ge(lam_abs, 1)
                link(dve.tensor_scalar(z[:], e[:], 2.0, None, ALU.add))
                link(dve.reciprocal(p[:], z[:]))
                link(dve.tensor_tensor(z[:], e[:], p[:], ALU.mult))
                link(dve.tensor_tensor(z2[:], z[:], z[:], ALU.mult))
                link(dve.tensor_scalar(p[:], z2[:], 1.0 / 15, 1.0 / 13, ALU.mult, ALU.add))
                for n in (11, 9, 7, 5, 3, 1):
                    link(dve.tensor_tensor(p[:], p[:], z2[:], ALU.mult))
                    link(dve.tensor_scalar(p[:], p[:], 1.0 / n, None, ALU.add))
                link(dve.tensor_tensor(p[:], p[:], z[:], ALU.mult))
                link(dve.scalar_tensor_tensor(out=z[:], in0=p[:], scalar=2.0, in1=m[:], op0=ALU.mult, op1=ALU.add))
                dve.tensor_scalar(S.derived[:, 0, :], z[:], 8.0, None, ALU.mult)
                dve.tensor_scalar(S.derived[:, 1, :], z[:], -8.0, None, ALU.mult)


def stage_project_a(nc, S, w_d, lru_w_d, conv0_d, h0_d, scr_d, lru_d, m0_d, out_conv_p, out_conv_s, out_h_p, out_h_s, out_m, w_out):
    with ExitStack() as ctx:
        a = make_alloc(nc, ctx)
        G = Projection(nc, S, a, "pa", w_d, A_TILES)
        stage = [a.sb(f"pa_stage{s}", [P, 3, TC]) for s in range(2)]
        flat = [s[:].rearrange("p a b -> p (a b)") for s in stage]
        xe_p = a.sb("pa_xe_p", [P, 3 + NP_TOK])
        xe_s = a.sb("pa_xe_s", [P, NSEQ, 3 + SLEN])
        xc = a.sb("pa_xc", [P, TP])
        gr_e = a.sb("pa_gate_r", [P, TP])
        gi_e = a.sb("pa_gate_i", [P, TP])
        av = a.sb("pa_decay", [P, T])
        tv = a.sb("pa_tanh", [P, T])
        lv = a.sb("pa_log", [P, T])
        hv = a.sb("pa_h", [P, T])
        silu = a.sb("pa_silu", [P, 3, TC])
        silu_f = silu[:].rearrange("p a b -> p (a b)")
        lout = a.sb("pa_lru_out", [P, T])
        lru_w = a.sb("pa_lru_w", [P, 2, P])
        conv0 = a.sb("pa_conv0", [P, 8, NSEQ, 3])
        h0 = a.sb("pa_h0", [P, 8, NSEQ])
        cp_out = a.sb("pa_conv_p_out", [P, 8, 3])
        cs_out = a.sb("pa_conv_s_out", [P, 8, NSEQ, 3])
        hp_out = a.sb("pa_h_p_out", [P, 8])
        hs_out = a.sb("pa_h_s_out", [P, 8, NSEQ])
        tmp8 = a.sb("pa_tmp8", [P, NSEQ])
        gates = a.sb("pa_gates", [P, TP])
        par = a.sb("pa_scalars", [P, 4])
        rows = a.sb("pa_rows", [P, T])
        m0 = a.sb("pa_m0", [4, NSEQ])
        m_prev = a.sb("pa_m_prev", [4, 17])
        m_out = a.sb("pa_m_out", [4, 9])
        e_last = a.sb("pa_e_last", [4, 17])

        sem = S.a.sem
        small_in = sem("pa_small_in")
        lru_w_in = sem("pa_lru_w_in")
        gates_out = sem("pa_gates_out")
        xr_ready = sem("pa_xr_ready")
        conv_ready = sem("pa_conv_ready")
        lru_gemm = sem("pa_lru_gemm_done")
        gates_ready = sem("pa_gates_ready")
        tanh_ready = sem("pa_tanh_ready")
        decay_ready = sem("pa_decay_ready")
        logs_ready = sem("pa_logs_ready")
        root_log = sem("pa_root_log_ready")
        root_ready = sem("pa_root_ready")
        silu_ready = sem("pa_silu_ready")
        dve_chain = sem("pa_dve_chain")
        scan_done = sem("pa_scan_done")
        lru_out_ready = sem("pa_lru_out_ready")
        lru_spilled = sem("pa_lru_spilled")
        ixc_ready = sem("pa_ixc_ready")
        stage_ready = sem("pa_stage_ready")
        z_ready = sem("pa_z_ready")
        sigmoid_ready = sem("pa_sigmoid_ready")
        spilled = [sem(f"pa_spilled{s}") for s in range(2)]
        finished = sem("pa_outputs_stored")
        row_act = sem("pa_rows_act")
        row_dve = sem("pa_rows_dve")
        rows_ready = sem("pa_rows_ready")
        rows_turned = sem("pa_rows_turned")
        tok_ready = sem("pa_tok_ready")

        PROMPT = slice(0, NP_TOK)
        STARTS = (NP_TOK, SLEN)

        def seq_cols(buf, off):
            return buf[:, NP_TOK:NP_TOK + NSEQ * SLEN].rearrange("p (s t) -> p s t", t=SLEN)[:, :, off]

        def seqs4(row, off):
            return seqs(row)[:, :, off]

        def seqs(buf):
            return buf[:, NP_TOK:NP_TOK + NSEQ * SLEN].rearrange("p (s t) -> p s t", t=SLEN)

        groups = ("q", "k", "v", "og", "z")

        xf, ab, lf, bb, mm = (x[0:4, 0:T] for x in (gr_e, gi_e, av, tv, lv))
        li = gates[0:4, 0:T]

        def chunked(row):
            return row[:, 0:8 * P].rearrange("p (c t) -> p c t", t=P)

        def gate_rows_act(act):
            act.wait_ge(lru_out_ready, 8)
            act.activation(xf, gates[32:36, 0:T], ACT.Copy).then_inc(row_act, 1)
            act.activation(ab, gates[32:36, 0:T], ACT.Abs).then_inc(row_act, 1)
            act.wait_ge(row_act, 2)
            act.activation(ab, ab, ACT.Exp, scale=-1.0).then_inc(row_act, 1)
            act.wait_ge(row_act, 3)
            act.activation(ab, ab, ACT.Ln, bias=1.0).then_inc(row_act, 1)

        def gate_rows_act_out(act):
            act.wait_ge(rows_turned, 1)
            act.activation(S.wc[:], G.ps[:, 6, 0:4 * 17].rearrange("p (h g) -> p h g", g=17), ACT.Exp)
            for bank, off, c0, n in ((6, 80, 0, 5), (7, 0, 5, 4)):
                turned = G.ps[:, bank, off:off + 68 * n].rearrange("p (c r) -> p c r", r=68)
                act.activation(S.tok[:, c0:c0 + n, 0, :], turned[:, :, 0:4], ACT.Copy)
                act.activation(S.tok[:, c0:c0 + n, 1, :], turned[:, :, 32:36], ACT.Exp)
                ins = act.activation(S.tok[:, c0:c0 + n, 2, :], turned[:, :, 64:68], ACT.Exp)
            ins.then_inc(tok_ready, 1)

        def gate_rows_dve(dve):
            link = linker(dve, row_dve)
            link(dve.memset(rows[:], 0.0))
            link(dve.memset(m_prev[:], 0.0))
            dve.wait_ge(row_act, 4)
            link(dve.scalar_tensor_tensor(out=lf, in0=xf, scalar=0.0, in1=ab, op0=ALU.min, op1=ALU.subtract))
            link(dve.tensor_tensor_scan(bb, S.reset[0:4, :], lf, 0.0, ALU.mult, ALU.add))
            link(dve.tensor_tensor_scan(mm[:, PROMPT], lf[:, PROMPT], li[:, PROMPT], 0.0, ALU.add, ALU.max))
            link(dve.tensor_copy(m_prev[:, 9:17], m0[:]))
            for t in range(SLEN):
                before = m_prev[:, 9:17] if t == 0 else seqs4(mm, t - 1)
                link(dve.tensor_tensor(seqs4(mm, t), before, seqs4(lf, t), ALU.add))
                link(dve.tensor_tensor(seqs4(mm, t), seqs4(mm, t), seqs4(li, t), ALU.max))
            link(dve.tensor_copy(m_prev[:, 1:9], chunked(mm)[:, :, P - 1]))
            link(dve.tensor_copy(m_out[:, 0:1], mm[:, NP_TOK - 1:NP_TOK]))
            link(dve.tensor_copy(m_out[:, 1:9], seqs4(mm, SLEN - 1)))
            link(dve.tensor_tensor(S.rrow[:], bb, mm, ALU.subtract))
            dve.tensor_tensor(rows[0:4, :], li, bb, ALU.subtract)
            dve.tensor_tensor(chunked(rows[32:36, :]), chunked(S.rrow[:]),
                              m_prev[:, 0:8].unsqueeze(2).to_broadcast([4, 8, P]), ALU.add)
            dve.tensor_scalar(rows[32:36, 8 * P:NP_TOK], S.rrow[:, 8 * P:NP_TOK], m_prev[:, 8:9], None, ALU.add)
            dve.tensor_tensor(seqs(rows[32:36, :]), seqs(S.rrow[:]),
                              m_prev[:, 9:17].unsqueeze(2).to_broadcast([4, NSEQ, SLEN]), ALU.add)
            dve.tensor_scalar(rows[64:68, :], mm, -1.0, None, ALU.mult)
            dve.tensor_tensor(e_last[:, 0:8], chunked(S.rrow[:])[:, :, P - 1], m_prev[:, 0:8], ALU.add)
            dve.tensor_tensor(e_last[:, 8:9], S.rrow[:, NP_TOK - 1:NP_TOK], m_prev[:, 8:9], ALU.add)
            dve.tensor_tensor(e_last[:, 9:17], seqs4(S.rrow[:], SLEN - 1), m_prev[:, 9:17], ALU.add).then_inc(rows_ready, 1)

        def gate_rows_pe(pe):
            pe.wait_ge(rows_ready, 1)
            pe.wait_ge(gates_ready, 24)
            for h in range(H):
                pe.matmul(G.ps[:, 6, 17 * h:17 * h + 17], S.sel[:, h, :], e_last[:], start=True, stop=True)
            for c in range(NC):
                w = P if c < 8 else LAST
                bank, off = (6, 80 + 68 * c) if c < 5 else (7, 68 * (c - 5))
                ins = pe.transpose(G.ps[0:w, bank, off:off + 68], rows[0:68, c * P:c * P + w], S.ident[0:68, 0:68])
            ins.then_inc(rows_turned, 1)

        with nc.Block() as block:
            @block.sync
            def _(sp):
                sp.dma_start(m0[:], m0_d).then_inc(small_in, 16)
                sp.dma_start(conv0[:], conv0_d).then_inc(small_in, 16)
                sp.dma_start(h0[:], h0_d).then_inc(small_in, 16)
                G.load(sp, 0, 0)
                G.load(sp, 1, 1)
                G.load(sp, 2, 0)

                def pair(i, first):
                    if not first:
                        sp.wait_ge(lru_gemm, 3 * i)
                    sp.dma_start(lru_w[:], lru_w_d[bass.ds(i, 1), :, :, :].rearrange("o i m j -> i (o m) j")
                                 ).then_inc(lru_w_in, 16)
                    G.load(sp, 2 * i + 3, 1)
                    G.load(sp, 2 * i + 4, 0)
                    sp.wait_ge(lru_out_ready, i + 1)
                    dst = lru_d[0:8, :, bass.ds(i, 1), :].rearrange("c p o t -> p c (o t)")
                    sp.dma_start(dst, lout[:, 0:8 * P].rearrange("p (c t) -> p c t", t=P)).then_inc(lru_spilled, 16)
                    sp.dma_start(lru_d[8, :, bass.ds(i, 1), 0:LAST].rearrange("p o t -> p (o t)"),
                                 lout[:, 8 * P:T]).then_inc(lru_spilled, 16)
                pair(0, True)
                with sp.Fori(1, 8) as i:
                    pair(i, False)
                sp.wait_ge(scan_done, 8)
                sp.dma_start(out_conv_p, cp_out[:]).then_inc(finished, 16)
                sp.dma_start(out_conv_s, cs_out[:]).then_inc(finished, 16)
                sp.dma_start(out_h_p, hp_out[:]).then_inc(finished, 16)
                sp.dma_start(out_h_s, hs_out[:]).then_inc(finished, 16)

                def spill(n, s, head, slot_in_head, m):
                    sp.wait_ge(z_ready if slot_in_head >= 8 else stage_ready, m + 1)
                    dst = scr_d[0:8, bass.ds(head, 1), :, slot_in_head, :].rearrange("c o p t -> p (o c) t")
                    sp.dma_start(dst, flat[s][:, 0:8 * P].rearrange("p (c t) -> p c t", t=P)).then_inc(spilled[s], 16)
                    sp.dma_start(scr_d[8, bass.ds(head, 1), :, slot_in_head, 0:LAST].rearrange("o p t -> (o p) t"),
                                 flat[s][:, 8 * P:T]).then_inc(spilled[s], 16)

                def group(g):
                    last = g == len(groups) - 1

                    def two(h, tail):
                        for d in range(2):
                            n = A_QKV0 + 8 * g + 2 * h + d
                            if not tail:
                                G.load(sp, n + 2, (1 + d) % 2)
                            spill(n, (1 + d) % 2, h, 2 * g + d, (0 if last else 8 * g) + 2 * h + d)
                    if last:
                        with sp.Fori(0, 3) as h:
                            two(h, False)
                        two(3, True)
                    else:
                        with sp.Fori(0, 4) as h:
                            two(h, False)
                for g in range(len(groups)):
                    if g:
                        w_out.load(sp, g - 1)
                    group(g)
                    if g == 0:
                        sp.wait_ge(rows_ready, 1)
                        sp.dma_start(out_m, m_out[:]).then_inc(finished, 16)
                sp.wait_ge(lru_spilled, 16 * 2 * 8)
                for s in range(2):
                    sp.wait_ge(spilled[s], 16 * 2 * 20)
                sp.wait_ge(finished, 80)

            @block.scalar
            def _(act):
                act.preload_act_table_set('natural_log_exp_and_others')
                G.split_hi(act, 0, 0, 0)
                G.split_hi(act, 1, 1, 0)
                act.wait_ge(G.gemm_done, 1)
                for t in range(3):
                    w = TC if t < 2 else T - 2 * TC
                    ins = act.activation(gates[:, t * TC:t * TC + w], G.ps[:, t, 0:w], ACT.Identity,
                                         bias=S.vecs[:, V_GATEB:V_GATEB + 1])
                ins.then_inc(G.psum_free[0], 1)
                G.split_hi(act, 2, 0, 1)

                def pair(i, first):
                    n = 2 * i + 1
                    act.wait_ge(G.gemm_done, n + 1)
                    if not first:
                        act.wait_ge(conv_ready, i)
                    act.activation(xe_p[:, 3:3 + 2 * TC].rearrange("p (a b) -> p a b", b=TC), G.ps[:, 3:5, 0:TC], ACT.Copy)
                    act.activation(xe_p[:, 3 + 2 * TC:3 + NP_TOK], G.ps[:, 5, 0:NP_TOK - 2 * TC], ACT.Copy)
                    act.activation(xe_s[:, :, 3:], G.ps[:, 5, NP_TOK - 2 * TC:T - 2 * TC].rearrange(
                        "p (s t) -> p s t", t=SLEN), ACT.Copy).then_inc(xr_ready, 1)
                    G.split_hi(act, n + 2, 1, i + 1)
                    act.preload_act_table_set('sigmoid_and_others')
                    for t in range(3):
                        act.wait_ge(lru_gemm, 3 * i + t + 1)
                        if t == 0 and not first:
                            act.wait_ge(scan_done, i)
                        act.activation(gr_e[:, t * TC:(t + 1) * TC], G.ps[:, 6, 0:TC], ACT.Sigmoid,
                                       bias=par[:, 0:1])
                        act.activation(gi_e[:, t * TC:(t + 1) * TC], G.ps[:, 7, 0:TC], ACT.Sigmoid,
                                       bias=par[:, 1:2]).then_inc(gates_ready, 1)
                    act.wait_ge(G.gemm_done, n + 2)
                    if not first:
                        act.wait_ge(lru_out_ready, i)
                    act.activation(silu[:], G.bank(0), ACT.Sigmoid).then_inc(silu_ready, 1)
                    G.split_hi(act, n + 3, 0, i + 2)
                    act.wait_ge(gates_ready, 3 * i + 3)
                    act.activation(tv[:], gr_e[:, 0:T], ACT.Tanh, scale=par[:, 2:3]).then_inc(tanh_ready, 1)
                    act.preload_act_table_set('natural_log_exp_and_others')
                    act.activation(av[:], gr_e[:, 0:T], ACT.Exp, scale=par[:, 3:4]).then_inc(decay_ready, 1)
                    act.wait_ge(tanh_ready, i + 1)
                    act.activation(lv[:], tv[:], ACT.Ln, scale=2.0, bias=S.tiny[:])
                    act.wait_ge(decay_ready, i + 1)
                    act.activation(gr_e[:, 0:T], tv[:], ACT.Ln, bias=1.0).then_inc(logs_ready, 1)
                    act.wait_ge(root_log, i + 1)
                    act.activation(lv[:], lv[:], ACT.Exp, scale=0.5).then_inc(root_ready, 1)

                pair(0, True)
                with act.Fori(1, 8) as i:
                    pair(i, False)

                gate_rows_act(act)

                def tile(g, h, d, tail, first):
                    s = (1 + d) % 2
                    n = A_QKV0 + 8 * g + 2 * h + d
                    kind = groups[g]
                    act.wait_ge(G.gemm_done, n + 1)
                    if not first:
                        act.wait_ge(spilled[s], 32 * (4 * g + h))
                    if kind in ("q", "k", "v"):
                        act.activation(stage[s][:], G.bank(s), ACT.Copy, scale=0.0625 if kind == "k" else 1.0
                                       ).then_inc(stage_ready, 1)
                        act.wait_ge(stage_ready, 8 * g + 2 * h + d + 1)
                        act.sem_inc(G.psum_free[s], 1)
                    else:
                        if kind == "og":
                            act.activation(stage[s][:], G.bank(s), ACT.Sigmoid).then_inc(stage_ready, 1)
                            act.wait_ge(stage_ready, 8 * g + 2 * h + d + 1)
                            act.sem_inc(G.psum_free[s], 1)
                        else:
                            act.activation(stage[s][:], G.bank(s), ACT.Sigmoid).then_inc(sigmoid_ready, 1)
                    if not tail:
                        G.split_hi(act, n + 2, s, (A_QKV0 + 8 * g + d) // 2 + 1 + h)

                for g in range(len(groups)):
                    last = g == len(groups) - 1
                    if g == 0:
                        for d in range(2):
                            tile(g, 0, d, False, True)
                    with act.Fori(1 if g == 0 else 0, 3 if last else 4) as h:
                        for d in range(2):
                            tile(g, h, d, False, False)
                    if last:
                        for d in range(2):
                            tile(g, 3, d, True, False)
                    if g == 1:
                        gate_rows_act_out(act)

            @block.vector
            def _(dve):
                dve.memset(xe_p[:, 0:3], 0.0)
                dve.memset(xc[:, T:TP], 0.0)
                G.split_lo(dve, 0, 0)
                G.split_lo(dve, 1, 1)
                G.split_lo(dve, 2, 0)
                dve.wait_ge(small_in, 48)

                def pair(i, first):
                    n = 2 * i + 1
                    K = LRU_DVE_STEPS
                    link = linker(dve, dve_chain, i * K)
                    cw = [S.vecs[:, bass.ds(V_CONVW + j * 8 + i, 1)] for j in range(4)]
                    cb = S.vecs[:, bass.ds(V_CONVB + i, 1)]
                    dve.tensor_copy(xe_s[:, :, 0:3], conv0[:, bass.ds(i, 1), :, :].rearrange("p o s j -> p (o s) j"))
                    dve.wait_ge(xr_ready, i + 1)
                    dve.sem_inc(G.psum_free[1], 1)
                    dve.tensor_copy(par[:, 0:2], S.vecs[:, V_BA:V_BA + 16].rearrange("p (m i) -> p m i", i=8)[:, :, bass.ds(i, 1)]
                                    .rearrange("p m o -> p (m o)"))
                    dve.tensor_copy(par[:, 2:4], S.derived[:, :, bass.ds(i, 1)].rearrange("p m o -> p (m o)"))
                    link(dve.tensor_scalar(xc[:, 0:NP_TOK], xe_p[:, 0:NP_TOK], cw[0], cb, ALU.mult, ALU.add))
                    link(dve.tensor_scalar(seqs(xc), xe_s[:, :, 0:SLEN], cw[0], cb, ALU.mult, ALU.add))
                    for j in range(1, 4):
                        link(dve.scalar_tensor_tensor(out=xc[:, 0:NP_TOK], in0=xe_p[:, j:j + NP_TOK], scalar=cw[j],
                                                      in1=xc[:, 0:NP_TOK], op0=ALU.mult, op1=ALU.add))
                        link(dve.scalar_tensor_tensor(out=seqs(xc), in0=xe_s[:, :, j:j + SLEN], scalar=cw[j],
                                                      in1=seqs(xc), op0=ALU.mult, op1=ALU.add))
                    dve.tensor_copy(cp_out[:, bass.ds(i, 1), :].rearrange("p o j -> p (o j)"), xe_p[:, NP_TOK:NP_TOK + 3])
                    dve.tensor_copy(cs_out[:, bass.ds(i, 1), :, :].rearrange("p o s j -> p (o s) j"),
                                    xe_s[:, :, SLEN:SLEN + 3]).then_inc(conv_ready, 1)
                    G.split_lo(dve, n + 2, 1)
                    dve.wait_ge(silu_ready, i + 1)
                    dve.tensor_tensor(silu[:], G.bank(0), silu[:], ALU.mult).then_inc(G.psum_free[0], 1)
                    G.split_lo(dve, n + 3, 0)
                    dve.wait_ge(logs_ready, i + 1)
                    dve.tensor_tensor(lv[:], lv[:], gr_e[:, 0:T], ALU.subtract).then_inc(root_log, 1)
                    dve.wait_ge(ixc_ready, i + 1)
                    dve.wait_ge(root_ready, i + 1)
                    link(dve.tensor_tensor(lv[:], lv[:], gi_e[:, 0:T], ALU.mult))
                    dve.wait_ge(decay_ready, i + 1)
                    link(dve.tensor_tensor(tmp8[:], seq_cols(av, 0), h0[:, bass.ds(i, 1), :].rearrange("p o s -> p (o s)"), ALU.mult))
                    link(dve.tensor_tensor(seq_cols(lv, 0), seq_cols(lv, 0), tmp8[:], ALU.add))
                    link(dve.memset(seq_cols(av, 0), 0.0))
                    link(dve.tensor_tensor_scan(hv[:], av[:], lv[:], 0.0, ALU.mult, ALU.add))
                    dve.tensor_copy(hp_out[:, bass.ds(i, 1)], hv[:, NP_TOK - 1:NP_TOK])
                    dve.tensor_copy(hs_out[:, bass.ds(i, 1), :].rearrange("p o s -> p (o s)"),
                                    seq_cols(hv, SLEN - 1)).then_inc(scan_done, 1)
                    if not first:
                        dve.wait_ge(lru_spilled, 32 * i)
                    dve.tensor_tensor(lout[:], hv[:], silu_f[:, 0:T], ALU.mult).then_inc(lru_out_ready, 1)
                    assert link.count() == K, link.count()

                pair(0, True)
                with dve.Fori(1, 8) as i:
                    pair(i, False)

                gate_rows_dve(dve)

                def tile(g, h, d, tail):
                    s = (1 + d) % 2
                    n = A_QKV0 + 8 * g + 2 * h + d
                    kind = groups[g]
                    if kind == "z":
                        dve.wait_ge(sigmoid_ready, 2 * h + d + 1)
                        dve.scalar_tensor_tensor(out=stage[s][:], in0=G.bank(s), scalar=S.vecs[:, bass.ds(V_MNORM + 2 * h + d, 1)],
                                                     in1=stage[s][:], op0=ALU.mult, op1=ALU.mult).then_inc(z_ready, 1)
                        dve.wait_ge(z_ready, 2 * h + d + 1)
                        dve.sem_inc(G.psum_free[s], 1)
                    if not tail:
                        G.split_lo(dve, n + 2, s)
                for g in range(len(groups)):
                    last = g == len(groups) - 1
                    with dve.Fori(0, 3 if last else 4) as h:
                        for d in range(2):
                            tile(g, h, d, False)
                    if last:
                        for d in range(2):
                            tile(g, 3, d, True)

            @block.gpsimd
            def _(pool):
                with pool.Fori(0, 8) as i:
                    pool.wait_ge(gates_ready, 3 * i + 3)
                    pool.tensor_tensor(gi_e[:, 0:T], gi_e[:, 0:T], xc[:, 0:T], ALU.mult).then_inc(ixc_ready, 1)

            @block.tensor
            def _(pe):
                G.products(pe, 0, 0, 0)

                def gate_round(i, t):
                    def go():
                        if t == 0:
                            pe.wait_ge(conv_ready, i + 1)
                            pe.wait_ge(lru_w_in, 16 * i + 16)
                        if not (isinstance(i, int) and i == 0 and t == 0):
                            pe.wait_ge(gates_ready, 3 * i + t)
                        for m in range(2):
                            ins = pe.matmul(G.ps[:, 6 + m, 0:TC], lru_w[:, m, :], xc[:, t * TC:(t + 1) * TC],
                                            start=True, stop=True)
                        ins.then_inc(lru_gemm, 1)
                    return go

                def pair(i):
                    G.products(pe, 2 * i + 1, 1, i)
                    G.products(pe, 2 * i + 2, 0, i + 1, {5: gate_round(i, 0), 6: gate_round(i, 1), 7: gate_round(i, 2)})
                pair(0)
                with pe.Fori(1, 8) as i:
                    pair(i)

                for g in range(len(groups)):
                    if g == 1:
                        gate_rows_pe(pe)
                    with pe.Fori(0, 4) as h:
                        for d in range(2):
                            G.products(pe, A_QKV0 + 8 * g + 2 * h + d, (1 + d) % 2, (A_QKV0 + 8 * g + d) // 2 + h)


LRU_DVE_STEPS = 13


class OutWeights:

    def __init__(self, S, a, name, w_d, first, tiles):
        self.rows = a.sb(name, [P, tiles, D])
        self.w_d, self.first, self.tiles = w_d, first, tiles
        self.loaded = S.a.sem(f"{name}_in")

    def load(self, sp, pair, done=None):
        sp.dma_start(self.rows[:, bass.ds(2 * pair, 2), :],
                     self.w_d[:, bass.ds(self.first + 2 * pair, 2), :]).then_inc(self.loaded if done is None else done, 16)


class OutProjection:

    def __init__(self, S, a, name, early, late, order, layer, x_d, y_d):
        self.w_low = a.sb(f"{name}_wout_lo", [P, 16, D], F32R)
        self.S, self.x_d, self.y_d = S, x_d, y_d
        self.early, self.late, self.order = early, late, order
        self.w_hi = a.sb(f"{name}_wout_hi", [P, 16, D], F32R)
        self.m_hi = a.sb(f"{name}_mix_hi", [P, 16, P], F32R)
        self.m_lo = a.sb(f"{name}_mix_lo", [P, 16, P], F32R)
        self.xres = a.sb(f"{name}_xres", [P, D])
        self.yb = a.sb(f"{name}_yb", [P, D])
        self.post = a.sb(f"{name}_post", [P, D])
        self.stat = a.sb(f"{name}_post_stat", [P, 6])
        self.layer = layer
        sem = S.a.sem
        self.late_in = [sem(f"{name}_wout_late_in{q}") for q in range(late.tiles // 2)] if late else []
        self.w_hi_ready = sem(f"{name}_wout_hi_ready")
        self.w_ready = sem(f"{name}_wout_ready")
        self.x_in = sem(f"{name}_xres_in")
        self.out_done = sem(f"{name}_out_done")
        self.squares = sem(f"{name}_squares")
        self.sq_sum = sem(f"{name}_square_sum")
        self.post_ln = sem(f"{name}_post_ln")
        self.post_rstd = sem(f"{name}_post_rstd")
        self.out_read = sem(f"{name}_out_read")
        self.y_ready = sem(f"{name}_y_ready")
        self.y_stored = sem(f"{name}_y_stored")

    def load_late(self, sp):
        for q, done in enumerate(self.late_in):
            self.late.load(sp, q, done)

    def load_post(self, sp, post_d):
        sp.dma_start(self.post[:], post_d[:, self.layer, :]).then_inc(self.y_stored, 16)

    def w_lo(self, e):
        return self.w_low[:, (e - self.early.first) % 16, :]

    def raw(self, e):
        w = self.early if self.early.first <= e < self.early.first + self.early.tiles else self.late
        return w.rows[:, e - w.first, :]

    def split_w_hi(self, act, k):
        for e in self.order[4 * k:4 * k + 4]:
            if self.late and e < self.early.first:
                act.wait_ge(self.late_in[e // 2], 16)
            else:
                act.wait_ge(self.early.loaded, 16 * self.early.tiles // 2)
            act.activation(self.w_hi[:, e, :], self.raw(e), ACT.Copy).then_inc(self.w_hi_ready, 1)

    def split_w_lo(self, dve, k):
        for j, e in enumerate(self.order[4 * k:4 * k + 4]):
            dve.wait_ge(self.w_hi_ready, 4 * k + j + 1)
            dve.tensor_tensor(self.w_lo(e), self.raw(e), self.w_hi[:, e, :].bitcast(F32), ALU.subtract
                              ).then_inc(self.w_ready, 1)

    def products(self, pe, ps, e, first, last, new_w):
        if new_w:
            pe.wait_ge(self.w_ready, self.order.index(e) + 1)
        w_lo = self.w_lo(e)
        for half in range(2):
            cols = slice(half * 512, half * 512 + 512)
            w_hi = self.w_hi[:, e, cols]
            for j, (m, w) in enumerate(((self.m_hi, w_hi), (self.m_hi, w_lo[:, cols]), (self.m_lo, w_hi))):
                ins = pe.matmul(ps[:, 6 + half, :], m[:, e, :], w, start=first and j == 0, stop=last and j == 2)
        if last:
            ins.then_inc(self.out_done, 1)

    def post_act(self, act, ps, c, rows):
        st = self.stat
        act.wait_ge(self.out_done, c + 1)
        for half in range(2):
            ins = act.activation(self.junk[0:rows, :], ps[0:rows, 6 + half, :], ACT.Square,
                                 accum_out=st[0:rows, half:half + 1])
            ins.then_inc(self.squares, 1)
            act.wait_ge(self.squares, 2 * c + half + 1)
        act.wait_ge(self.sq_sum, c + 1)
        act.activation(st[0:rows, 3:4], st[0:rows, 2:3], ACT.Ln, scale=1.0 / D, bias=self.S.eps[0:rows, :]).then_inc(self.post_ln, 1)
        act.wait_ge(self.post_ln, c + 1)
        act.activation(st[0:rows, 4:5], st[0:rows, 3:4], ACT.Exp, scale=-0.5).then_inc(self.post_rstd, 1)

    def post_dve(self, dve, ps, c, rows):
        st = self.stat
        dve.wait_ge(self.squares, 2 * c + 2)
        dve.tensor_tensor(st[0:rows, 2:3], st[0:rows, 0:1], st[0:rows, 1:2], ALU.add).then_inc(self.sq_sum, 1)
        dve.wait_ge(self.y_stored, 16 * c + 16)
        dve.wait_ge(self.post_rstd, c + 1)
        for half in range(2):
            cols = slice(half * 512, half * 512 + 512)
            ins = dve.scalar_tensor_tensor(out=self.yb[0:rows, cols], in0=ps[0:rows, 6 + half, :], scalar=st[0:rows, 4:5],
                                           in1=self.post[0:rows, cols], op0=ALU.mult, op1=ALU.mult)
        ins.then_inc(self.out_read, 1)

    def post_pool(self, pool, c, rows):
        pool.wait_ge(self.out_read, c + 1)
        pool.wait_ge(self.x_in, 16 * c + 16)
        pool.tensor_tensor(self.yb[0:rows, :], self.yb[0:rows, :], self.xres[0:rows, :], ALU.add).then_inc(self.y_ready, 1)

    def load_x(self, sp, c, rows, first):
        if not first:
            sp.wait_ge(self.y_ready, c)
        sp.dma_start(self.xres[0:rows, :], self.x_d[bass.ds(c * P, rows), :]).then_inc(self.x_in, 16)

    def store_y(self, sp, c, rows):
        sp.wait_ge(self.y_ready, c + 1)
        sp.dma_start(self.y_d[bass.ds(c * P, rows), :], self.yb[0:rows, :]).then_inc(self.y_stored, 16)


NRING = 4


def stage_mix_a(nc, S, scr_d, lru_d, w_early, w_late, post_d, x_d, y_d, c0_d, out_cp, out_cs):
    with ExitStack() as ctx:
        a = make_alloc(nc, ctx)
        sem = S.a.sem
        STEP_TILES = [(14, 15, 6, 7)] + [(6 + 2 * h, 7 + 2 * h, 2 * h - 2, 2 * h - 1) for h in range(1, H)]
        order = [8, 9, 10, 11, 0, 1, 12, 13, 2, 3, 14, 15, 4, 5, 6, 7]
        O = OutProjection(S, a, "ma", w_early, w_late, order, 0, x_d, y_d)
        hin = [a.sb(f"ma_hin{s}", [P, AF, P]) for s in range(2)]
        hl = a.sb("ma_hl", [P, 8, P])
        cst = a.sb("ma_state", [P, H, 2, MV])
        vv = [a.sb(f"ma_v{s}", [P, MV + 3]) for s in range(2)]
        og = [a.sb(f"ma_og{s}", [P, 256]) for s in range(2)]
        kw = [a.sb(f"ma_kw{s}", [P, 256]) for s in range(2)]
        ei = a.sb("ma_exponent", [P, P])
        ee = [a.sb(f"ma_decay{s}", [P, P]) for s in range(2)]
        sc = [a.sb(f"ma_scores{s}", [P, P]) for s in range(2)]
        inter = a.sb("ma_inter", [P, MV])
        num = a.sb("ma_num", [P, MV])
        gg = a.sb("ma_gated", [P, 256])
        gn = a.sb("ma_normed", [P, 256])
        mp = a.sb("ma_mix_plain", [P, 256])
        sm = a.sb("ma_small", [P, 8])
        O.junk = a.sb("ma_junk", [P, 512])
        kw8 = a.sb("ma_kw8", [LAST, 2, 256])
        qm = a.sb("ma_q_masked", [P, 2, 480])
        cs = [a.sb(f"ma_sample_state{r}", [P, 2, MV]) for r in range(NRING)]
        ps = a.ps("ma_ps", [P, 8, 512])

        hin_in = [sem(f"ma_hin_in{s}") for s in range(2)]
        z_in = [sem(f"ma_z_in{s}") for s in range(2)]
        hl_in = sem("ma_hl_in")
        hl_hi = sem("ma_hl_hi_ready")
        hl_ready = sem("ma_hl_ready")
        init_done = sem("ma_init_done")
        turned = sem("ma_turned")
        v_ready = sem("ma_v_ready")
        ei_ready = sem("ma_exponent_ready")
        e_ready = sem("ma_decay_ready")
        kw_ready = sem("ma_kw_ready")
        sc_ready = sem("ma_scores_ready")
        b_done = sem("ma_products_done")
        inter_ready = sem("ma_inter_ready")
        num_ready = sem("ma_num_ready")
        state_ready = sem("ma_state_ready")
        den_chain = sem("ma_den_chain")
        gated_ready = sem("ma_gated_ready")
        sq_chain = sem("ma_square_chain")
        rstd_ready = sem("ma_rstd_ready")
        gn_ready = sem("ma_normed_ready")
        c_done = sem("ma_head_turned")
        mp_ready = sem("ma_mix_plain_ready")
        mhi_ready = sem("ma_mix_hi_ready")
        mix_ready = sem("ma_mix_ready")
        qm_ready = sem("ma_q_masked_ready")
        s_in = [sem(f"ma_sample_in{r}") for r in range(NRING)]
        s_out = [sem(f"ma_sample_out{r}") for r in range(NRING)]
        upd_done = sem("ma_update_done")
        kw8_ready = sem("ma_group_keys_ready")
        s_ready = sem("ma_sample_ready")
        s_read = sem("ma_update_read")
        p_stored = sem("ma_prompt_state_stored")
        pool_chain = sem("ma_pool_chain")

        BQ, BK, BV, BO, BZ = (slice(2 * j, 2 * j + 2) for j in range(5))
        LASTS = [TAIL - 1] + [TAIL + SLEN * b + SLEN - 1 for b in range(NSEQ)]

        def not_first(n, least=1):
            return not (isinstance(n, int) and n < least)

        with nc.Block() as block:
            @block.sync
            def _(sp):
                def load_head(n, c, h, rows):
                    piece = scr_d[bass.ds(c, 1), h, :, :, 0:rows].rearrange("o p f t -> (o p) f t")
                    if not_first(n, 2):
                        sp.wait_ge(b_done, n - 1)
                    sp.dma_start(hin[h % 2][:, 0:8, 0:rows], piece[:, 0:8, :]).then_inc(hin_in[h % 2], 16)
                    if not_first(n, 2):
                        sp.wait_ge(mp_ready, n - 1)
                    sp.dma_start(hin[h % 2][:, 8:10, 0:rows], piece[:, 8:10, :]).then_inc(z_in[h % 2], 16)

                def load_hl(c, rows):
                    if not_first(c):
                        sp.wait_ge(hl_ready, c)
                    sp.dma_start(hl[:, :, 0:rows], lru_d[bass.ds(c, 1), :, :, 0:rows].rearrange("o p f t -> (o p) f t")
                                 ).then_inc(hl_in, 16)
                load_head(0, 0, 0, P)
                load_head(1, 0, 1, P)
                load_hl(0, P)
                O.load_late(sp)
                O.load_post(sp, post_d)
                O.load_x(sp, 0, P, True)
                load_head(2, 0, 2, P)
                load_head(3, 0, 3, P)

                with sp.Fori(1, 8) as c:
                    load_head(4 * c, c, 0, P)
                    load_hl(c, P)
                    for h in range(1, H):
                        load_head(4 * c + h, c, h, P)
                    O.store_y(sp, c - 1, P)
                    O.load_x(sp, c, P, False)
                load_head(32, 8, 0, LAST)
                load_hl(8, LAST)
                load_head(33, 8, 1, LAST)

                def load_state(m):
                    r = m % NRING
                    if m >= NRING:
                        sp.wait_ge(s_out[r], 16 * (m // NRING))
                    sp.dma_start(cs[r][:], c0_d[m % NSEQ, m // NSEQ]).then_inc(s_in[r], 16)

                def store_state(m):
                    r = m % NRING
                    sp.wait_ge(s_ready, m + 1)
                    sp.dma_start(out_cs[m % NSEQ, m // NSEQ], cs[r][:]).then_inc(s_out[r], 16)
                for m in range(NRING):
                    load_state(m)
                O.store_y(sp, 7, P)
                O.load_x(sp, 8, LAST, False)
                for h in range(H):
                    for b in range(NSEQ):
                        m = h * NSEQ + b
                        store_state(m)
                        if m + NRING < H * NSEQ:
                            load_state(m + NRING)
                    sp.wait_ge(state_ready, 32 + h + 1)
                    sp.dma_start(out_cp[h], cst[:, h, :, :]).then_inc(p_stored, 16)
                    if h < 2:
                        load_head(34 + h, 8, 2 + h, LAST)
                O.store_y(sp, 8, LAST)
                sp.wait_ge(O.y_stored, 16 * NC + 16)
                sp.wait_ge(p_stored, 16 * H)
                for r in range(NRING):
                    sp.wait_ge(s_out[r], 16 * (H * NSEQ // NRING))

            @block.tensor
            def _(pe):
                def part_a(n, c, h, s, rows):
                    pe.wait_ge(hin_in[s], 16 * (2 * c + h // 2) + 16)
                    t = hin[s]
                    for d in range(2):
                        pe.transpose(ps[0:rows, 1, 256 + d * P:256 + (d + 1) * P], t[:, 2 + d, 0:rows], S.ident[:])
                        pe.transpose(ps[0:rows, 1, d * P:(d + 1) * P], t[:, 4 + d, 0:rows], S.ident[:])
                        pe.transpose(ps[0:rows, 0, 256 + d * P:256 + (d + 1) * P], t[:, 6 + d, 0:rows], S.ident[:])
                    pe.matmul(ps[0:rows, 0, 128:128 + rows], S.sel[:, h, 0:rows], S.rrow[:, bass.ds(c * P, rows)],
                              start=True, stop=True)
                    for d in range(2):
                        ins = pe.matmul(ps[0:rows, 0, 0:rows], t[:, 2 + d, 0:rows], t[:, d, 0:rows], start=(d == 0), stop=(d == 1))
                    ins.then_inc(turned, 1)

                def part_b(n, c, h, s):
                    if not_first(n):
                        pe.wait_ge(num_ready, n)
                        pe.wait_ge(state_ready, n)
                    else:
                        pe.wait_ge(init_done, 1)
                    for d in range(2):
                        pe.matmul(ps[:, 2, 0:MV], hin[s][:, d, :], cst[:, h, d, :], start=(d == 0), stop=(d == 1))
                    pe.wait_ge(v_ready, n + 1)
                    pe.wait_ge(sc_ready, n + 1)
                    pe.matmul(ps[:, 3, 0:MV], sc[s][:], vv[s][:, 0:MV], start=True, stop=True)
                    pe.wait_ge(kw_ready, n + 1)
                    if not_first(n):
                        pe.wait_ge(mp_ready, n)
                    for d in range(2):
                        ins = pe.matmul(ps[:, 4 + d, 0:MV], kw[s][:, d * P:(d + 1) * P], vv[s][:, 0:MV], start=True, stop=True)
                    ins.then_inc(b_done, 1)

                def part_c(n, s, rows):
                    pe.wait_ge(gn_ready, n + 1)
                    for d in range(2):
                        ins = pe.transpose(ps[:, 4 + d, 384:384 + rows], gn[0:rows, d * P:(d + 1) * P], S.ident[0:rows, 0:rows])
                    ins.then_inc(c_done, 1)

                def out(c, h, new_w):
                    for e in STEP_TILES[(h + 1) % H]:
                        if e == 8:
                            pe.wait_ge(hl_ready, c + 1)
                            if not_first(c):
                                pe.wait_ge(O.out_read, c)
                        if e < 8 and e % 2 == 0:
                            pe.wait_ge(mix_ready, 4 * c + e // 2 + 1)
                        O.products(pe, ps, e, e == 8, e == 7, new_w)

                def chunk(c, first, last):
                    for h in range(H):
                        n, h1 = 4 * c + h, (h + 1) % H
                        c1 = c + (h == 3)
                        if not (last and h == 3):
                            part_a(n + 1, c1, h1, h1 % 2, P)
                        if not (first and h == 0):
                            out(c - (h == 0), (h - 1) % H, first)
                        part_c(n, h % 2, P)
                        if not (last and h == 3):
                            part_b(n + 1, c1, h1, h1 % 2)
                part_a(0, 0, 0, 0, P)
                part_b(0, 0, 0, 0)
                chunk(0, True, False)
                pe.wait_ge(O.w_ready, 16)
                with pe.Fori(1, 7) as c:
                    chunk(c, False, False)
                chunk(7, False, True)
                out(7, 3, False)

                pe.wait_ge(O.out_read, 8)
                part_a(32, 8, 0, 0, LAST)
                for h in range(H):
                    n, s = 32 + h, h % 2
                    pe.wait_ge(num_ready, n)
                    pe.wait_ge(state_ready, n)
                    pe.wait_ge(mp_ready, n)
                    pe.wait_ge(qm_ready, h + 1)
                    pe.wait_ge(v_ready, n + 1)
                    for g in range(NG):
                        m = h * NSEQ + g - 1
                        r = m % NRING
                        if g:
                            pe.wait_ge(s_in[r], 16 * (m // NRING) + 16)
                        for d in range(2):
                            st = cst[:, h, d, :] if g == 0 else cs[r][:, d, :]
                            pe.matmul(ps[0:LAST, 2, 0:MV], qm[:, d, g * LAST:(g + 1) * LAST], st,
                                      start=(g == 0 and d == 0), stop=(g == NG - 1 and d == 1))
                        u = h * NG + g
                        if u >= 2:
                            pe.wait_ge(s_read, u - 1)
                        pe.wait_ge(kw8_ready, u + 1)
                        for d in range(2):
                            ins = pe.matmul(ps[:, 4 + 2 * (u % 2) + d, 0:MV], kw8[:, u % 2, d * P:(d + 1) * P],
                                            vv[s][0:LAST, 0:MV], start=True, stop=True)
                        ins.then_inc(upd_done, 1)
                    pe.wait_ge(sc_ready, n + 1)
                    pe.matmul(ps[0:LAST, 3, 0:MV], sc[s][0:LAST, 0:LAST], vv[s][0:LAST, 0:MV], start=True, stop=True).then_inc(b_done, 1)
                    if h < 3:
                        part_a(n + 1, 8, h + 1, 1 - s, LAST)
                    part_c(n, s, LAST)
                pe.wait_ge(s_read, H * NG)
                pe.wait_ge(hl_ready, 9)
                for e in [*range(8, 16), *range(8)]:
                    if e < 8 and e % 2 == 0:
                        pe.wait_ge(mix_ready, 32 + e // 2 + 1)
                    O.products(pe, ps, e, e == 8, e == 7, False)

            @block.scalar
            def _(act):
                act.preload_act_table_set('natural_log_exp_and_others')
                def hl_split(c, rows):
                    act.wait_ge(hl_in, 16 * c + 16)
                    if not_first(c):
                        act.wait_ge(O.out_done, c)
                    act.activation(O.m_hi[:, 8:16, 0:rows], hl[:, :, 0:rows], ACT.Copy).then_inc(hl_hi, 1)

                def copies(n, s, rows):
                    act.wait_ge(turned, n + 1)
                    if not_first(n, 2):
                        act.wait_ge(b_done, n - 1)
                    act.activation(vv[s][0:rows, 0:256], ps[0:rows, 1, 0:256], ACT.Copy).then_inc(v_ready, 1)
                    act.wait_ge(ei_ready, n + 1)
                    act.activation(ee[s][0:rows, 0:rows], ei[0:rows, 0:rows], ACT.Exp).then_inc(e_ready, 1)
                    act.wait_ge(e_ready, n + 1)

                def part_a(n, s):
                    copies(n, s, P)
                    act.activation(kw[s][:], ps[:, 1, 256:512], ACT.Copy, scale=ee[s][:, P - 1:P]).then_inc(kw_ready, 1)

                def part_b(n, c, h, rows):
                    act.wait_ge(b_done, n + 1)
                    w = S.tok[0:rows, bass.ds(c, 1), 1, h]
                    act.activation(inter[0:rows, :], ps[0:rows, 2, 0:MV], ACT.Copy, scale=w).then_inc(inter_ready, 1)

                def part_c(n, rows):
                    act.wait_ge(gated_ready, n + 1)
                    act.activation(O.junk[0:rows, 0:256], gg[0:rows, :], ACT.Square, accum_out=sm[0:rows, 4:5]).then_inc(sq_chain, 1)
                    act.wait_ge(sq_chain, 2 * n + 1)
                    act.activation(sm[0:rows, 5:6], sm[0:rows, 4:5], ACT.Ln, scale=1.0 / 256, bias=S.eps[0:rows, :]).then_inc(sq_chain, 1)
                    act.wait_ge(sq_chain, 2 * n + 2)
                    act.activation(sm[0:rows, 6:7], sm[0:rows, 5:6], ACT.Exp, scale=-0.5).then_inc(rstd_ready, 1)

                def part_m(n, c, h, rows):
                    act.wait_ge(mp_ready, n + 1)
                    if h == 0 and not_first(c):
                        act.wait_ge(O.out_done, c)
                    act.activation(O.m_hi[:, 2 * h:2 * h + 2, 0:rows], mp[:].rearrange("p (d t) -> p d t", d=2)[:, :, 0:rows], ACT.Copy
                                   ).then_inc(mhi_ready, 1)

                def chunk(c, first, last):
                    for h in range(H):
                        n = 4 * c + h
                        part_b(n, c, h, P)
                        part_c(n, P)
                        if not (last and h == 3):
                            part_a(n + 1, (h + 1) % 2)
                        if first:
                            O.split_w_hi(act, h)
                        if h == 0:
                            if not first:
                                O.post_act(act, ps, c - 1, P)
                            hl_split(c, P)
                        part_m(n, c, h, P)
                part_a(0, 0)
                chunk(0, True, False)
                with act.Fori(1, 7) as c:
                    chunk(c, False, False)
                chunk(7, False, True)
                O.post_act(act, ps, 7, P)
                copies(32, 0, LAST)
                for h in range(H):
                    n, s = 32 + h, h % 2
                    for g in range(NG):
                        u = h * NG + g
                        if u >= 2:
                            act.wait_ge(upd_done, u - 1)
                        act.activation(kw8[:, u % 2, :], ps[0:LAST, 1, 256:512], ACT.Copy,
                                       scale=ee[s][0:LAST, LASTS[g]:LASTS[g] + 1]).then_inc(kw8_ready, 1)
                    part_b(n, 8, h, LAST)
                    part_c(n, LAST)
                    if h == 0:
                        hl_split(8, LAST)
                    if h < 3:
                        copies(n + 1, 1 - s, LAST)
                    part_m(n, 8, h, LAST)
                O.post_act(act, ps, 8, LAST)

            @block.vector
            def _(dve):
                for s in range(2):
                    dve.memset(vv[s][:, 256:257], 1.0)
                dve.memset(cst[:], 0.0).then_inc(init_done, 1)

                def part_a1(n, c, h, s, rows, mask):
                    dve.wait_ge(turned, n + 1)
                    if not_first(n):
                        dve.wait_ge(e_ready, n)
                    dve.scalar_tensor_tensor(out=ei[0:rows, 0:rows], in0=ps[0:rows, 0, 128:128 + rows],
                                             scalar=S.tok[0:rows, bass.ds(c, 1), 0, h], in1=mask[:],
                                             op0=ALU.add, op1=ALU.add).then_inc(ei_ready, 1)
                    if not_first(n, 2):
                        dve.wait_ge(gated_ready, n - 1)
                    dve.tensor_copy(og[s][0:rows, :], ps[0:rows, 0, 256:512])

                def part_a2(n, s, rows):
                    dve.wait_ge(e_ready, n + 1)
                    if not_first(n, 2):
                        dve.wait_ge(b_done, n - 1)
                    dve.tensor_tensor(sc[s][0:rows, 0:rows], ps[0:rows, 0, 0:rows], ee[s][0:rows, 0:rows], ALU.mult).then_inc(sc_ready, 1)

                def part_num(n, rows):
                    dve.wait_ge(inter_ready, n + 1)
                    dve.tensor_tensor(num[0:rows, :], inter[0:rows, :], ps[0:rows, 3, 0:MV], ALU.add).then_inc(num_ready, 1)

                def update(dst, scale, bank):
                    for d in range(2):
                        ins = dve.scalar_tensor_tensor(out=dst[:, d, :], in0=dst[:, d, :], scalar=scale,
                                                       in1=ps[:, bank + d, 0:MV], op0=ALU.mult, op1=ALU.add)
                    return ins

                def part_den(n, c, h, s, rows):
                    link = linker(dve, den_chain, 3 * n)
                    dve.wait_ge(num_ready, n + 1)
                    link(dve.scalar_tensor_tensor(out=sm[0:rows, 0:1], in0=num[0:rows, 256:257], scalar=-1.0,
                                                  in1=num[0:rows, 256:257], op0=ALU.mult, op1=ALU.max))
                    link(dve.tensor_tensor(sm[0:rows, 1:2], sm[0:rows, 0:1], S.tok[0:rows, bass.ds(c, 1), 2, h], ALU.max))
                    link(dve.reciprocal(sm[0:rows, 2:3], sm[0:rows, 1:2]))
                    dve.scalar_tensor_tensor(out=gg[0:rows, :], in0=num[0:rows, 0:256], scalar=sm[0:rows, 2:3],
                                             in1=og[s][0:rows, :], op0=ALU.mult, op1=ALU.mult).then_inc(gated_ready, 1)

                def part_c(n, rows):
                    dve.wait_ge(rstd_ready, n + 1)
                    dve.tensor_scalar(gn[0:rows, :], gg[0:rows, :], sm[0:rows, 6:7], None, ALU.mult).then_inc(gn_ready, 1)

                def part_m(n, c, h, s, rows):
                    dve.wait_ge(c_done, n + 1)
                    dve.wait_ge(z_in[s], 16 * (2 * c + h // 2) + 16)
                    if not_first(n):
                        dve.wait_ge(mix_ready, n)
                    for d in range(2):
                        ins = dve.tensor_tensor(mp[:, d * P:d * P + rows], ps[:, 4 + d, 384:384 + rows], hin[s][:, 8 + d, 0:rows], ALU.mult)
                    ins.then_inc(mp_ready, 1)

                def chunk(c, first, last):
                    for h in range(H):
                        n, s = 4 * c + h, h % 2
                        part_num(n, P)
                        part_den(n, c, h, s, P)
                        update(cst[:, h, :, :], S.wc[:, h, bass.ds(c, 1)], 4).then_inc(state_ready, 1)
                        if not (last and h == 3):
                            part_a1(n + 1, c + (h == 3), (h + 1) % H, 1 - s, P, S.mask_add)
                        part_c(n, P)
                        if not (last and h == 3):
                            part_a2(n + 1, 1 - s, P)
                        if first:
                            O.split_w_lo(dve, h)
                        part_m(n, c, h, s, P)
                        if h == 0 and not first:
                            O.post_dve(dve, ps, c - 1, P)
                part_a1(0, 0, 0, 0, P, S.mask_add)
                part_a2(0, 0, P)
                chunk(0, True, False)
                with dve.Fori(1, 7) as c:
                    chunk(c, False, False)
                chunk(7, False, True)
                O.post_dve(dve, ps, 7, P)
                part_a1(32, 8, 0, 0, LAST, S.mask_add8)
                part_a2(32, 0, LAST)
                for h in range(H):
                    n, s = 32 + h, h % 2
                    for g in range(NG):
                        u = h * NG + g
                        dve.wait_ge(upd_done, u + 1)
                        bank = 4 + 2 * (u % 2)
                        if g == 0:
                            update(cst[:, h, :, :], S.wc[:, h, 8:9], bank).then_inc(state_ready, 1)
                            dve.wait_ge(state_ready, n + 1)
                        else:
                            m = u - h - 1
                            update(cs[m % NRING][:], S.wc[:, h, 8 + g:9 + g], bank).then_inc(s_ready, 1)
                            dve.wait_ge(s_ready, m + 1)
                        dve.sem_inc(s_read, 1)
                    part_num(n, LAST)
                    part_den(n, 8, h, s, LAST)
                    part_c(n, LAST)
                    if h < 3:
                        part_a1(n + 1, 8, h + 1, 1 - s, LAST, S.mask_add8)
                        part_a2(n + 1, 1 - s, LAST)
                    part_m(n, 8, h, s, LAST)
                O.post_dve(dve, ps, 8, LAST)

            @block.gpsimd
            def _(pool):
                link = linker(pool, pool_chain)
                link(pool.memset(qm[:], 0.0))

                def lo(tiles, plain, rows):
                    return pool.tensor_tensor(O.m_lo[:, tiles, 0:rows], plain, O.m_hi[:, tiles, 0:rows].bitcast(F32), ALU.subtract)

                def masked_q(h):
                    pool.wait_ge(hin_in[h % 2], 16 * (16 + h // 2) + 16)
                    if h:
                        pool.wait_ge(upd_done, NG * h)
                    for d in range(2):
                        q = hin[h % 2][:, d, :]
                        pool.tensor_copy(qm[:, d, 0:TAIL], q[:, 0:TAIL])
                        ins = pool.tensor_copy(qm[:, d, 64:480].rearrange("p (s r) -> p s r", r=LAST + SLEN)[:, :, 0:SLEN],
                                               q[:, TAIL:LAST].rearrange("p (s t) -> p s t", t=SLEN))
                    ins.then_inc(qm_ready, 1)

                def lo_head(c, h, rows):
                    pool.wait_ge(mhi_ready, 4 * c + h + 1)
                    lo(slice(2 * h, 2 * h + 2), mp[:].rearrange("p (d t) -> p d t", d=2)[:, :, 0:rows], rows).then_inc(mix_ready, 1)

                def lo_hl(c, rows):
                    pool.wait_ge(hl_hi, c + 1)
                    lo(slice(8, 16), hl[:, :, 0:rows], rows).then_inc(hl_ready, 1)

                def chunk(c, first):
                    lo_hl(c, P)
                    lo_head(c, 0, P)
                    if not first:
                        O.post_pool(pool, c - 1, P)
                    for h in range(1, H):
                        lo_head(c, h, P)
                chunk(0, True)
                with pool.Fori(1, 8) as c:
                    chunk(c, False)
                O.post_pool(pool, 7, P)
                for h in range(H):
                    masked_q(h)
                    if h == 0:
                        lo_hl(8, LAST)
                    lo_head(8, h, LAST)
                O.post_pool(pool, 8, LAST)


def stage_project_c(nc, S, w_d, a_up_d, scr_d, w_out):
    with ExitStack() as ctx:
        a = make_alloc(nc, ctx)
        G = Projection(nc, S, a, "pc", w_d, C_TILES)
        stage = [a.sb(f"pc_stage{s}", [P, 3, TC]) for s in range(2)]
        flat = [s[:].rearrange("p a b -> p (a b)") for s in stage]
        alow = a.sb("pc_alow", [16, TP])
        a_up = a.sb("pc_a_up", [16, P])
        xg = a.sb("pc_gate", [P, TP])
        ab = a.sb("pc_gate_abs", [P, TP])
        bsum = a.sb("pc_decay_sum", [P, T])
        eq = a.sb("pc_exp_q", [P, 3, TC])
        ek = a.sb("pc_exp_k", [P, 3, TC])
        eqf, ekf = (e[:].rearrange("p a b -> p (a b)") for e in (eq, ek))
        gt = a.sb("pc_group_sum", [P, 17])
        par = a.sb("pc_bias", [P, 1])
        mid = a.sb("pc_mid", [P, 8])

        sem = S.a.sem
        alow_ready = sem("pc_alow_ready")
        a_up_in = sem("pc_a_up_in")
        lg_done = sem("pc_log_gate_done")
        lg_read = sem("pc_log_gate_read")
        act_chain = sem("pc_act_chain")
        soft_ready = sem("pc_softplus_ready")
        par_ready = sem("pc_bias_ready")
        dve_chain = sem("pc_dve_chain")
        cent_ready = sem("pc_centred_ready")
        exps_ready = sem("pc_exps_ready")
        qk_ready = sem("pc_qk_ready")
        v_ready = sem("pc_v_ready")
        r_ready = sem("pc_r_ready")
        sigmoid_ready = sem("pc_sigmoid_ready")
        spilled = [sem(f"pc_spilled{s}") for s in range(2)]

        def n_slot(d):
            return (C_V0 + d) % 2

        def seqs(buf):
            return buf[:, NP_TOK:T].rearrange("p (s t) -> p s t", t=SLEN)

        def chunked(buf):
            return buf[:, 0:8 * P].rearrange("p (c t) -> p c t", t=P)

        with nc.Block() as block:
            @block.sync
            def _(sp):
                def spill(ready, m, s, head, f):
                    sp.wait_ge(ready, m + 1)
                    dst = scr_d[0:8, bass.ds(head, 1), :, f, :].rearrange("c o p t -> p (o c) t")
                    sp.dma_start(dst, flat[s][:, 0:8 * P].rearrange("p (c t) -> p c t", t=P)).then_inc(spilled[s], 16)
                    sp.dma_start(scr_d[8, bass.ds(head, 1), :, f, 0:LAST].rearrange("o p t -> (o p) t"),
                                 flat[s][:, 8 * P:T]).then_inc(spilled[s], 16)
                for n in range(3):
                    G.load(sp, n, n % 2)
                with sp.Fori(0, 4) as hh:
                    for d in range(2):
                        i = 2 * hh + d
                        n = 2 * i + 1
                        sp.wait_ge(lg_done, 3 * i)
                        sp.dma_start(a_up[:], a_up_d[:, bass.ds(i, 1), :].rearrange("r o k -> r (o k)")).then_inc(a_up_in, 16)
                        G.load(sp, n + 2, 1)
                        G.load(sp, n + 3, 0)
                        spill(qk_ready, 2 * i, 1, hh, d)
                        spill(qk_ready, 2 * i + 1, 0, hh, 2 + d)

                def two(g, h, d, tail):
                    n = C_V0 + 16 * g + 4 * h + d
                    if not tail:
                        G.load(sp, n + 2, n_slot(d))
                    spill((v_ready, r_ready)[g], 4 * h + d, n_slot(d), h, 4 + 4 * g + d)
                for g in range(2):
                    with sp.Fori(0, 4 - g) as h:
                        w_out.load(sp, h + 4 * g)
                        for d in range(4):
                            two(g, h, d, False)
                w_out.load(sp, 7)
                for d in range(4):
                    two(1, 3, d, d >= 2)
                for s in range(2):
                    sp.wait_ge(spilled[s], 32 * 24)

            @block.scalar
            def _(act):
                act.preload_act_table_set('natural_log_exp_and_others')
                G.split_hi(act, 0, 0, 0)
                G.split_hi(act, 1, 1, 0)
                act.wait_ge(G.gemm_done, 1)
                for t in range(3):
                    ins = act.activation(alow[:, t * TC:(t + 1) * TC], G.ps[0:16, t, 0:TC], ACT.Copy)
                ins.then_inc(alow_ready, 1)
                G.split_hi(act, 2, 0, 1)
                with act.Fori(0, 4) as hh:
                    for d in range(2):
                        i = 2 * hh + d
                        n = 2 * i + 1
                        link = linker(act, act_chain, i)
                        ba = par[:]
                        act.wait_ge(par_ready, i + 1)
                        for t in range(3):
                            act.wait_ge(lg_done, 3 * i + t + 1)
                            act.activation(ab[:, t * TC:(t + 1) * TC], G.ps[:, 6 + t % 2, 0:TC], ACT.Abs, bias=ba)
                            act.activation(xg[:, t * TC:(t + 1) * TC], G.ps[:, 6 + t % 2, 0:TC], ACT.Identity, bias=ba
                                           ).then_inc(lg_read, 1)
                        act.wait_ge(lg_read, 3 * i + 3)
                        link(act.activation(ab[:], ab[:], ACT.Exp, scale=-1.0))
                        act.activation(ab[:], ab[:], ACT.Ln, bias=1.0).then_inc(soft_ready, 1)
                        G.split_hi(act, n + 2, 1, i + 1)
                        act.wait_ge(cent_ready, i + 1)
                        act.wait_ge(qk_ready, 2 * i)
                        act.activation(eqf[:, 0:T], bsum[:], ACT.Exp, scale=1.0 / 16)
                        act.activation(S.gf[:, bass.ds(i, 1), :].rearrange("p o g -> p (o g)"), gt[:], ACT.Exp, scale=1.0 / 16)
                        act.activation(ekf[:, 0:T], bsum[:], ACT.Exp, scale=-1.0 / 16).then_inc(exps_ready, 1)
                        G.split_hi(act, n + 3, 0, i + 2)
                act.preload_act_table_set('sigmoid_and_others')

                def tile(g, h, d, tail):
                    s = n_slot(d)
                    n = C_V0 + 16 * g + 4 * h + d
                    act.wait_ge(G.gemm_done, n + 1)
                    act.wait_ge(spilled[s], 32 * (8 + 8 * g + 2 * h + d // 2))
                    if g == 0:
                        act.activation(stage[s][:], G.bank(s), ACT.Copy).then_inc(v_ready, 1)
                        act.wait_ge(v_ready, 4 * h + d + 1)
                        act.sem_inc(G.psum_free[s], 1)
                    else:
                        act.activation(stage[s][:], G.bank(s), ACT.Sigmoid).then_inc(sigmoid_ready, 1)
                    if not tail:
                        G.split_hi(act, n + 2, s, (C_V0 + 16 * g + d) // 2 + 1 + 2 * h)
                for g in range(2):
                    with act.Fori(0, 4 - g) as h:
                        for d in range(4):
                            tile(g, h, d, False)
                for d in range(4):
                    tile(1, 3, d, d >= 2)

            @block.vector
            def _(dve):
                dve.memset(eqf[:, T:TP], 0.0)
                dve.memset(ekf[:, T:TP], 0.0)
                G.split_lo(dve, 0, 0)
                G.split_lo(dve, 1, 1)
                dve.wait_ge(alow_ready, 1)
                dve.sem_inc(G.psum_free[0], 1)
                G.split_lo(dve, 2, 0)
                dve.tensor_copy(par[:], S.vecs[:, V_ALPHAB:V_ALPHAB + 1]).then_inc(par_ready, 1)
                K = 5
                with dve.Fori(0, 4) as hh:
                    for d in range(2):
                        i = 2 * hh + d
                        n = 2 * i + 1
                        link = linker(dve, dve_chain, K * i)
                        dve.wait_ge(soft_ready, i + 1)
                        link(dve.scalar_tensor_tensor(out=xg[:, 0:T], in0=xg[:, 0:T], scalar=0.0, in1=ab[:, 0:T],
                                                      op0=ALU.min, op1=ALU.subtract))
                        dve.wait_ge(exps_ready, i)
                        link(dve.tensor_tensor_scan(bsum[:], S.reset[:], xg[:, 0:T], 0.0, ALU.mult, ALU.add))
                        link(dve.tensor_tensor(gt[:, 0:8], chunked(bsum)[:, :, P - 1], chunked(bsum)[:, :, P // 2 - 1], ALU.subtract))
                        link(dve.tensor_tensor(gt[:, 0:7], gt[:, 0:7], chunked(bsum)[:, 1:8, P // 2 - 1], ALU.add))
                        dve.tensor_copy(gt[:, 8:9], bsum[:, NP_TOK - 1:NP_TOK])
                        dve.tensor_copy(gt[:, 9:17], seqs(bsum)[:, :, SLEN - 1])
                        link(dve.tensor_copy(mid[:], chunked(bsum)[:, :, P // 2 - 1]))
                        assert link.count() == K
                        dve.tensor_tensor(chunked(bsum), chunked(bsum), mid[:].unsqueeze(2).to_broadcast([P, 8, P]), ALU.subtract
                                          ).then_inc(cent_ready, 1)
                        dve.tensor_copy(par[:], S.vecs[:, bass.ds(V_ALPHAB + 1 + i, 1)]).then_inc(par_ready, 1)
                        G.split_lo(dve, n + 2, 1)
                        dve.wait_ge(exps_ready, i + 1)
                        dve.wait_ge(spilled[1], 32 * i)
                        dve.scalar_tensor_tensor(out=stage[1][:], in0=G.bank(1), scalar=DK ** -0.5, in1=eq[:],
                                                 op0=ALU.mult, op1=ALU.mult).then_inc(qk_ready, 1)
                        dve.wait_ge(qk_ready, 2 * i + 1)
                        dve.sem_inc(G.psum_free[1], 1)
                        dve.wait_ge(G.gemm_done, n + 2)
                        dve.wait_ge(spilled[0], 32 * i)
                        dve.tensor_tensor(stage[0][:], G.bank(0), ek[:], ALU.mult).then_inc(qk_ready, 1)
                        dve.wait_ge(qk_ready, 2 * i + 2)
                        dve.sem_inc(G.psum_free[0], 1)
                        G.split_lo(dve, n + 3, 0)

                def tile(g, h, d, tail):
                    s = n_slot(d)
                    n = C_V0 + 16 * g + 4 * h + d
                    if g == 1:
                        dve.wait_ge(sigmoid_ready, 4 * h + d + 1)
                        dve.scalar_tensor_tensor(out=stage[s][:], in0=G.bank(s), scalar=S.vecs[:, bass.ds(V_GNORM + 4 * h + d, 1)],
                                                 in1=stage[s][:], op0=ALU.mult, op1=ALU.mult).then_inc(r_ready, 1)
                        dve.wait_ge(r_ready, 4 * h + d + 1)
                        dve.sem_inc(G.psum_free[s], 1)
                    if not tail:
                        G.split_lo(dve, n + 2, s)
                for g in range(2):
                    with dve.Fori(0, 4 - g) as h:
                        for d in range(4):
                            tile(g, h, d, False)
                for d in range(4):
                    tile(1, 3, d, d >= 2)

            @block.tensor
            def _(pe):
                G.products(pe, 0, 0, 0)

                def gate_round(i, t):
                    def go():
                        if t == 0:
                            pe.wait_ge(alow_ready, 1)
                            pe.wait_ge(a_up_in, 16 * i + 16)
                            pe.wait_ge(lg_read, 3 * i)
                        if t == 2:
                            pe.wait_ge(lg_read, 3 * i + 1)
                        pe.matmul(G.ps[:, 6 + t % 2, 0:TC], a_up[:], alow[:, t * TC:(t + 1) * TC], start=True, stop=True
                                  ).then_inc(lg_done, 1)
                    return go
                with pe.Fori(0, 4) as hh:
                    for d in range(2):
                        i = 2 * hh + d
                        G.products(pe, 2 * i + 1, 1, i, {1: gate_round(i, 0), 2: gate_round(i, 1), 3: gate_round(i, 2)})
                        G.products(pe, 2 * i + 2, 0, i + 1)
                with pe.Fori(0, 8) as h:
                    for d in range(4):
                        G.products(pe, C_V0 + 4 * h + d, n_slot(d), (C_V0 + d) // 2 + 2 * h)


def stage_mix_c(nc, S, scr_d, w_early, post_d, x_d, y_d, s0_d, out_sp, out_ss):
    with ExitStack() as ctx:
        a = make_alloc(nc, ctx)
        sem = S.a.sem
        O = OutProjection(S, a, "mc", w_early, None, list(range(16)), 1, x_d, y_d)
        hin = [a.sb(f"mc_hin{s}", [P, CF, P]) for s in range(2)]
        cst = a.sb("mc_state", [P, H, 2, GV])
        vv = [a.sb(f"mc_v{s}", [P, GV]) for s in range(2)]
        kk = [a.sb(f"mc_k{s}", [P, 256]) for s in range(2)]
        sc = [a.sb(f"mc_scores{s}", [P, P]) for s in range(2)]
        sc8 = a.sb("mc_scores_last", [LAST, LAST])
        gn = a.sb("mc_normed", [P, GV])
        mp = a.sb("mc_mix_plain", [P, GV])
        sm = a.sb("mc_small", [P, 4])
        gfc = a.sb("mc_factors", [P, 8])
        O.junk = mp
        kw8 = a.sb("mc_group_keys", [LAST, 2, 256])
        qm = a.sb("mc_q_masked", [P, 2, 480])
        cs = [a.sb(f"mc_sample_state{r}", [P, 2, GV]) for r in range(CRING)]
        ps = a.ps("mc_ps", [P, 8, 512])

        hin_in = [sem(f"mc_hin_in{s}") for s in range(2)]
        r_in = [sem(f"mc_r_in{s}") for s in range(2)]
        init_done = sem("mc_init_done")
        turned = sem("mc_turned")
        v_ready = sem("mc_v_ready")
        k_ready = sem("mc_k_ready")
        sc_ready = sem("mc_scores_ready")
        b_done = sem("mc_products_done")
        added = sem("mc_state_added")
        gfc_ready = sem("mc_factors_ready")
        state_ready = sem("mc_state_ready")
        sq_chain = sem("mc_square_chain")
        gn_ready = sem("mc_normed_ready")
        c_done = sem("mc_head_turned")
        mp_ready = sem("mc_mix_plain_ready")
        mhi_ready = sem("mc_mix_hi_ready")
        mix_ready = sem("mc_mix_ready")
        head_out = sem("mc_head_out_done")
        qm_ready = sem("mc_q_masked_ready")
        s_in = [sem(f"mc_sample_in{r}") for r in range(CRING)]
        s_out = [sem(f"mc_sample_out{r}") for r in range(CRING)]
        upd_done = sem("mc_update_done")
        s_added = sem("mc_sample_added")
        s_ready = sem("mc_sample_ready")
        p_stored = sem("mc_prompt_state_stored")
        pool_chain = sem("mc_pool_chain")
        kw8_ready = sem("mc_group_keys_ready")

        with nc.Block() as block:
            @block.sync
            def _(sp):
                def load_head(n, c, h, rows, first=False):
                    piece = scr_d[bass.ds(c, 1), h, :, :, 0:rows].rearrange("o p f t -> (o p) f t")
                    if not first:
                        sp.wait_ge(b_done, n - 1)
                    sp.dma_start(hin[h % 2][:, 0:8, 0:rows], piece[:, 0:8, :]).then_inc(hin_in[h % 2], 16)
                    if not first:
                        sp.wait_ge(mp_ready, n - 1)
                    sp.dma_start(hin[h % 2][:, 8:12, 0:rows], piece[:, 8:12, :]).then_inc(r_in[h % 2], 16)
                load_head(0, 0, 0, P, True)
                load_head(1, 0, 1, P, True)
                O.load_post(sp, post_d)
                O.load_x(sp, 0, P, True)
                load_head(2, 0, 2, P)
                load_head(3, 0, 3, P)
                with sp.Fori(1, 8) as c:
                    for h in range(H):
                        load_head(4 * c + h, c, h, P)
                    O.store_y(sp, c - 1, P)
                    O.load_x(sp, c, P, False)
                load_head(32, 8, 0, LAST)
                load_head(33, 8, 1, LAST)

                def load_state(m):
                    r = m % CRING
                    if m >= CRING:
                        sp.wait_ge(s_out[r], 16 * (m // CRING))
                    sp.dma_start(cs[r][:], s0_d[m % NSEQ, m // NSEQ]).then_inc(s_in[r], 16)

                def store_state(m):
                    r = m % CRING
                    sp.wait_ge(s_ready, m + 1)
                    sp.dma_start(out_ss[m % NSEQ, m // NSEQ], cs[r][:]).then_inc(s_out[r], 16)
                for m in range(CRING):
                    load_state(m)
                O.store_y(sp, 7, P)
                O.load_x(sp, 8, LAST, False)
                for h in range(H):
                    for b in range(NSEQ):
                        m = h * NSEQ + b
                        store_state(m)
                        if m + CRING < H * NSEQ:
                            load_state(m + CRING)
                    sp.wait_ge(state_ready, 32 + h + 1)
                    sp.dma_start(out_sp[h], cst[:, h, :, :]).then_inc(p_stored, 16)
                    if h < 2:
                        load_head(34 + h, 8, 2 + h, LAST)
                O.store_y(sp, 8, LAST)
                sp.wait_ge(O.y_stored, 16 * NC + 16)
                sp.wait_ge(p_stored, 16 * H)
                for r in range(CRING):
                    sp.wait_ge(s_out[r], 16 * len(range(r, H * NSEQ, CRING)))

            @block.tensor
            def _(pe):
                def part_a(n, c, h, rows):
                    s = h % 2
                    pe.wait_ge(hin_in[s], 16 * (2 * c + h // 2) + 16)
                    t = hin[s]
                    for d in range(2):
                        pe.transpose(ps[0:rows, 0, P + d * P:P + (d + 1) * P], t[:, 2 + d, 0:rows], S.ident[:])
                    for d in range(4):
                        pe.transpose(ps[0:rows, 2, d * P:(d + 1) * P], t[:, 4 + d, 0:rows], S.ident[:])
                    for d in range(2):
                        ins = pe.matmul(ps[0:rows, 0, 0:rows], t[:, 2 + d, 0:rows], t[:, d, 0:rows], start=(d == 0), stop=(d == 1))
                    ins.then_inc(turned, 1)

                def part_b(n, h):
                    s = h % 2
                    pe.wait_ge(gn_ready, n)
                    pe.wait_ge(state_ready, n)
                    for d in range(2):
                        pe.matmul(ps[:, 3, :], hin[s][:, d, :], cst[:, h, d, :], start=(d == 0), stop=False)
                    pe.wait_ge(v_ready, n + 1)
                    pe.wait_ge(sc_ready, n + 1)
                    pe.matmul(ps[:, 3, :], sc[s][:], vv[s][:], start=False, stop=True)
                    for d in range(2):
                        ins = pe.matmul(ps[:, 4 + d, :], kk[s][:, d * P:(d + 1) * P], vv[s][:], start=True, stop=True)
                    ins.then_inc(b_done, 1)

                def part_c(n, rows):
                    pe.wait_ge(gn_ready, n + 1)
                    pe.wait_ge(mp_ready, n)
                    for d in range(4):
                        ins = pe.transpose(ps[:, 1, d * rows:(d + 1) * rows], gn[0:rows, d * P:(d + 1) * P], S.ident[0:rows, 0:rows])
                    ins.then_inc(c_done, 1)

                def out(c, h, new_w=False):
                    if h == 0:
                        pe.wait_ge(O.out_read, c)
                    pe.wait_ge(mix_ready, 4 * c + h + 1)
                    for e in range(4 * h, 4 * h + 4):
                        O.products(pe, ps, e, e == 0, e == 15, new_w)

                def chunk(c, first, last):
                    for h in range(H):
                        n = 4 * c + h
                        if not (last and h == 3):
                            part_a(n + 1, c + (h == 3), (h + 1) % H, P)
                        if not (first and h == 0):
                            out(c - (h == 0), (h - 1) % H, first)
                        part_c(n, P)
                        if not (last and h == 3):
                            part_b(n + 1, (h + 1) % H)
                pe.wait_ge(init_done, 1)
                part_a(0, 0, 0, P)
                part_b(0, 0)
                chunk(0, True, False)
                pe.wait_ge(O.w_ready, 16)
                with pe.Fori(1, 7) as c:
                    chunk(c, False, False)
                chunk(7, False, True)
                out(7, 3)
                pe.wait_ge(O.out_read, 8)
                part_a(32, 8, 0, LAST)
                for h in range(H):
                    n, s = 32 + h, h % 2
                    pe.wait_ge(gn_ready, n)
                    pe.wait_ge(state_ready, n)
                    pe.wait_ge(qm_ready, h + 1)
                    pe.wait_ge(v_ready, n + 1)
                    for g in range(NG):
                        m = h * NSEQ + g - 1
                        r = m % CRING
                        if g:
                            pe.wait_ge(s_in[r], 16 * (m // CRING) + 16)
                        for d in range(2):
                            st = cst[:, h, d, :] if g == 0 else cs[r][:, d, :]
                            pe.matmul(ps[0:LAST, 3, :], qm[:, d, g * LAST:(g + 1) * LAST], st,
                                      start=(g == 0 and d == 0), stop=False)
                        u = h * NG + g
                        if u >= 2:
                            pe.wait_ge(s_added, u - 1)
                        pe.wait_ge(kw8_ready, u + 1)
                        for d in range(2):
                            ins = pe.matmul(ps[:, 4 + 2 * (u % 2) + d, :], kw8[:, u % 2, d * P:(d + 1) * P],
                                            vv[s][0:LAST, :], start=True, stop=True)
                        ins.then_inc(upd_done, 1)
                    pe.wait_ge(sc_ready, n + 1)
                    pe.matmul(ps[0:LAST, 3, :], sc8[:], vv[s][0:LAST, :], start=False, stop=True).then_inc(b_done, 1)
                    if h < 3:
                        part_a(n + 1, 8, h + 1, LAST)
                    part_c(n, LAST)
                pe.wait_ge(s_added, H * NG)
                for h in range(H):
                    out(8, h)

            @block.scalar
            def _(act):
                act.preload_act_table_set('natural_log_exp_and_others')

                def part_a(n, s, rows, first=False):
                    act.wait_ge(turned, n + 1)
                    if not first:
                        act.wait_ge(b_done, n - 1)
                    act.activation(vv[s][0:rows, :], ps[0:rows, 2, :], ACT.Copy).then_inc(v_ready, 1)

                def norm(n, rows):
                    act.wait_ge(b_done, n + 1)
                    act.activation(gn[0:rows, :], ps[0:rows, 3, :], ACT.Square, accum_out=sm[0:rows, 0:1]).then_inc(sq_chain, 1)
                    act.wait_ge(sq_chain, 3 * n + 1)
                    act.activation(sm[0:rows, 1:2], sm[0:rows, 0:1], ACT.Ln, scale=1.0 / GV, bias=S.eps[0:rows, :]).then_inc(sq_chain, 1)
                    act.wait_ge(sq_chain, 3 * n + 2)
                    act.activation(sm[0:rows, 2:3], sm[0:rows, 1:2], ACT.Exp, scale=-0.5).then_inc(sq_chain, 1)
                    act.wait_ge(sq_chain, 3 * n + 3)
                    act.activation(gn[0:rows, :], ps[0:rows, 3, :], ACT.Copy, scale=sm[0:rows, 2:3]).then_inc(gn_ready, 1)

                def part_m(n, c, h, rows):
                    act.wait_ge(mp_ready, n + 1)
                    act.wait_ge(O.out_done, c)
                    act.activation(O.m_hi[:, 4 * h:4 * h + 4, 0:rows], mp[:, 0:4 * rows].rearrange("p (d t) -> p d t", d=4), ACT.Copy
                                   ).then_inc(mhi_ready, 1)

                def chunk(c, first, last):
                    for h in range(H):
                        n = 4 * c + h
                        norm(n, P)
                        if not (last and h == 3):
                            part_a(n + 1, (h + 1) % 2, P, first and h == 0)
                        if first:
                            O.split_w_hi(act, h)
                        if h == 0 and not first:
                            O.post_act(act, ps, c - 1, P)
                        part_m(n, c, h, P)
                part_a(0, 0, P, True)
                chunk(0, True, False)
                with act.Fori(1, 7) as c:
                    chunk(c, False, False)
                chunk(7, False, True)
                O.post_act(act, ps, 7, P)
                for h in range(H):
                    n = 32 + h
                    if h == 0:
                        part_a(n, 0, LAST)
                    for g in range(1, NG):
                        m = h * NSEQ + g - 1
                        act.wait_ge(s_added, h * NG + g + 1)
                        for d in range(2):
                            ins = act.activation(cs[m % CRING][:, d, :], cs[m % CRING][:, d, :], ACT.Copy,
                                                 scale=S.gf[:, 2 * h + d, 8 + g:9 + g])
                        ins.then_inc(s_ready, 1)
                    norm(n, LAST)
                    if h < 3:
                        part_a(n + 1, (h + 1) % 2, LAST)
                    part_m(n, 8, h, LAST)
                O.post_act(act, ps, 8, LAST)

            @block.vector
            def _(dve):
                dve.memset(sc[0][:], 0.0)
                dve.memset(sc[1][:], 0.0)
                dve.memset(sc8[:], 0.0)
                dve.memset(cst[:], 0.0).then_inc(init_done, 1)

                def part_a(n, s, rows, first=False):
                    dve.wait_ge(turned, n + 1)
                    if not first:
                        dve.wait_ge(b_done, n - 1)
                    dve.tensor_copy(kk[s][0:rows, :], ps[0:rows, 0, P:P + 256])
                    dst, mask = (sc[s], S.mask_one) if rows == P else (sc8, S.mask_one8)
                    dve.copy_predicated(dst[:], mask[:].bitcast(mybir.dt.uint32), ps[0:rows, 0, 0:rows]).then_inc(sc_ready, 1)

                def add_state(dst, bank):
                    for d in range(2):
                        ins = dve.tensor_tensor(dst[:, d, :], ps[:, bank + d, :], dst[:, d, :], ALU.add)
                    return ins

                def part_m(n, c, h, s, rows):
                    dve.wait_ge(c_done, n + 1)
                    dve.wait_ge(r_in[s], 16 * (2 * c + h // 2) + 16)
                    dve.wait_ge(mix_ready, n)
                    dve.tensor_tensor(mp[:, 0:4 * rows].rearrange("p (d t) -> p d t", d=4),
                                      ps[:, 1, 0:4 * rows].rearrange("p (d t) -> p d t", d=4), hin[s][:, 8:12, 0:rows],
                                      ALU.mult).then_inc(mp_ready, 1)

                def chunk(c, first, last):
                    for h in range(H):
                        n = 4 * c + h
                        dve.wait_ge(b_done, n + 1)
                        add_state(cst[:, h, :, :], 4).then_inc(added, 1)
                        if not (last and h == 3):
                            part_a(n + 1, (h + 1) % 2, P, first and h == 0)
                        if first:
                            O.split_w_lo(dve, h)
                        if h == 0 and not first:
                            O.post_dve(dve, ps, c - 1, P)
                        part_m(n, c, h, h % 2, P)
                part_a(0, 0, P, True)
                chunk(0, True, False)
                with dve.Fori(1, 7) as c:
                    chunk(c, False, False)
                chunk(7, False, True)
                O.post_dve(dve, ps, 7, P)
                for h in range(H):
                    n, s = 32 + h, h % 2
                    if h == 0:
                        part_a(n, s, LAST)
                    for g in range(NG + 1):
                        u = h * NG + g
                        if g < NG:
                            if u >= 2:
                                dve.wait_ge(upd_done, u - 1)
                            mask = S.tail_mask[:] if g == 0 else S.seq_mask[:, g - 1:g]
                            dve.tensor_scalar(kw8[:, u % 2, :], ps[0:LAST, 0, P:P + 256], mask, None, ALU.mult).then_inc(kw8_ready, 1)
                        if g:
                            u -= 1
                            dve.wait_ge(upd_done, u + 1)
                            dst = cst[:, h, :, :] if g == 1 else cs[(h * NSEQ + g - 2) % CRING]
                            add_state(dst, 4 + 2 * (u % 2)).then_inc(s_added, 1)
                    if h < 3:
                        part_a(n + 1, 1 - s, LAST)
                    part_m(n, 8, h, s, LAST)
                O.post_dve(dve, ps, 8, LAST)

            @block.gpsimd
            def _(pool):
                link = linker(pool, pool_chain)
                link(pool.memset(qm[:], 0.0))

                def take_factors(c):
                    pool.wait_ge(state_ready, 4 * c)
                    pool.tensor_copy(gfc[:], S.gf[:, :, bass.ds(c, 1)].rearrange("p t o -> p (t o)")).then_inc(gfc_ready, 1)
                    pool.wait_ge(gfc_ready, c + 1)

                def scale_state(h):
                    for d in range(2):
                        factor = gfc[:, 2 * h + d:2 * h + d + 1].to_broadcast([P, GV])
                        ins = pool.tensor_tensor(cst[:, h, d, :], cst[:, h, d, :], factor, ALU.mult)
                    ins.then_inc(state_ready, 1)

                def lo(n, h, rows):
                    pool.wait_ge(mhi_ready, n + 1)
                    tiles = slice(4 * h, 4 * h + 4)
                    pool.tensor_tensor(O.m_lo[:, tiles, 0:rows], mp[:, 0:4 * rows].rearrange("p (d t) -> p d t", d=4),
                                       O.m_hi[:, tiles, 0:rows].bitcast(F32), ALU.subtract).then_inc(mix_ready, 1)

                def chunk(c, first):
                    take_factors(c)
                    for h in range(H):
                        n = 4 * c + h
                        pool.wait_ge(added, n + 1)
                        scale_state(h)
                        if h == 0 and not first:
                            O.post_pool(pool, c - 1, P)
                        lo(n, h, P)
                chunk(0, True)
                with pool.Fori(1, 8) as c:
                    chunk(c, False)
                O.post_pool(pool, 7, P)
                take_factors(8)
                for h in range(H):
                    n, s = 32 + h, h % 2
                    pool.wait_ge(hin_in[s], 16 * (16 + h // 2) + 16)
                    if h:
                        pool.wait_ge(upd_done, NG * h)
                    for d in range(2):
                        q = hin[s][:, d, :]
                        pool.tensor_copy(qm[:, d, 0:TAIL], q[:, 0:TAIL])
                        ins = pool.tensor_copy(qm[:, d, 64:480].rearrange("p (s r) -> p s r", r=LAST + SLEN)[:, :, 0:SLEN],
                                               q[:, TAIL:LAST].rearrange("p (s t) -> p s t", t=SLEN))
                    ins.then_inc(qm_ready, 1)
                    pool.wait_ge(s_added, NG * h + 1)
                    scale_state(h)
                    lo(n, h, LAST)
                O.post_pool(pool, 8, LAST)


CRING = 3


def build_program(nc, io, upto=99):
    with ExitStack() as ctx:
        S = Names()
        S.a = make_alloc(nc, ctx)
        sb = S.a.sb
        S.vecs = sb("vecs", [P, NVEC])
        S.derived = sb("derived", [P, 2, 8])
        S.eps = sb("eps", [P, 1])
        S.tiny = sb("tiny", [P, 1])
        S.ident = sb("ident", [P, P])
        S.sel = sb("sel", [H, H, P])
        S.reset = sb("reset", [P, T])
        S.mask_add = sb("mask_add", [P, P])
        S.mask_one = sb("mask_one", [P, P])
        S.mask_add8 = sb("mask_add8", [LAST, LAST])
        S.mask_one8 = sb("mask_one8", [LAST, LAST])
        S.seq_mask = sb("seq_mask", [LAST, NSEQ])
        S.tail_mask = sb("tail_mask", [LAST, 1])
        stage_constants(nc, S, io["vecs"])
        stage_vectors(nc, S)
        scr_a = nc.dram_tensor("scr_a", [NC, H, P, AF, P], F32, kind="Internal").ap()
        scr_l = nc.dram_tensor("scr_l", [NC, P, 8, P], F32, kind="Internal").ap()
        with ExitStack() as actx:
            la = make_alloc(nc, actx)
            S.wc = la.sb("wc", [P, H, 17])
            S.tok = la.sb("tok", [P, NC, 3, H])
            S.rrow = la.sb("rrow", [H, T])
            raw_rows = ExitStack()
            w_early = OutWeights(S, make_alloc(nc, raw_rows), "wout_a_early", io["w_oa"], 8, 8)
            with ExitStack() as xctx:
                xa = make_alloc(nc, xctx)
                S.XT_hi = xa.sb("a_XT_hi", [P, KT, TP], F32R)
                S.XT_lo = xa.sb("a_XT_lo", [P, KT, TP], F32R)
                stage_norm(nc, S, "na", io["x"], V_PRE_A)
                stage_project_a(nc, S, io["w_a"], io["lru_w"], io["conv0"], io["h0"], scr_a, scr_l, io["m0"],
                                io["conv_p"], io["conv_s"], io["h_p"], io["h_s"], io["m_out"], w_early)
            scr_y = nc.dram_tensor("scr_y", [T, D], F32, kind="Internal").ap()
            w_late = OutWeights(S, make_alloc(nc, raw_rows), "wout_a_late", io["w_oa"], 0, 8)
            raw_rows.close()
            stage_mix_a(nc, S, scr_a, scr_l, w_early, w_late, io["post"], io["x"], scr_y, io["c0"], io["c_p"], io["c_s"])
        clear_semaphores(nc, S.a)
        with ExitStack() as cctx:
            lc = make_alloc(nc, cctx)
            S.gf = lc.sb("gf", [P, 8, 17])
            scr_c = nc.dram_tensor("scr_c", [NC, H, P, CF, P], F32, kind="Internal").ap()
            raw_rows = ExitStack()
            w_out = OutWeights(S, make_alloc(nc, raw_rows), "wout_c", io["w_oc"], 0, 16)
            with ExitStack() as xctx:
                xa = make_alloc(nc, xctx)
                S.XT_hi = xa.sb("c_XT_hi", [P, KT, TP], F32R)
                S.XT_lo = xa.sb("c_XT_lo", [P, KT, TP], F32R)
                stage_norm(nc, S, "nc", scr_y, V_PRE_C)
                stage_project_c(nc, S, io["w_c"], io["a_up"], scr_c, w_out)
            raw_rows.close()
            stage_mix_c(nc, S, scr_c, w_out, io["post"], scr_y, io["y"], io["s0"], io["s_p"], io["s_s"])


def _features(v, n):
    return v.reshape(n, P).T


def _tiles(w, columns):
    import numpy as np
    wz = np.concatenate([w, np.zeros((w.shape[0], 1), w.dtype)], axis=1)
    t = wz[:, columns].reshape(KT, P, -1, P)
    return t.transpose(2, 1, 0, 3)


def lay_out(i):
    import numpy as np
    r = np.arange
    none = -np.ones(P, np.int64)
    gates = none.copy()
    gates[0:4], gates[32:36] = r(4096, 4100), r(4100, 4104)
    cols = [gates]
    for t in range(8):
        cols += [5128 + P * t + r(P), 6152 + P * t + r(P)]
    cols += [r(0, 4096), r(4104, 5128)]
    alow = none.copy()
    alow[0:16] = r(6144, 6160)
    ccols = [alow]
    for t in range(8):
        ccols += [P * t + r(P), 1024 + P * t + r(P)]
    ccols += [r(2048, 6144)]
    vecs = [_features(i["pre_norm_a"][0], 8), _features(i["pre_norm_c"][0], 8)]
    vecs += [_features(i["conv_w"][0, j], 8) for j in range(4)]
    vecs += [_features(i[k][0], n) for k, n in (("conv_b", 8), ("lru_b_a", 8), ("lru_b_x", 8), ("lru_lambda", 8),
                                                ("mlstm_norm", 8), ("gla_norm", 16), ("gla_alpha_b", 8))]
    gb = np.zeros((P, 1), np.float32)
    gb[0:4, 0], gb[32:36, 0] = i["mlstm_b_i"][0], i["mlstm_b_f"][0]
    vecs.append(gb)
    c = i["state_mlstm_C"][0].transpose(0, 1, 3, 2)
    caug = np.concatenate([c, i["state_mlstm_n"][0][..., None]], axis=-1)
    return {
        "x": np.concatenate([i["meta_tokens"], i["x_prompt"][0], i["x_sample"].reshape(-1, D)], axis=0),
        "vecs": np.concatenate(vecs, axis=1),
        "w_a": _tiles(i["w_in_a"][0], np.concatenate(cols)),
        "w_c": _tiles(i["w_in_c"][0], np.concatenate(ccols)),
        "lru_w": np.stack([i["lru_w_a"][0], i["lru_w_x"][0]], axis=2),
        "conv0": i["state_rglru_conv"][0].reshape(NSEQ, 3, 8, P).transpose(3, 2, 0, 1),
        "h0": i["state_rglru_h"][0].reshape(NSEQ, 8, P).transpose(2, 1, 0),
        "m0": i["state_mlstm_m"][0].T,
        "c0": caug.reshape(NSEQ, H, 2, P, MV).transpose(0, 1, 3, 2, 4),
        "s0": i["state_gla_S"][0].reshape(NSEQ, H, 2, P, GV).transpose(0, 1, 3, 2, 4),
        "w_oa": i["w_out_a"][0].reshape(16, P, D).transpose(1, 0, 2),
        "w_oc": i["w_out_c"][0].reshape(16, P, D).transpose(1, 0, 2),
        "post": np.stack([np.broadcast_to(i["post_norm_a"][0], (P, D)), np.broadcast_to(i["post_norm_c"][0], (P, D))], axis=1),
        "a_up": i["gla_alpha_up"][0].reshape(16, 8, P),
    }


OUTS = {
    "y": (T, D), "conv_p": (P, 8, 3), "conv_s": (P, 8, NSEQ, 3), "h_p": (P, 8), "h_s": (P, 8, NSEQ), "m_out": (H, 9),
    "c_p": (H, P, 2, MV), "c_s": (NSEQ, H, P, 2, MV), "s_p": (H, P, 2, GV), "s_s": (NSEQ, H, P, 2, GV),
}


def take_out(o):
    import numpy as np
    y = o["y"]

    def c_state(c):
        c = np.moveaxis(c, -2, -3)
        c = c.reshape(c.shape[:-3] + (DK, MV))
        return np.ascontiguousarray(np.swapaxes(c[..., 0:DK], -1, -2)), np.ascontiguousarray(c[..., DK])

    def s_state(c):
        c = np.moveaxis(c, -2, -3)
        return c.reshape(c.shape[:-3] + (DK, GV))
    pc, pn = c_state(o["c_p"])
    sc, sn = c_state(o["c_s"])
    con = np.ascontiguousarray
    return (
        con(y[16:NP_TOK][None]), con(y[NP_TOK:].reshape(NSEQ, SLEN, D)),
        pc[None, None], pn[None, None], con(o["m_out"][:, 0][None, None]),
        con(o["h_p"].T.reshape(1, 1, D)), con(o["conv_p"].transpose(2, 1, 0).reshape(1, 1, 3, D)), con(s_state(o["s_p"])[None, None]),
        sc[None], sn[None], con(o["m_out"][:, 1:].T[None]),
        con(o["h_s"].transpose(2, 1, 0).reshape(1, NSEQ, D)), con(o["conv_s"].transpose(2, 3, 1, 0).reshape(1, NSEQ, 3, D)),
        con(s_state(o["s_s"])[None]),
    )


def kernel(**inputs):
    import numpy as _np
    import concourse.bacc as _bacc
    from concourse.bass_utils import run_bass_kernel_spmd as _run

    nc = _bacc.Bacc("TRN2", target_bir_lowering=False, num_devices=1,
                    dynamic_dma_scratch_size=1024)
    arrays = {k: _np.ascontiguousarray(v) for k, v in lay_out({k: _np.asarray(v) for k, v in inputs.items()}).items()}
    io = {k: nc.dram_tensor("in_" + k, v.shape, F32, kind="ExternalInput").ap() for k, v in arrays.items()}
    for k, shape in OUTS.items():
        io[k] = nc.dram_tensor("out_" + k, shape, F32, kind="ExternalOutput").ap()
    build_program(nc, io)
    r = _run(nc, [{"in_" + k: v for k, v in arrays.items()}], core_ids=[0])
    return take_out({k: r.results[0]["out_" + k] for k in OUTS})
```

```python
from contextlib import ExitStack

import concourse.bass as bass
from concourse import mybir

P = 128
D = 1024
KT = D // P
NP_TOK = 1040
NSEQ, SLEN = 8, 4
T = NP_TOK + NSEQ * SLEN
NC = 9
LAST = T - 8 * P
TAIL = NP_TOK - 8 * P
NG = 1 + NSEQ
TC = 358
TP = 3 * TC
H = 4
DK = 256
MV = 257
GV = 512
EPS = 1e-6
NEG = -1e30

A_QKV0 = 17
C_V0 = 17
AF = 10
CF = 12

V_PRE_A, V_PRE_C = 0, 8
V_CONVW, V_CONVB = 16, 48
V_BA, V_BX, V_LAM = 56, 64, 72
V_MNORM, V_GNORM = 80, 88
V_ALPHAB = 104
V_GATEB = 112
NVEC = 113

F32 = mybir.dt.float32
F32R = mybir.dt.float32r
ALU = mybir.AluOpType
ACT = mybir.ActivationFunctionType


class Names:
    pass


def make_alloc(nc, ctx):
    a = Names()
    a.sb = lambda name, shape, dt=F32: ctx.enter_context(nc.sbuf_tensor(name, shape, dt))
    a.ps = lambda name, shape: ctx.enter_context(nc.psum_tensor(name, shape, F32))
    a.sems = []

    def sem(name):
        a.sems.append(nc.alloc_semaphore(name=name))
        return a.sems[-1]
    a.sem = sem
    return a


def clear_semaphores(nc, a):
    nc.clear_and_free_semaphores(a.sems)
    a.sems.clear()
    nc.all_engine_barrier()


def linker(eng, sem, base=0):
    k = [0]

    def link(ins):
        k[0] += 1
        ins.then_inc(sem, 1)
        eng.wait_ge(sem, base + k[0])
    link.count = lambda: k[0]
    return link


def stage_constants(nc, S, vecs_d):
    made = S.a.sem("const_made")
    loaded = S.a.sem("const_loaded")
    chain_a = S.a.sem("vec_act_chain")
    chain_d = S.a.sem("vec_dve_chain")
    lam_abs = S.a.sem("lam_exp_ready")
    with ExitStack() as ctx, nc.Block() as block:
        a = make_alloc(nc, ctx)
        e, w, z, z2, p, m = (a.sb(f"vec_{n}", [P, 8]) for n in ("e", "w", "z", "z2", "p", "m"))
        lam = S.vecs[:, V_LAM:V_LAM + 8]

        @block.sync
        def _(sp):
            sp.dma_start(S.vecs[:], vecs_d).then_inc(loaded, 16)
            sp.wait_ge(loaded, 16)

        @block.gpsimd
        def _(pool):
            link = linker(pool, made)
            link(pool.memset(S.ident[:], 0.0))
            link(pool.affine_select(out=S.ident[:], in_=S.ident[:], compare_op=ALU.not_equal, fill=1.0,
                                    base=0, pattern=[[-1, P]], channel_multiplier=1))
            link(pool.memset(S.sel[:], 0.0))
            link(pool.affine_select(out=S.sel[:], in_=S.sel[:], compare_op=ALU.not_equal, fill=1.0,
                                    base=0, pattern=[[-1, H], [0, P]], channel_multiplier=1))
            for m, seen, hidden in ((S.mask_add, 0.0, NEG), (S.mask_add8, 0.0, NEG), (S.mask_one, 1.0, 0.0), (S.mask_one8, 1.0, 0.0)):
                w = m.shape[1]
                link(pool.memset(m[:], seen))
                link(pool.affine_select(out=m[:], in_=m[:], compare_op=ALU.is_ge, fill=hidden,
                                        base=0, pattern=[[1, w]], channel_multiplier=-1))
                if w == LAST:
                    part = m[:, TAIL:LAST].rearrange("p (s t) -> p s t", t=SLEN)
                    link(pool.affine_select(out=part, in_=part, compare_op=ALU.is_ge, fill=hidden,
                                            base=-TAIL, pattern=[[-SLEN, NSEQ], [0, SLEN]], channel_multiplier=1))
            link(pool.memset(S.seq_mask[:], 1.0))
            link(pool.affine_select(out=S.seq_mask[:], in_=S.seq_mask[:], compare_op=ALU.is_ge, fill=0.0,
                                    base=-TAIL, pattern=[[-SLEN, NSEQ]], channel_multiplier=1))
            link(pool.affine_select(out=S.seq_mask[:], in_=S.seq_mask[:], compare_op=ALU.is_ge, fill=0.0,
                                    base=TAIL + SLEN - 1, pattern=[[SLEN, NSEQ]], channel_multiplier=-1))
            link(pool.memset(S.tail_mask[:], 1.0))
            link(pool.affine_select(out=S.tail_mask[:], in_=S.tail_mask[:], compare_op=ALU.is_ge, fill=0.0,
                                    base=TAIL - 1, pattern=[[0, 1]], channel_multiplier=-1))

        @block.scalar
        def _(act):
            act.preload_act_table_set('natural_log_exp_and_others')
            act.wait_ge(loaded, 16)
            link = linker(act, chain_a)
            link(act.activation(w[:], lam, ACT.Abs))
            act.activation(e[:], w[:], ACT.Exp, scale=-1.0).then_inc(lam_abs, 1)

        @block.vector
        def _(dve):
            link = linker(dve, chain_d)
            dve.memset(S.eps[:], EPS)
            dve.memset(S.tiny[:], 1e-18)
            dve.wait_ge(loaded, 16)
            link(dve.tensor_scalar(m[:], lam, -1.0, 0.0, ALU.mult, ALU.max))
            dve.wait_ge(lam_abs, 1)
            link(dve.tensor_scalar(z[:], e[:], 2.0, None, ALU.add))
            link(dve.reciprocal(p[:], z[:]))
            link(dve.tensor_tensor(z[:], e[:], p[:], ALU.mult))
            link(dve.tensor_tensor(z2[:], z[:], z[:], ALU.mult))
            link(dve.tensor_scalar(p[:], z2[:], 1.0 / 15, 1.0 / 13, ALU.mult, ALU.add))
            for n in (11, 9, 7, 5, 3, 1):
                link(dve.tensor_tensor(p[:], p[:], z2[:], ALU.mult))
                link(dve.tensor_scalar(p[:], p[:], 1.0 / n, None, ALU.add))
            link(dve.tensor_tensor(p[:], p[:], z[:], ALU.mult))
            link(dve.scalar_tensor_tensor(out=z[:], in0=p[:], scalar=2.0, in1=m[:], op0=ALU.mult, op1=ALU.add))
            dve.tensor_scalar(S.derived[:, 0, :], z[:], 8.0, None, ALU.mult)
            dve.tensor_scalar(S.derived[:, 1, :], z[:], -8.0, None, ALU.mult)


def stage_norm(nc, S, G, name, x_d, gcol):
    with ExitStack() as ctx:
        a = make_alloc(nc, ctx)
        NX = 4
        xin = [a.sb(f"{name}_xin{s}", [P, D]) for s in range(NX)]
        junk = a.sb(f"{name}_junk", [P, D])
        xn = [a.sb(f"{name}_xn{s}", [P, D]) for s in range(2)]
        xg = [a.sb(f"{name}_gained{s}", [P, KT, P]) for s in range(2)]
        stat = [a.sb(f"{name}_stat{s}", [P, 4]) for s in range(NX)]
        loaded = [S.a.sem(f"{name}_x_loaded{s}") for s in range(NX)]
        rstd_ready = S.a.sem(f"{name}_rstd_ready")
        act_chain = S.a.sem(f"{name}_act_chain")
        xn_ready = S.a.sem(f"{name}_xn_ready")
        turned = S.a.sem(f"{name}_turned")
        gained = S.a.sem(f"{name}_gained")
        reset_chain = S.a.sem(f"{name}_reset_chain")
        hi_ready = S.a.sem(f"{name}_hi_ready")
        lo_ready = S.a.sem(f"{name}_lo_ready")
        gain = S.vecs[:, gcol:gcol + KT]

        def later(c, least):
            return not (isinstance(c, int) and c < least)

        with nc.Block() as block:
            @block.sync
            def _(sp):
                def load(i, u):
                    c = NX * i + u
                    rows = LAST if isinstance(c, int) and c == 8 else P
                    if later(i, 1):
                        sp.wait_ge(xn_ready, c - NX + 1)
                    sp.dma_start(xin[u][0:rows, :], x_d[bass.ds(c * P, rows), :]).then_inc(loaded[u], 16)
                for u in range(NX):
                    load(0, u)
                for s in range(2):
                    G.load(sp, s, s)
                for u in range(NX):
                    load(1, u)
                load(2, 0)

            @block.scalar
            def _(act):
                act.preload_act_table_set('natural_log_exp_and_others')

                def root(i, u, rows):
                    c = NX * i + u
                    st, x = stat[u], xin[u][0:rows, :]
                    act.wait_ge(loaded[u], 16 * i + 16)
                    if later(c, NX):
                        act.wait_ge(xn_ready, c - NX + 1)
                    act.activation(junk[0:rows, :], x, ACT.Square, accum_out=st[0:rows, 0:1]).then_inc(act_chain, 1)
                    act.wait_ge(act_chain, 2 * c + 1)
                    act.activation(st[0:rows, 1:2], st[0:rows, 0:1], ACT.Ln, scale=1.0 / D,
                                   bias=S.eps[0:rows, :]).then_inc(act_chain, 1)
                    act.wait_ge(act_chain, 2 * c + 2)
                    act.activation(st[0:rows, 2:3], st[0:rows, 1:2], ACT.Exp, scale=-0.5).then_inc(rstd_ready, 1)

                def high(c, v, rows):
                    act.wait_ge(gained, c + 1)
                    act.activation(S.XT_hi[:, :, bass.ds(c * P, rows)], xg[v][:, :, 0:rows], ACT.Copy).then_inc(hi_ready, 1)
                for c in range(NC + 2):
                    if c < NC:
                        root(c // NX, c % NX, LAST if c == 8 else P)
                    if c >= 2:
                        high(c - 2, c % 2, LAST if c == NC + 1 else P)
                    if c in (2, 5):
                        G.split_hi(act, c // 3, c // 3, 0)

            @block.vector
            def _(dve):
                for t in (S.XT_hi, S.XT_lo):
                    dve.memset(t[:, :, T:TP].bitcast(F32), 0.0).then_inc(G.cleared, 1)

                def scaled(c, v, rows):
                    dve.wait_ge(turned, c + 1)
                    if later(c, 2):
                        dve.wait_ge(lo_ready, c - 1)
                    for half in range(2):
                        ks = slice(4 * half, 4 * half + 4)
                        ins = dve.tensor_tensor(xg[v][:, ks, 0:rows],
                                                G.ps[:, 4 + 2 * v + half, :].rearrange("p (k t) -> p k t", t=P)[:, :, 0:rows],
                                                gain[:, ks].unsqueeze(2).to_broadcast([P, 4, rows]), ALU.mult)
                    ins.then_inc(gained, 1)

                def low(c, v, rows):
                    dve.wait_ge(hi_ready, c + 1)
                    at = bass.ds(c * P, rows)
                    dve.tensor_tensor(S.XT_lo[:, :, at], xg[v][:, :, 0:rows], S.XT_hi[:, :, at].bitcast(F32), ALU.subtract
                                      ).then_inc(lo_ready, 1)
                scaled(0, 0, P)
                for c in range(1, NC):
                    low(c - 1, (c - 1) % 2, P)
                    scaled(c, c % 2, LAST if c == 8 else P)
                    if c in (2, 5):
                        G.split_lo(dve, c // 3, c // 3)
                low(8, 0, LAST)

            @block.gpsimd
            def _(pool):
                link = linker(pool, reset_chain)
                link(pool.memset(S.reset[:], 1.0))
                link(pool.memset(S.reset[:, 0:8 * P].rearrange("p (c t) -> p c t", t=P)[:, :, 0:1], 0.0))
                link(pool.memset(S.reset[:, 8 * P:8 * P + 1], 0.0))
                link(pool.memset(S.reset[:, NP_TOK:T].rearrange("p (s t) -> p s t", t=SLEN)[:, :, 0:1], 0.0))
                for c in range(NC):
                    rows = LAST if c == 8 else P
                    pool.wait_ge(rstd_ready, c + 1)
                    if c >= 2:
                        pool.wait_ge(turned, c - 1)
                    pool.tensor_tensor(xn[c % 2][0:rows, :], xin[c % NX][0:rows, :],
                                       stat[c % NX][0:rows, 2:3].to_broadcast([rows, D]), ALU.mult).then_inc(xn_ready, 1)

            @block.tensor
            def _(pe):
                def turn(c, v, rows):
                    pe.wait_ge(xn_ready, c + 1)
                    if later(c, 2):
                        pe.wait_ge(gained, c - 1)
                    for k in range(KT):
                        ins = pe.transpose(G.ps[:, 4 + 2 * v + k // 4, bass.ds(k % 4 * P, rows)],
                                           xn[v][0:rows, k * P:(k + 1) * P], S.ident[0:rows, 0:rows])
                    ins.then_inc(turned, 1)
                for c in range(NC):
                    turn(c, c % 2, LAST if c == 8 else P)
                    if c in (4, 7):
                        pe.wait_ge(lo_ready, c - 1)
                        G.products_of_tile_0(pe, (c - 4) // 3)
                pe.wait_ge(lo_ready, NC)
                G.products_of_tile_0(pe, 2)


class Projection:

    def __init__(self, S, a, name, w_d):
        self.S, self.w_d = S, w_d
        self.raw = [a.sb(f"{name}_w_raw{s}", [P, KT, P]) for s in range(2)]
        self.hi = [a.sb(f"{name}_w_hi{s}", [P, KT, P], F32R) for s in range(2)]
        self.lo = [a.sb(f"{name}_w_lo{s}", [P, KT, P], F32R) for s in range(2)]
        self.ps = a.ps(f"{name}_ps", [P, 8, 512])
        self.w_loaded = [S.a.sem(f"{name}_w_loaded{s}") for s in range(2)]
        self.w_hi_ready = S.a.sem(f"{name}_w_hi_ready")
        self.w_lo_ready = S.a.sem(f"{name}_w_lo_ready")
        self.gemm_done = S.a.sem(f"{name}_gemm_done")
        self.cleared = S.a.sem(f"{name}_pad_cleared")
        self.psum_free = [S.a.sem(f"{name}_psum_free{s}") for s in range(2)]

    def bank(self, s):
        return self.ps[:, 3 * s:3 * s + 3, 0:TC]

    def load(self, sp, n, s):
        if not (isinstance(n, int) and n < 2):
            sp.wait_ge(self.w_lo_ready, n - 1)
        sp.dma_start(self.raw[s][:], self.w_d[bass.ds(n, 1), :, :, :].rearrange("o p k f -> p (o k) f")
                     ).then_inc(self.w_loaded[s], 16)

    def split_hi(self, act, n, s, half):
        act.wait_ge(self.w_loaded[s], 16 * half + 16)
        if not (isinstance(n, int) and n < 2):
            act.wait_ge(self.gemm_done, n - 1)
        act.activation(self.hi[s][:], self.raw[s][:], ACT.Copy).then_inc(self.w_hi_ready, 1)

    def split_lo(self, dve, n, s):
        dve.wait_ge(self.w_hi_ready, n + 1)
        dve.tensor_tensor(self.lo[s][:], self.raw[s][:], self.hi[s][:].bitcast(F32), ALU.subtract
                          ).then_inc(self.w_lo_ready, 1)

    def passes(self, s):
        return (self.hi[s], self.S.XT_hi), (self.hi[s], self.S.XT_lo), (self.lo[s], self.S.XT_hi)

    def products(self, pe, n, s, half, hooks):
        pe.wait_ge(self.w_lo_ready, n + 1)
        if not (isinstance(n, int) and n < 2):
            pe.wait_ge(self.psum_free[s], half)
        for k in range(KT):
            if k in hooks:
                hooks[k]()
            for j, (w, x) in enumerate(self.passes(s)):
                for t in range(3):
                    ins = pe.matmul(self.ps[:, 3 * s + t, 0:TC], w[:, k, :], x[:, k, t * TC:(t + 1) * TC],
                                    start=(k == 0 and j == 0), stop=(k == KT - 1 and j == 2))
        ins.then_inc(self.gemm_done, 1)

    def products_of_tile_0(self, pe, t):
        if t == 0:
            pe.wait_ge(self.w_lo_ready, 1)
        if t == 2:
            pe.wait_ge(self.cleared, 2)
        for k in range(KT):
            for j, (w, x) in enumerate(self.passes(0)):
                ins = pe.matmul(self.ps[:, t, 0:TC], w[:, k, :], x[:, k, t * TC:(t + 1) * TC],
                                start=(k == 0 and j == 0), stop=(k == KT - 1 and j == 2))
        if t == 2:
            ins.then_inc(self.gemm_done, 1)


def stage_project_a(nc, S, G, lru_w_d, conv0_d, h0_d, scr_d, lru_d, m0_d, out_conv_p, out_conv_s, out_h_p, out_h_s, out_m, w_out):
    with ExitStack() as ctx:
        a = make_alloc(nc, ctx)
        stage = [a.sb(f"pa_stage{s}", [P, 3, TC]) for s in range(2)]
        flat = [s[:].rearrange("p a b -> p (a b)") for s in stage]
        xe_p = a.sb("pa_xe_p", [P, 3 + NP_TOK])
        xe_s = a.sb("pa_xe_s", [P, NSEQ, 3 + SLEN])
        xc = a.sb("pa_xc", [P, TP])
        gr_e = a.sb("pa_gate_r", [P, TP])
        gi_e = a.sb("pa_gate_i", [P, TP])
        av = a.sb("pa_decay", [P, T])
        tv = a.sb("pa_tanh", [P, T])
        lv = a.sb("pa_log", [P, T])
        hv = a.sb("pa_h", [P, T])
        silu = a.sb("pa_silu", [P, 3, TC])
        sig = a.sb("pa_sigmoid", [P, 3, TC])
        silu_f = silu[:].rearrange("p a b -> p (a b)")
        lout = a.sb("pa_lru_out", [P, T])
        lru_w = a.sb("pa_lru_w", [P, 2, P])
        conv0 = a.sb("pa_conv0", [P, 8, NSEQ, 3])
        h0 = a.sb("pa_h0", [P, 8, NSEQ])
        cp_out = a.sb("pa_conv_p_out", [P, 8, 3])
        cs_out = a.sb("pa_conv_s_out", [P, 8, NSEQ, 3])
        hp_out = a.sb("pa_h_p_out", [P, 8])
        hs_out = a.sb("pa_h_s_out", [P, 8, NSEQ])
        tmp8 = a.sb("pa_tmp8", [P, NSEQ])
        gates = a.sb("pa_gates", [P, TP])
        par = a.sb("pa_scalars", [P, 4])
        rows = a.sb("pa_rows", [P, T])
        m0 = a.sb("pa_m0", [4, NSEQ])
        m_prev = a.sb("pa_m_prev", [4, 17])
        m_out = a.sb("pa_m_out", [4, 9])
        e_last = a.sb("pa_e_last", [4, 17])

        sem = S.a.sem
        small_in = sem("pa_small_in")
        lru_w_in = sem("pa_lru_w_in")
        xr_ready = sem("pa_xr_ready")
        conv_ready = sem("pa_conv_ready")
        lru_gemm = sem("pa_lru_gemm_done")
        gates_ready = sem("pa_gates_ready")
        tanh_ready = sem("pa_tanh_ready")
        decay_ready = sem("pa_decay_ready")
        logs_ready = sem("pa_logs_ready")
        root_log = sem("pa_root_log_ready")
        root_ready = sem("pa_root_ready")
        silu_ready = sem("pa_silu_ready")
        cleared = sem("pa_cleared")
        gates_used = sem("pa_gates_used")
        conv_chain = sem("pa_conv_chain")
        scan_chain = sem("pa_scan_chain")
        scan_done = sem("pa_scan_done")
        lru_out_ready = sem("pa_lru_out_ready")
        lru_spilled = sem("pa_lru_spilled")
        ixc_ready = sem("pa_ixc_ready")
        stage_ready = sem("pa_stage_ready")
        z_ready = sem("pa_z_ready")
        sigmoid_ready = sem("pa_sigmoid_ready")
        spilled = [sem(f"pa_spilled{s}") for s in range(2)]
        finished = sem("pa_outputs_stored")
        row_act = sem("pa_rows_act")
        row_dve = sem("pa_rows_dve")
        rows_ready = sem("pa_rows_ready")
        rows_turned = sem("pa_rows_turned")

        PROMPT = slice(0, NP_TOK)

        def seq_cols(buf, off):
            return buf[:, NP_TOK:NP_TOK + NSEQ * SLEN].rearrange("p (s t) -> p s t", t=SLEN)[:, :, off]

        def seqs4(row, off):
            return seqs(row)[:, :, off]

        def seqs(buf):
            return buf[:, NP_TOK:NP_TOK + NSEQ * SLEN].rearrange("p (s t) -> p s t", t=SLEN)

        groups = ("q", "k", "v", "og", "z")

        xf, ab, lf, bb, mm = (x[0:4, 0:T] for x in (gr_e, gi_e, av, tv, lv))
        li = gates[0:4, 0:T]

        def chunked(row):
            return row[:, 0:8 * P].rearrange("p (c t) -> p c t", t=P)

        def gate_rows_act(act):
            act.wait_ge(lru_out_ready, 8)
            act.activation(xf, gates[32:36, 0:T], ACT.Copy).then_inc(row_act, 1)
            act.activation(ab, gates[32:36, 0:T], ACT.Abs).then_inc(row_act, 1)
            act.wait_ge(row_act, 2)
            act.activation(ab, ab, ACT.Exp, scale=-1.0).then_inc(row_act, 1)
            act.wait_ge(row_act, 3)
            act.activation(ab, ab, ACT.Ln, bias=1.0).then_inc(row_act, 1)

        def gate_rows_act_out(act):
            act.wait_ge(rows_turned, 1)
            act.activation(S.wc[:], G.ps[:, 6, 0:4 * 17].rearrange("p (h g) -> p h g", g=17), ACT.Exp)
            for bank, off, c0, n in ((6, 80, 0, 5), (7, 0, 5, 4)):
                turned = G.ps[:, bank, off:off + 68 * n].rearrange("p (c r) -> p c r", r=68)
                act.activation(S.tok[:, c0:c0 + n, 0, :], turned[:, :, 0:4], ACT.Copy)
                act.activation(S.tok[:, c0:c0 + n, 1, :], turned[:, :, 32:36], ACT.Exp)
                act.activation(S.tok[:, c0:c0 + n, 2, :], turned[:, :, 64:68], ACT.Exp)

        def gate_rows_dve(dve, part):
            link = linker(dve, row_dve, 0 if part == 0 else ROW_STEPS)
            (gate_rows_dve_0 if part == 0 else gate_rows_dve_1)(dve, link)

        def gate_rows_dve_0(dve, link):
            link(dve.memset(rows[:], 0.0))
            link(dve.memset(m_prev[:], 0.0))
            dve.wait_ge(row_act, 4)
            link(dve.scalar_tensor_tensor(out=lf, in0=xf, scalar=0.0, in1=ab, op0=ALU.min, op1=ALU.subtract))
            link(dve.tensor_tensor_scan(bb, S.reset[0:4, :], lf, 0.0, ALU.mult, ALU.add))
            link(dve.tensor_tensor_scan(mm[:, PROMPT], lf[:, PROMPT], li[:, PROMPT], 0.0, ALU.add, ALU.max))
            link(dve.tensor_copy(m_prev[:, 9:17], m0[:]))
            for t in range(SLEN):
                before = m_prev[:, 9:17] if t == 0 else seqs4(mm, t - 1)
                link(dve.tensor_tensor(seqs4(mm, t), before, seqs4(lf, t), ALU.add))
                link(dve.tensor_tensor(seqs4(mm, t), seqs4(mm, t), seqs4(li, t), ALU.max))
            assert link.count() == ROW_STEPS

        def gate_rows_dve_1(dve, link):
            link(dve.tensor_copy(m_prev[:, 1:9], chunked(mm)[:, :, P - 1]))
            link(dve.tensor_copy(m_out[:, 0:1], mm[:, NP_TOK - 1:NP_TOK]))
            link(dve.tensor_copy(m_out[:, 1:9], seqs4(mm, SLEN - 1)))
            link(dve.tensor_tensor(S.rrow[:], bb, mm, ALU.subtract))
            dve.tensor_tensor(rows[0:4, :], li, bb, ALU.subtract)
            dve.tensor_tensor(chunked(rows[32:36, :]), chunked(S.rrow[:]),
                              m_prev[:, 0:8].unsqueeze(2).to_broadcast([4, 8, P]), ALU.add)
            dve.tensor_scalar(rows[32:36, 8 * P:NP_TOK], S.rrow[:, 8 * P:NP_TOK], m_prev[:, 8:9], None, ALU.add)
            dve.tensor_tensor(seqs(rows[32:36, :]), seqs(S.rrow[:]),
                              m_prev[:, 9:17].unsqueeze(2).to_broadcast([4, NSEQ, SLEN]), ALU.add)
            dve.tensor_scalar(rows[64:68, :], mm, -1.0, None, ALU.mult)
            dve.tensor_tensor(e_last[:, 0:8], chunked(S.rrow[:])[:, :, P - 1], m_prev[:, 0:8], ALU.add)
            dve.tensor_tensor(e_last[:, 8:9], S.rrow[:, NP_TOK - 1:NP_TOK], m_prev[:, 8:9], ALU.add)
            dve.tensor_tensor(e_last[:, 9:17], seqs4(S.rrow[:], SLEN - 1), m_prev[:, 9:17], ALU.add).then_inc(rows_ready, 1)

        def gate_rows_pe(pe):
            pe.wait_ge(rows_ready, 1)
            pe.wait_ge(gates_ready, 24)
            for h in range(H):
                pe.matmul(G.ps[:, 6, 17 * h:17 * h + 17], S.sel[:, h, :], e_last[:], start=True, stop=True)
            for c in range(NC):
                w = P if c < 8 else LAST
                bank, off = (6, 80 + 68 * c) if c < 5 else (7, 68 * (c - 5))
                ins = pe.transpose(G.ps[0:w, bank, off:off + 68], rows[0:68, c * P:c * P + w], S.ident[0:68, 0:68])
            ins.then_inc(rows_turned, 1)

        with nc.Block() as block:
            @block.sync
            def _(sp):
                sp.dma_start(m0[:], m0_d).then_inc(small_in, 16)
                sp.dma_start(conv0[:], conv0_d).then_inc(small_in, 16)
                sp.dma_start(h0[:], h0_d).then_inc(small_in, 16)
                G.load(sp, 2, 0)

                def spill_lru(i):
                    sp.wait_ge(lru_out_ready, i + 1)
                    dst = lru_d[0:8, :, bass.ds(i, 1), :].rearrange("c p o t -> p c (o t)")
                    sp.dma_start(dst, lout[:, 0:8 * P].rearrange("p (c t) -> p c t", t=P)).then_inc(lru_spilled, 16)
                    sp.dma_start(lru_d[8, :, bass.ds(i, 1), 0:LAST].rearrange("p o t -> p (o t)"),
                                 lout[:, 8 * P:T]).then_inc(lru_spilled, 16)

                def pair(i, first):
                    if not first:
                        sp.wait_ge(lru_gemm, 3 * i)
                    sp.dma_start(lru_w[:], lru_w_d[bass.ds(i, 1), :, :, :].rearrange("o i m j -> i (o m) j")
                                 ).then_inc(lru_w_in, 16)
                    G.load(sp, 2 * i + 3, 1)
                    G.load(sp, 2 * i + 4, 0)
                    if not first:
                        spill_lru(i - 1)
                pair(0, True)
                with sp.Fori(1, 8) as i:
                    pair(i, False)

                def spill(n, s, head, slot_in_head, m):
                    sp.wait_ge(z_ready if slot_in_head >= 8 else stage_ready, m + 1)
                    dst = scr_d[0:8, bass.ds(head, 1), :, slot_in_head, :].rearrange("c o p t -> p (o c) t")
                    sp.dma_start(dst, flat[s][:, 0:8 * P].rearrange("p (c t) -> p c t", t=P)).then_inc(spilled[s], 16)
                    sp.dma_start(scr_d[8, bass.ds(head, 1), :, slot_in_head, 0:LAST].rearrange("o p t -> (o p) t"),
                                 flat[s][:, 8 * P:T]).then_inc(spilled[s], 16)

                def group(g):
                    last = g == len(groups) - 1

                    def two(h, tail):
                        for d in range(2):
                            n = A_QKV0 + 8 * g + 2 * h + d
                            if not tail:
                                G.load(sp, n + 2, (1 + d) % 2)
                            spill(n, (1 + d) % 2, h, 2 * g + d, (0 if last else 8 * g) + 2 * h + d)
                    if last:
                        with sp.Fori(0, 3) as h:
                            two(h, False)
                        two(3, True)
                    else:
                        with sp.Fori(0, 4) as h:
                            two(h, False)
                for g in range(len(groups)):
                    if g:
                        w_out.load(sp, g - 1)
                    group(g)
                    if g == 0:
                        spill_lru(7)
                        sp.dma_start(out_conv_p, cp_out[:]).then_inc(finished, 16)
                        sp.dma_start(out_conv_s, cs_out[:]).then_inc(finished, 16)
                        sp.dma_start(out_h_p, hp_out[:]).then_inc(finished, 16)
                        sp.dma_start(out_h_s, hs_out[:]).then_inc(finished, 16)
                    if g == 3:
                        sp.wait_ge(rows_ready, 1)
                        sp.dma_start(out_m, m_out[:]).then_inc(finished, 16)
                sp.wait_ge(lru_spilled, 16 * 2 * 8)
                for s in range(2):
                    sp.wait_ge(spilled[s], 16 * 2 * 20)
                sp.wait_ge(finished, 80)

            @block.scalar
            def _(act):
                act.preload_act_table_set('natural_log_exp_and_others')
                act.wait_ge(G.gemm_done, 1)
                for t in range(3):
                    w = TC if t < 2 else T - 2 * TC
                    ins = act.activation(gates[:, t * TC:t * TC + w], G.ps[:, t, 0:w], ACT.Identity,
                                         bias=S.vecs[:, V_GATEB:V_GATEB + 1])
                ins.then_inc(G.psum_free[0], 1)
                G.split_hi(act, 2, 0, 1)

                def pair(i, first):
                    n = 2 * i + 1
                    act.wait_ge(G.gemm_done, n + 1)
                    if not first:
                        act.wait_ge(conv_ready, i)
                    act.activation(xe_p[:, 3:3 + 2 * TC].rearrange("p (a b) -> p a b", b=TC), G.ps[:, 3:5, 0:TC], ACT.Copy)
                    act.activation(xe_p[:, 3 + 2 * TC:3 + NP_TOK], G.ps[:, 5, 0:NP_TOK - 2 * TC], ACT.Copy)
                    act.activation(xe_s[:, :, 3:], G.ps[:, 5, NP_TOK - 2 * TC:T - 2 * TC].rearrange(
                        "p (s t) -> p s t", t=SLEN), ACT.Copy).then_inc(xr_ready, 1)
                    if not first:
                        root(i - 1)
                    G.split_hi(act, n + 2, 1, i + 1)
                    act.preload_act_table_set('sigmoid_and_others')
                    act.wait_ge(G.gemm_done, n + 2)
                    act.activation(sig[:], G.bank(0), ACT.Sigmoid).then_inc(silu_ready, 1)
                    G.split_hi(act, n + 3, 0, i + 2)
                    for t in range(3):
                        act.wait_ge(lru_gemm, 3 * i + t + 1)
                        if t == 0 and not first:
                            act.wait_ge(gates_used, i)
                        act.activation(gr_e[:, t * TC:(t + 1) * TC], G.ps[:, 6, 0:TC], ACT.Sigmoid,
                                       bias=par[:, 0:1])
                        act.activation(gi_e[:, t * TC:(t + 1) * TC], G.ps[:, 7, 0:TC], ACT.Sigmoid,
                                       bias=par[:, 1:2]).then_inc(gates_ready, 1)
                    act.wait_ge(gates_ready, 3 * i + 3)
                    act.activation(tv[:], gr_e[:, 0:T], ACT.Tanh, scale=par[:, 2:3]).then_inc(tanh_ready, 1)
                    act.preload_act_table_set('natural_log_exp_and_others')
                    if not first:
                        act.wait_ge(scan_done, i)
                    act.activation(av[:], gr_e[:, 0:T], ACT.Exp, scale=par[:, 3:4]).then_inc(decay_ready, 1)
                    act.wait_ge(tanh_ready, i + 1)
                    act.activation(lv[:], tv[:], ACT.Ln, scale=2.0, bias=S.tiny[:])
                    act.wait_ge(decay_ready, i + 1)
                    act.activation(gr_e[:, 0:T], tv[:], ACT.Ln, bias=1.0).then_inc(logs_ready, 1)

                def root(i):
                    act.wait_ge(root_log, i + 1)
                    act.activation(lv[:], lv[:], ACT.Exp, scale=0.5).then_inc(root_ready, 1)

                pair(0, True)
                with act.Fori(1, 8) as i:
                    pair(i, False)
                root(7)

                def tile(g, h, d, tail, first):
                    s = (1 + d) % 2
                    n = A_QKV0 + 8 * g + 2 * h + d
                    kind = groups[g]
                    act.wait_ge(G.gemm_done, n + 1)
                    if not first:
                        act.wait_ge(spilled[s], 32 * (4 * g + h))
                    if kind in ("q", "k", "v"):
                        act.activation(stage[s][:], G.bank(s), ACT.Copy, scale=0.0625 if kind == "k" else 1.0
                                       ).then_inc(stage_ready, 1)
                        act.wait_ge(stage_ready, 8 * g + 2 * h + d + 1)
                        act.sem_inc(G.psum_free[s], 1)
                    else:
                        if kind == "og":
                            act.activation(stage[s][:], G.bank(s), ACT.Sigmoid).then_inc(stage_ready, 1)
                            act.wait_ge(stage_ready, 8 * g + 2 * h + d + 1)
                            act.sem_inc(G.psum_free[s], 1)
                        else:
                            act.activation(stage[s][:], G.bank(s), ACT.Sigmoid).then_inc(sigmoid_ready, 1)
                    if not tail:
                        G.split_hi(act, n + 2, s, (A_QKV0 + 8 * g + d) // 2 + 1 + h)

                for g in range(len(groups)):
                    last = g == len(groups) - 1
                    if g == 0:
                        for d in range(2):
                            tile(g, 0, d, False, True)
                    with act.Fori(1 if g == 0 else 0, 3 if last else 4) as h:
                        for d in range(2):
                            tile(g, h, d, False, False)
                    if last:
                        for d in range(2):
                            tile(g, 3, d, True, False)
                    if g == 0:
                        gate_rows_act(act)
                    if g == 3:
                        gate_rows_act_out(act)

            @block.vector
            def _(dve):
                dve.memset(xe_p[:, 0:3], 0.0).then_inc(cleared, 1)
                dve.memset(xc[:, T:TP], 0.0).then_inc(cleared, 1)
                dve.wait_ge(cleared, 2)
                G.split_lo(dve, 2, 0)
                dve.wait_ge(small_in, 48)

                def conv(i, first):
                    link = linker(dve, conv_chain, i * CONV_STEPS)
                    cw = [S.vecs[:, bass.ds(V_CONVW + j * 8 + i, 1)] for j in range(4)]
                    cb = S.vecs[:, bass.ds(V_CONVB + i, 1)]
                    dve.tensor_copy(xe_s[:, :, 0:3], conv0[:, bass.ds(i, 1), :, :].rearrange("p o s j -> p (o s) j"))
                    dve.wait_ge(xr_ready, i + 1)
                    dve.sem_inc(G.psum_free[1], 1)
                    dve.tensor_copy(par[:, 0:2], S.vecs[:, V_BA:V_BA + 16].rearrange("p (m i) -> p m i", i=8)[:, :, bass.ds(i, 1)]
                                    .rearrange("p m o -> p (m o)"))
                    dve.tensor_copy(par[:, 2:4], S.derived[:, :, bass.ds(i, 1)].rearrange("p m o -> p (m o)"))
                    if not first:
                        dve.wait_ge(ixc_ready, i)
                    link(dve.tensor_scalar(xc[:, 0:NP_TOK], xe_p[:, 0:NP_TOK], cw[0], cb, ALU.mult, ALU.add))
                    link(dve.tensor_scalar(seqs(xc), xe_s[:, :, 0:SLEN], cw[0], cb, ALU.mult, ALU.add))
                    for j in range(1, 4):
                        link(dve.scalar_tensor_tensor(out=xc[:, 0:NP_TOK], in0=xe_p[:, j:j + NP_TOK], scalar=cw[j],
                                                      in1=xc[:, 0:NP_TOK], op0=ALU.mult, op1=ALU.add))
                        link(dve.scalar_tensor_tensor(out=seqs(xc), in0=xe_s[:, :, j:j + SLEN], scalar=cw[j],
                                                      in1=seqs(xc), op0=ALU.mult, op1=ALU.add))
                        if j == 1:
                            G.split_lo(dve, 2 * i + 3, 1)
                    dve.tensor_copy(cp_out[:, bass.ds(i, 1), :].rearrange("p o j -> p (o j)"), xe_p[:, NP_TOK:NP_TOK + 3])
                    dve.tensor_copy(cs_out[:, bass.ds(i, 1), :, :].rearrange("p o s j -> p (o s) j"),
                                    xe_s[:, :, SLEN:SLEN + 3]).then_inc(conv_ready, 1)
                    assert link.count() == CONV_STEPS

                def inputs(i):
                    dve.wait_ge(ixc_ready, i + 1)
                    dve.wait_ge(root_ready, i + 1)
                    dve.tensor_tensor(lv[:], lv[:], gi_e[:, 0:T], ALU.mult).then_inc(gates_used, 1)

                def scan(i, first):
                    link = linker(dve, scan_chain, i * SCAN_STEPS)
                    dve.wait_ge(gates_used, i + 1)
                    link(dve.tensor_tensor(tmp8[:], seq_cols(av, 0), h0[:, bass.ds(i, 1), :].rearrange("p o s -> p (o s)"), ALU.mult))
                    link(dve.tensor_tensor(seq_cols(lv, 0), seq_cols(lv, 0), tmp8[:], ALU.add))
                    link(dve.memset(seq_cols(av, 0), 0.0))
                    link(dve.tensor_tensor_scan(hv[:], av[:], lv[:], 0.0, ALU.mult, ALU.add))
                    dve.tensor_copy(hp_out[:, bass.ds(i, 1)], hv[:, NP_TOK - 1:NP_TOK])
                    dve.tensor_copy(hs_out[:, bass.ds(i, 1), :].rearrange("p o s -> p (o s)"),
                                    seq_cols(hv, SLEN - 1)).then_inc(scan_done, 1)
                    if not first:
                        dve.wait_ge(lru_spilled, 32 * i)
                    dve.tensor_tensor(lout[:], hv[:], silu_f[:, 0:T], ALU.mult).then_inc(lru_out_ready, 1)
                    assert link.count() == SCAN_STEPS

                def gate(i):
                    dve.wait_ge(silu_ready, i + 1)
                    if not (isinstance(i, int) and i == 0):
                        dve.wait_ge(lru_out_ready, i)
                    dve.tensor_tensor(silu[:], G.bank(0), sig[:], ALU.mult).then_inc(G.psum_free[0], 1)
                    G.split_lo(dve, 2 * i + 4, 0)
                    dve.wait_ge(logs_ready, i + 1)
                    dve.tensor_tensor(lv[:], lv[:], gr_e[:, 0:T], ALU.subtract).then_inc(root_log, 1)

                conv(0, True)
                gate(0)
                inputs(0)
                conv(1, False)
                scan(0, True)
                gate(1)
                with dve.Fori(2, 8) as i:
                    inputs(i - 1)
                    conv(i, False)
                    scan(i - 1, False)
                    gate(i)
                inputs(7)
                scan(7, False)

                def tile(g, h, d, tail):
                    s = (1 + d) % 2
                    n = A_QKV0 + 8 * g + 2 * h + d
                    kind = groups[g]
                    if kind == "z":
                        dve.wait_ge(sigmoid_ready, 2 * h + d + 1)
                        dve.scalar_tensor_tensor(out=stage[s][:], in0=G.bank(s), scalar=S.vecs[:, bass.ds(V_MNORM + 2 * h + d, 1)],
                                                     in1=stage[s][:], op0=ALU.mult, op1=ALU.mult).then_inc(z_ready, 1)
                        dve.wait_ge(z_ready, 2 * h + d + 1)
                        dve.sem_inc(G.psum_free[s], 1)
                    if not tail:
                        G.split_lo(dve, n + 2, s)
                for g in range(len(groups)):
                    last = g == len(groups) - 1
                    with dve.Fori(0, 3 if last else 4) as h:
                        for d in range(2):
                            tile(g, h, d, False)
                    if g < 2:
                        gate_rows_dve(dve, g)
                    if last:
                        for d in range(2):
                            tile(g, 3, d, True)

            @block.gpsimd
            def _(pool):
                with pool.Fori(0, 8) as i:
                    pool.wait_ge(gates_ready, 3 * i + 3)
                    pool.tensor_tensor(gi_e[:, 0:T], gi_e[:, 0:T], xc[:, 0:T], ALU.mult).then_inc(ixc_ready, 1)

            @block.tensor
            def _(pe):
                def gate_round(i, t):
                    def go():
                        if t == 0:
                            pe.wait_ge(conv_ready, i + 1)
                            pe.wait_ge(lru_w_in, 16 * i + 16)
                        if not (isinstance(i, int) and i == 0 and t == 0):
                            pe.wait_ge(gates_ready, 3 * i + t)
                        for m in range(2):
                            ins = pe.matmul(G.ps[:, 6 + m, 0:TC], lru_w[:, m, :], xc[:, t * TC:(t + 1) * TC],
                                            start=True, stop=True)
                        ins.then_inc(lru_gemm, 1)
                    return go

                def gates(i):
                    return {1: gate_round(i, 0), 2: gate_round(i, 1), 3: gate_round(i, 2)}

                def pair(i, hooks):
                    G.products(pe, 2 * i + 1, 1, i, hooks)
                    G.products(pe, 2 * i + 2, 0, i + 1, {})
                pair(0, {})
                pair(1, gates(0))
                with pe.Fori(2, 8) as i:
                    pair(i, gates(i - 1))
                G.products(pe, A_QKV0, 1, A_QKV0 // 2, gates(7))
                G.products(pe, A_QKV0 + 1, 0, A_QKV0 // 2 + 1, {})

                for g in range(len(groups)):
                    if g == 3:
                        gate_rows_pe(pe)
                    with pe.Fori(1 if g == 0 else 0, 4) as h:
                        for d in range(2):
                            G.products(pe, A_QKV0 + 8 * g + 2 * h + d, (1 + d) % 2, (A_QKV0 + 8 * g + d) // 2 + h, {})


ROW_STEPS = 14
CONV_STEPS, SCAN_STEPS = 8, 4


class OutWeights:

    def __init__(self, S, a, name, w_d, first, tiles):
        self.rows = a.sb(name, [P, tiles, D])
        self.w_d, self.first, self.tiles = w_d, first, tiles
        self.loaded = S.a.sem(f"{name}_in")

    def load(self, sp, pair, done=None):
        sp.dma_start(self.rows[:, bass.ds(2 * pair, 2), :],
                     self.w_d[:, bass.ds(self.first + 2 * pair, 2), :]).then_inc(self.loaded if done is None else done, 16)


class OutProjection:

    def __init__(self, S, a, name, early, late, order, layer, x_d, y_d):
        self.w_low = a.sb(f"{name}_wout_lo", [P, 16, D], F32R)
        self.S, self.x_d, self.y_d = S, x_d, y_d
        self.early, self.late, self.order = early, late, order
        self.w_hi = a.sb(f"{name}_wout_hi", [P, 16, D], F32R)
        self.m_hi = a.sb(f"{name}_mix_hi", [P, 16, P], F32R)
        self.m_lo = a.sb(f"{name}_mix_lo", [P, 16, P], F32R)
        self.xres = a.sb(f"{name}_xres", [P, D])
        self.yb = a.sb(f"{name}_yb", [P, D])
        self.post = a.sb(f"{name}_post", [P, D])
        self.stat = a.sb(f"{name}_post_stat", [P, 6])
        self.layer = layer
        sem = S.a.sem
        self.late_in = [sem(f"{name}_wout_late_in{q}") for q in range(late.tiles // 2)] if late else []
        self.w_hi_ready = sem(f"{name}_wout_hi_ready")
        self.w_ready = sem(f"{name}_wout_ready")
        self.x_in = sem(f"{name}_xres_in")
        self.out_done = sem(f"{name}_out_done")
        self.squares = sem(f"{name}_squares")
        self.sq_sum = sem(f"{name}_square_sum")
        self.post_ln = sem(f"{name}_post_ln")
        self.post_rstd = sem(f"{name}_post_rstd")
        self.out_read = sem(f"{name}_out_read")
        self.y_ready = sem(f"{name}_y_ready")
        self.y_stored = sem(f"{name}_y_stored")

    def load_late(self, sp):
        for q, done in enumerate(self.late_in):
            self.late.load(sp, q, done)

    def load_post(self, sp, post_d):
        sp.dma_start(self.post[:], post_d[:, self.layer, :]).then_inc(self.y_stored, 16)

    def w_lo(self, e):
        return self.w_low[:, (e - self.early.first) % 16, :]

    def raw(self, e):
        w = self.early if self.early.first <= e < self.early.first + self.early.tiles else self.late
        return w.rows[:, e - w.first, :]

    def split_w_hi(self, act, k):
        for e in self.order[4 * k:4 * k + 4]:
            if self.late and e < self.early.first:
                act.wait_ge(self.late_in[e // 2], 16)
            else:
                act.wait_ge(self.early.loaded, 16 * self.early.tiles // 2)
            act.activation(self.w_hi[:, e, :], self.raw(e), ACT.Copy).then_inc(self.w_hi_ready, 1)

    def split_w_lo(self, dve, k):
        for j, e in enumerate(self.order[4 * k:4 * k + 4]):
            dve.wait_ge(self.w_hi_ready, 4 * k + j + 1)
            dve.tensor_tensor(self.w_lo(e), self.raw(e), self.w_hi[:, e, :].bitcast(F32), ALU.subtract
                              ).then_inc(self.w_ready, 1)

    def products(self, pe, ps, e, first, last, new_w):
        if new_w:
            pe.wait_ge(self.w_ready, self.order.index(e) + 1)
        w_lo = self.w_lo(e)
        for half in range(2):
            cols = slice(half * 512, half * 512 + 512)
            w_hi = self.w_hi[:, e, cols]
            for j, (m, w) in enumerate(((self.m_hi, w_hi), (self.m_hi, w_lo[:, cols]), (self.m_lo, w_hi))):
                ins = pe.matmul(ps[:, 6 + half, :], m[:, e, :], w, start=first and j == 0, stop=last and j == 2)
        if last:
            ins.then_inc(self.out_done, 1)

    def post_act(self, act, ps, c, rows):
        st = self.stat
        act.wait_ge(self.y_stored, 16 * c + 16)
        act.wait_ge(self.out_done, c + 1)
        for half in range(2):
            ins = act.activation(self.yb[0:rows, half * 512:half * 512 + 512], ps[0:rows, 6 + half, :], ACT.Square,
                                 accum_out=st[0:rows, half:half + 1])
            ins.then_inc(self.squares, 1)
            act.wait_ge(self.squares, 2 * c + half + 1)
        act.wait_ge(self.sq_sum, c + 1)
        act.activation(st[0:rows, 3:4], st[0:rows, 2:3], ACT.Ln, scale=1.0 / D, bias=self.S.eps[0:rows, :]).then_inc(self.post_ln, 1)
        act.wait_ge(self.post_ln, c + 1)
        act.activation(st[0:rows, 4:5], st[0:rows, 3:4], ACT.Exp, scale=-0.5).then_inc(self.post_rstd, 1)

    def post_dve(self, dve, ps, c, rows):
        st = self.stat
        dve.wait_ge(self.squares, 2 * c + 2)
        dve.tensor_tensor(st[0:rows, 2:3], st[0:rows, 0:1], st[0:rows, 1:2], ALU.add).then_inc(self.sq_sum, 1)
        dve.wait_ge(self.post_rstd, c + 1)
        for half in range(2):
            cols = slice(half * 512, half * 512 + 512)
            ins = dve.scalar_tensor_tensor(out=self.yb[0:rows, cols], in0=ps[0:rows, 6 + half, :], scalar=st[0:rows, 4:5],
                                           in1=self.post[0:rows, cols], op0=ALU.mult, op1=ALU.mult)
        ins.then_inc(self.out_read, 1)

    def post_pool(self, pool, c, rows):
        pool.wait_ge(self.out_read, c + 1)
        pool.wait_ge(self.x_in, 16 * c + 16)
        pool.tensor_tensor(self.yb[0:rows, :], self.yb[0:rows, :], self.xres[0:rows, :], ALU.add).then_inc(self.y_ready, 1)

    def load_x(self, sp, c, rows, first):
        if not first:
            sp.wait_ge(self.y_ready, c)
        sp.dma_start(self.xres[0:rows, :], self.x_d[bass.ds(c * P, rows), :]).then_inc(self.x_in, 16)

    def store_y(self, sp, c, rows):
        sp.wait_ge(self.y_ready, c + 1)
        sp.dma_start(self.y_d[bass.ds(c * P, rows), :], self.yb[0:rows, :]).then_inc(self.y_stored, 16)


NRING = 6


def stage_mix_a(nc, S, scr_d, lru_d, w_early, w_late, post_d, x_d, y_d, c0_d, out_cp, out_cs):
    with ExitStack() as ctx:
        a = make_alloc(nc, ctx)
        sem = S.a.sem
        STEP_TILES = [(14, 15, 6, 7)] + [(2 * h - 2, 2 * h - 1, 6 + 2 * h, 7 + 2 * h) for h in range(1, H)]
        order = [8, 9, 0, 1, 10, 11, 2, 3, 12, 13, 4, 5, 14, 15, 6, 7]
        O = OutProjection(S, a, "ma", w_early, w_late, order, 0, x_d, y_d)
        hin = [a.sb(f"ma_hin{s}", [P, AF, P]) for s in range(2)]
        hl = a.sb("ma_hl", [P, 8, P])
        cst = a.sb("ma_state", [P, H, 2, MV])
        vv = [a.sb(f"ma_v{s}", [P, MV + 3]) for s in range(2)]
        og = [a.sb(f"ma_og{s}", [P, 256]) for s in range(2)]
        kw = [a.sb(f"ma_kw{s}", [P, 256]) for s in range(2)]
        ei = a.sb("ma_exponent", [P, P])
        ee = [a.sb(f"ma_decay{s}", [P, P]) for s in range(2)]
        sc = [a.sb(f"ma_scores{s}", [P, P]) for s in range(2)]
        inter = a.sb("ma_inter", [P, MV])
        num = a.sb("ma_num", [P, MV])
        gg = a.sb("ma_gated", [P, 256])
        gn = a.sb("ma_normed", [P, 256])
        mp = a.sb("ma_mix_plain", [P, 256])
        sm = a.sb("ma_small", [P, 8])
        junk = a.sb("ma_junk", [P, 256])
        kw8 = a.sb("ma_kw8", [LAST, 2, 256])
        qm = [a.sb(f"ma_q_masked{i}", [P, 2, 480]) for i in range(2)]
        cs = [a.sb(f"ma_sample_state{r}", [P, 2, MV]) for r in range(NRING - 2)]
        cs += [t[:, 0:2 * MV].rearrange("p (d v) -> p d v", d=2) for t in (O.xres, O.yb)]
        ps = a.ps("ma_ps", [P, 8, 512])

        hin_in = [sem(f"ma_hin_in{s}") for s in range(2)]
        z_in = [sem(f"ma_z_in{s}") for s in range(2)]
        hl_in = sem("ma_hl_in")
        hl_hi = sem("ma_hl_hi_ready")
        hl_ready = sem("ma_hl_ready")
        init_done = sem("ma_init_done")
        turned = sem("ma_turned")
        v_ready = sem("ma_v_ready")
        ei_ready = sem("ma_exponent_ready")
        e_ready = sem("ma_decay_ready")
        kw_ready = sem("ma_kw_ready")
        sc_ready = sem("ma_scores_ready")
        b_done = sem("ma_products_done")
        inter_ready = sem("ma_inter_ready")
        num_ready = sem("ma_num_ready")
        state_ready = sem("ma_state_ready")
        den_chain = sem("ma_den_chain")
        gated_ready = sem("ma_gated_ready")
        sq_chain = sem("ma_square_chain")
        rstd_ready = sem("ma_rstd_ready")
        gn_ready = sem("ma_normed_ready")
        c_done = sem("ma_head_turned")
        mp_ready = sem("ma_mix_plain_ready")
        mhi_ready = sem("ma_mix_hi_ready")
        mix_ready = sem("ma_mix_ready")
        qm_ready = sem("ma_q_masked_ready")
        s_in = [sem(f"ma_sample_in{r}") for r in range(NRING)]
        s_out = [sem(f"ma_sample_out{r}") for r in range(NRING)]
        upd_done = sem("ma_update_done")
        kw8_ready = sem("ma_group_keys_ready")
        s_ready = sem("ma_sample_ready")
        s_read = sem("ma_update_read")
        p_stored = sem("ma_prompt_state_stored")
        pool_chain = sem("ma_pool_chain")

        LASTS = [TAIL - 1] + [TAIL + SLEN * b + SLEN - 1 for b in range(NSEQ)]

        def not_first(n, least=1):
            return not (isinstance(n, int) and n < least)

        def turned_head(rows):
            return [ps[:, 4 + d, 384:384 + rows] if rows == P else ps[:, 3, 384 + d * rows:384 + (d + 1) * rows]
                    for d in range(2)]

        with nc.Block() as block:
            @block.sync
            def _(sp):
                def load_head(n, c, h, rows):
                    piece = scr_d[bass.ds(c, 1), h, :, :, 0:rows].rearrange("o p f t -> (o p) f t")
                    if not_first(n, 2):
                        sp.wait_ge(b_done, n - 1)
                    sp.dma_start(hin[h % 2][:, 0:8, 0:rows], piece[:, 0:8, :]).then_inc(hin_in[h % 2], 16)
                    if not_first(n, 2):
                        sp.wait_ge(mp_ready, n - 1)
                    sp.dma_start(hin[h % 2][:, 8:10, 0:rows], piece[:, 8:10, :]).then_inc(z_in[h % 2], 16)

                def load_hl(c, rows):
                    if not_first(c):
                        sp.wait_ge(hl_ready, c)
                    sp.dma_start(hl[:, :, 0:rows], lru_d[bass.ds(c, 1), :, :, 0:rows].rearrange("o p f t -> (o p) f t")
                                 ).then_inc(hl_in, 16)
                load_head(0, 0, 0, P)
                load_head(1, 0, 1, P)
                load_hl(0, P)
                O.load_late(sp)
                O.load_post(sp, post_d)
                O.load_x(sp, 0, P, True)
                load_head(2, 0, 2, P)
                load_head(3, 0, 3, P)

                with sp.Fori(1, 8) as c:
                    load_head(4 * c, c, 0, P)
                    load_hl(c, P)
                    for h in range(1, H):
                        load_head(4 * c + h, c, h, P)
                    O.store_y(sp, c - 1, P)
                    O.load_x(sp, c, P, False)
                load_head(32, 8, 0, LAST)
                load_hl(8, LAST)
                load_head(33, 8, 1, LAST)

                def load_state(m):
                    r = m % NRING
                    if m >= NRING:
                        sp.wait_ge(s_out[r], 16 * (m // NRING))
                    sp.dma_start(cs[r][:], c0_d[m % NSEQ, m // NSEQ]).then_inc(s_in[r], 16)

                def store_state(m):
                    r = m % NRING
                    sp.wait_ge(s_ready, m + 1)
                    sp.dma_start(out_cs[m % NSEQ, m // NSEQ], cs[r][:]).then_inc(s_out[r], 16)
                for m in range(NRING - 2):
                    load_state(m)
                O.store_y(sp, 7, P)
                load_state(NRING - 2)
                sp.wait_ge(O.y_stored, 16 * NC)
                load_state(NRING - 1)
                for h in range(H):
                    for b in range(NSEQ):
                        m = h * NSEQ + b
                        store_state(m)
                        if m + NRING < H * NSEQ:
                            load_state(m + NRING)
                        if h in (1, 2) and b == 3:
                            load_head(33 + h, 8, 1 + h, LAST)
                    sp.wait_ge(state_ready, 32 + h + 1)
                    sp.dma_start(out_cp[h], cst[:, h, :, :]).then_inc(p_stored, 16)
                sp.wait_ge(s_out[NRING - 2], 16 * len(range(NRING - 2, H * NSEQ, NRING)))
                O.load_x(sp, 8, LAST, False)
                O.store_y(sp, 8, LAST)
                sp.wait_ge(O.y_stored, 16 * NC + 16)
                sp.wait_ge(p_stored, 16 * H)
                for r in range(NRING):
                    sp.wait_ge(s_out[r], 16 * len(range(r, H * NSEQ, NRING)))

            @block.tensor
            def _(pe):
                def part_a(n, c, h, s, rows):
                    pe.wait_ge(hin_in[s], 16 * (2 * c + h // 2) + 16)
                    t = hin[s]
                    for d in range(2):
                        pe.transpose(ps[0:rows, 1, 256 + d * P:256 + (d + 1) * P], t[:, 2 + d, 0:rows], S.ident[:])
                        pe.transpose(ps[0:rows, 1, d * P:(d + 1) * P], t[:, 4 + d, 0:rows], S.ident[:])
                        pe.transpose(ps[0:rows, 0, 256 + d * P:256 + (d + 1) * P], t[:, 6 + d, 0:rows], S.ident[:])
                    pe.matmul(ps[0:rows, 0, 128:128 + rows], S.sel[:, h, 0:rows], S.rrow[:, bass.ds(c * P, rows)],
                              start=True, stop=True)
                    for d in range(2):
                        ins = pe.matmul(ps[0:rows, 0, 0:rows], t[:, 2 + d, 0:rows], t[:, d, 0:rows], start=(d == 0), stop=(d == 1))
                    ins.then_inc(turned, 1)

                def part_b(n, c, h, s):
                    if not_first(n):
                        pe.wait_ge(num_ready, n)
                        pe.wait_ge(state_ready, n)
                    else:
                        pe.wait_ge(init_done, 1)
                    for d in range(2):
                        pe.matmul(ps[:, 2, 0:MV], hin[s][:, d, :], cst[:, h, d, :], start=(d == 0), stop=(d == 1))
                    pe.wait_ge(v_ready, n + 1)
                    pe.wait_ge(sc_ready, n + 1)
                    pe.matmul(ps[:, 3, 0:MV], sc[s][:], vv[s][:, 0:MV], start=True, stop=True)
                    pe.wait_ge(kw_ready, n + 1)
                    if not_first(n):
                        pe.wait_ge(mp_ready, n)
                    for d in range(2):
                        ins = pe.matmul(ps[:, 4 + d, 0:MV], kw[s][:, d * P:(d + 1) * P], vv[s][:, 0:MV], start=True, stop=True)
                    ins.then_inc(b_done, 1)

                def part_c(n, s, rows):
                    pe.wait_ge(gn_ready, n + 1)
                    for d in range(2):
                        ins = pe.transpose(turned_head(rows)[d], gn[0:rows, d * P:(d + 1) * P], S.ident[0:rows, 0:rows])
                    ins.then_inc(c_done, 1)

                def out(c, h, new_w):
                    tiles = order[0:4] if new_w and h == 0 else STEP_TILES[(h + 1) % H]
                    for e in tiles:
                        if e == 8:
                            pe.wait_ge(hl_ready, c + 1)
                        if e == 0 and not_first(c):
                            pe.wait_ge(O.out_read, c)
                        if e < 8 and e % 2 == 0:
                            pe.wait_ge(mix_ready, 4 * c + e // 2 + 1)
                        O.products(pe, ps, e, h == 0 and e == tiles[0], e == 7, new_w)

                def chunk(c, first, last):
                    for h in range(H):
                        n, h1 = 4 * c + h, (h + 1) % H
                        c1 = c + (h == 3)
                        if not (last and h == 3):
                            part_a(n + 1, c1, h1, h1 % 2, P)
                        if not (first and h == 0):
                            out(c - (h == 0), (h - 1) % H, first)
                        part_c(n, h % 2, P)
                        if not (last and h == 3):
                            part_b(n + 1, c1, h1, h1 % 2)
                part_a(0, 0, 0, 0, P)
                part_b(0, 0, 0, 0)
                chunk(0, True, False)
                pe.wait_ge(O.w_ready, 16)
                with pe.Fori(1, 7) as c:
                    chunk(c, False, False)
                chunk(7, False, True)
                part_a(32, 8, 0, 0, LAST)
                out(7, 3, False)

                for h in range(H):
                    n, s = 32 + h, h % 2
                    pe.wait_ge(num_ready, n)
                    if h == 0:
                        pe.wait_ge(state_ready, n)
                        pe.wait_ge(mp_ready, n)
                    pe.wait_ge(qm_ready, h + 1)
                    pe.wait_ge(v_ready, n + 1)
                    for g in range(NG):
                        m = h * NSEQ + g - 1
                        r = m % NRING
                        if g:
                            pe.wait_ge(s_in[r], 16 * (m // NRING) + 16)
                        for d in range(2):
                            st = cst[:, h, d, :] if g == 0 else cs[r][:, d, :]
                            pe.matmul(ps[0:LAST, 2, 0:MV], qm[s][:, d, g * LAST:(g + 1) * LAST], st,
                                      start=(g == 0 and d == 0), stop=(g == NG - 1 and d == 1))
                        u = h * NG + g
                        if u >= 2:
                            pe.wait_ge(s_read, u - 1)
                        if u == 1:
                            pe.wait_ge(O.out_read, 8)
                        pe.wait_ge(kw8_ready, u + 1)
                        for d in range(2):
                            ins = pe.matmul(ps[:, 4 + 2 * (u % 2) + d, 0:MV], kw8[:, u % 2, d * P:(d + 1) * P],
                                            vv[s][0:LAST, 0:MV], start=True, stop=True)
                        ins.then_inc(upd_done, 1)
                        if h and g == 2:
                            part_c(n - 1, 1 - s, LAST)
                    pe.wait_ge(sc_ready, n + 1)
                    pe.wait_ge(mp_ready, n)
                    pe.matmul(ps[0:LAST, 3, 0:MV], sc[s][0:LAST, 0:LAST], vv[s][0:LAST, 0:MV], start=True, stop=True).then_inc(b_done, 1)
                    if h < 3:
                        part_a(n + 1, 8, h + 1, 1 - s, LAST)
                part_c(35, 1, LAST)
                pe.wait_ge(s_read, H * NG)
                pe.wait_ge(hl_ready, 9)
                for e in [*range(8, 16), *range(8)]:
                    if e < 8 and e % 2 == 0:
                        pe.wait_ge(mix_ready, 32 + e // 2 + 1)
                    O.products(pe, ps, e, e == 8, e == 7, False)

            @block.scalar
            def _(act):
                act.preload_act_table_set('natural_log_exp_and_others')
                def hl_split(c, rows):
                    act.wait_ge(hl_in, 16 * c + 16)
                    if not_first(c):
                        act.wait_ge(O.out_done, c)
                    act.activation(O.m_hi[:, 8:16, 0:rows], hl[:, :, 0:rows], ACT.Copy).then_inc(hl_hi, 1)

                def copies(n, s, rows):
                    act.wait_ge(turned, n + 1)
                    if not_first(n, 2):
                        act.wait_ge(b_done, n - 1)
                    act.activation(vv[s][0:rows, 0:256], ps[0:rows, 1, 0:256], ACT.Copy).then_inc(v_ready, 1)
                    act.wait_ge(ei_ready, n + 1)
                    act.activation(ee[s][0:rows, 0:rows], ei[0:rows, 0:rows], ACT.Exp).then_inc(e_ready, 1)
                    act.wait_ge(e_ready, n + 1)

                def part_a(n, s):
                    copies(n, s, P)
                    act.activation(kw[s][:], ps[:, 1, 256:512], ACT.Copy, scale=ee[s][:, P - 1:P]).then_inc(kw_ready, 1)

                def part_b(n, c, h, rows):
                    act.wait_ge(b_done, n + 1)
                    w = S.tok[0:rows, bass.ds(c, 1), 1, h]
                    act.activation(inter[0:rows, :], ps[0:rows, 2, 0:MV], ACT.Copy, scale=w).then_inc(inter_ready, 1)

                def part_c(n, rows):
                    act.wait_ge(gated_ready, n + 1)
                    act.activation(junk[0:rows, :], gg[0:rows, :], ACT.Square, accum_out=sm[0:rows, 4:5]).then_inc(sq_chain, 1)
                    act.wait_ge(sq_chain, 2 * n + 1)
                    act.activation(sm[0:rows, 5:6], sm[0:rows, 4:5], ACT.Ln, scale=1.0 / 256, bias=S.eps[0:rows, :]).then_inc(sq_chain, 1)
                    act.wait_ge(sq_chain, 2 * n + 2)
                    act.activation(sm[0:rows, 6:7], sm[0:rows, 5:6], ACT.Exp, scale=-0.5).then_inc(rstd_ready, 1)

                def part_m(n, c, h, rows):
                    act.wait_ge(mp_ready, n + 1)
                    if h == 0 and not_first(c):
                        act.wait_ge(O.out_done, c)
                    act.activation(O.m_hi[:, 2 * h:2 * h + 2, 0:rows], mp[:].rearrange("p (d t) -> p d t", d=2)[:, :, 0:rows], ACT.Copy
                                   ).then_inc(mhi_ready, 1)

                def chunk(c, first, last):
                    for h in range(H):
                        n = 4 * c + h
                        part_b(n, c, h, P)
                        part_c(n, P)
                        if not (last and h == 3):
                            part_a(n + 1, (h + 1) % 2)
                        if first:
                            O.split_w_hi(act, h)
                        if h == 0:
                            if not first:
                                O.post_act(act, ps, c - 1, P)
                        part_m(n, c, h, P)
                        if h == 0:
                            hl_split(c, P)
                part_a(0, 0)
                chunk(0, True, False)
                with act.Fori(1, 7) as c:
                    chunk(c, False, False)
                chunk(7, False, True)
                copies(32, 0, LAST)
                O.post_act(act, ps, 7, P)
                for h in range(H):
                    n, s = 32 + h, h % 2
                    for g in range(NG):
                        u = h * NG + g
                        if u >= 2:
                            act.wait_ge(upd_done, u - 1)
                        act.activation(kw8[:, u % 2, :], ps[0:LAST, 1, 256:512], ACT.Copy,
                                       scale=ee[s][0:LAST, LASTS[g]:LASTS[g] + 1]).then_inc(kw8_ready, 1)
                        if h and g == 1:
                            part_c(n - 1, LAST)
                        if h and g == 3:
                            part_m(n - 1, 8, h - 1, LAST)
                        if h == 1 and g == 4:
                            hl_split(8, LAST)
                    part_b(n, 8, h, LAST)
                    if h < 3:
                        copies(n + 1, 1 - s, LAST)
                part_c(35, LAST)
                part_m(35, 8, 3, LAST)
                act.wait_ge(s_out[NRING - 1], 16 * len(range(NRING - 1, H * NSEQ, NRING)))
                O.post_act(act, ps, 8, LAST)

            @block.vector
            def _(dve):
                for s in range(2):
                    dve.memset(vv[s][:, 256:257], 1.0)
                dve.memset(cst[:], 0.0).then_inc(init_done, 1)

                def part_a1(n, c, h, s, rows, mask):
                    dve.wait_ge(turned, n + 1)
                    if not_first(n):
                        dve.wait_ge(e_ready, n)
                    dve.scalar_tensor_tensor(out=ei[0:rows, 0:rows], in0=ps[0:rows, 0, 128:128 + rows],
                                             scalar=S.tok[0:rows, bass.ds(c, 1), 0, h], in1=mask[:],
                                             op0=ALU.add, op1=ALU.add).then_inc(ei_ready, 1)
                    if not_first(n, 2):
                        dve.wait_ge(gated_ready, n - 1)
                    dve.tensor_copy(og[s][0:rows, :], ps[0:rows, 0, 256:512])

                def part_a2(n, s, rows):
                    dve.wait_ge(e_ready, n + 1)
                    if not_first(n, 2):
                        dve.wait_ge(b_done, n - 1)
                    dve.tensor_tensor(sc[s][0:rows, 0:rows], ps[0:rows, 0, 0:rows], ee[s][0:rows, 0:rows], ALU.mult).then_inc(sc_ready, 1)

                def part_num(n, rows):
                    dve.wait_ge(inter_ready, n + 1)
                    dve.tensor_tensor(num[0:rows, :], inter[0:rows, :], ps[0:rows, 3, 0:MV], ALU.add).then_inc(num_ready, 1)

                def update(dst, scale, bank):
                    for d in range(2):
                        ins = dve.scalar_tensor_tensor(out=dst[:, d, :], in0=dst[:, d, :], scalar=scale,
                                                       in1=ps[:, bank + d, 0:MV], op0=ALU.mult, op1=ALU.add)
                    return ins

                def part_den(n, c, h, s, rows):
                    link = linker(dve, den_chain, 3 * n)
                    dve.wait_ge(num_ready, n + 1)
                    link(dve.scalar_tensor_tensor(out=sm[0:rows, 0:1], in0=num[0:rows, 256:257], scalar=-1.0,
                                                  in1=num[0:rows, 256:257], op0=ALU.mult, op1=ALU.max))
                    link(dve.tensor_tensor(sm[0:rows, 1:2], sm[0:rows, 0:1], S.tok[0:rows, bass.ds(c, 1), 2, h], ALU.max))
                    link(dve.reciprocal(sm[0:rows, 2:3], sm[0:rows, 1:2]))
                    dve.scalar_tensor_tensor(out=gg[0:rows, :], in0=num[0:rows, 0:256], scalar=sm[0:rows, 2:3],
                                             in1=og[s][0:rows, :], op0=ALU.mult, op1=ALU.mult).then_inc(gated_ready, 1)

                def part_c(n, rows):
                    dve.wait_ge(rstd_ready, n + 1)
                    dve.tensor_scalar(gn[0:rows, :], gg[0:rows, :], sm[0:rows, 6:7], None, ALU.mult).then_inc(gn_ready, 1)

                def part_m(n, c, h, s, rows):
                    dve.wait_ge(c_done, n + 1)
                    dve.wait_ge(z_in[s], 16 * (2 * c + h // 2) + 16)
                    if not_first(n):
                        dve.wait_ge(mix_ready, n)
                    for d in range(2):
                        ins = dve.tensor_tensor(mp[:, d * P:d * P + rows], turned_head(rows)[d], hin[s][:, 8 + d, 0:rows], ALU.mult)
                    ins.then_inc(mp_ready, 1)

                def chunk(c, first, last):
                    for h in range(H):
                        n, s = 4 * c + h, h % 2
                        part_num(n, P)
                        part_den(n, c, h, s, P)
                        update(cst[:, h, :, :], S.wc[:, h, bass.ds(c, 1)], 4).then_inc(state_ready, 1)
                        if not (last and h == 3):
                            part_a1(n + 1, c + (h == 3), (h + 1) % H, 1 - s, P, S.mask_add)
                        part_c(n, P)
                        if not (last and h == 3):
                            part_a2(n + 1, 1 - s, P)
                        if first:
                            O.split_w_lo(dve, h)
                        part_m(n, c, h, s, P)
                        if h == 0 and not first:
                            O.post_dve(dve, ps, c - 1, P)
                part_a1(0, 0, 0, 0, P, S.mask_add)
                part_a2(0, 0, P)
                chunk(0, True, False)
                with dve.Fori(1, 7) as c:
                    chunk(c, False, False)
                chunk(7, False, True)
                part_a1(32, 8, 0, 0, LAST, S.mask_add8)
                part_a2(32, 0, LAST)
                O.post_dve(dve, ps, 7, P)
                for h in range(H):
                    n, s = 32 + h, h % 2
                    for g in range(NG):
                        u = h * NG + g
                        dve.wait_ge(upd_done, u + 1)
                        bank = 4 + 2 * (u % 2)
                        if g == 0:
                            update(cst[:, h, :, :], S.wc[:, h, 8:9], bank).then_inc(state_ready, 1)
                            dve.wait_ge(state_ready, n + 1)
                        else:
                            m = u - h - 1
                            update(cs[m % NRING][:], S.wc[:, h, 8 + g:9 + g], bank).then_inc(s_ready, 1)
                            dve.wait_ge(s_ready, m + 1)
                        dve.sem_inc(s_read, 1)
                        if h and g == 1:
                            part_c(n - 1, LAST)
                        if h and g == 3:
                            part_m(n - 1, 8, h - 1, 1 - s, LAST)
                    part_num(n, LAST)
                    if h < 3:
                        part_a1(n + 1, 8, h + 1, 1 - s, LAST, S.mask_add8)
                        part_a2(n + 1, 1 - s, LAST)
                    part_den(n, 8, h, s, LAST)
                part_c(35, LAST)
                part_m(35, 8, 3, 1, LAST)
                O.post_dve(dve, ps, 8, LAST)

            @block.gpsimd
            def _(pool):
                link = linker(pool, pool_chain)
                for i in range(2):
                    link(pool.memset(qm[i][:], 0.0))

                def lo(tiles, plain, rows):
                    return pool.tensor_tensor(O.m_lo[:, tiles, 0:rows], plain, O.m_hi[:, tiles, 0:rows].bitcast(F32), ALU.subtract)

                def masked_q(h):
                    pool.wait_ge(hin_in[h % 2], 16 * (16 + h // 2) + 16)
                    if h >= 2:
                        pool.wait_ge(upd_done, NG * (h - 1))
                    for d in range(2):
                        q = hin[h % 2][:, d, :]
                        pool.tensor_copy(qm[h % 2][:, d, 0:TAIL], q[:, 0:TAIL])
                        ins = pool.tensor_copy(qm[h % 2][:, d, 64:480].rearrange("p (s r) -> p s r", r=LAST + SLEN)[:, :, 0:SLEN],
                                               q[:, TAIL:LAST].rearrange("p (s t) -> p s t", t=SLEN))
                    ins.then_inc(qm_ready, 1)

                def lo_head(c, h, rows):
                    pool.wait_ge(mhi_ready, 4 * c + h + 1)
                    lo(slice(2 * h, 2 * h + 2), mp[:].rearrange("p (d t) -> p d t", d=2)[:, :, 0:rows], rows).then_inc(mix_ready, 1)

                def lo_hl(c, rows):
                    pool.wait_ge(hl_hi, c + 1)
                    lo(slice(8, 16), hl[:, :, 0:rows], rows).then_inc(hl_ready, 1)

                def chunk(c, first):
                    lo_head(c, 0, P)
                    lo_hl(c, P)
                    if not first:
                        O.post_pool(pool, c - 1, P)
                    for h in range(1, H):
                        lo_head(c, h, P)
                chunk(0, True)
                with pool.Fori(1, 8) as c:
                    chunk(c, False)
                masked_q(0)
                O.post_pool(pool, 7, P)
                masked_q(1)
                for h in range(H):
                    lo_head(8, h, LAST)
                    if h == 0:
                        lo_hl(8, LAST)
                    if h < 2:
                        masked_q(h + 2)
                O.post_pool(pool, 8, LAST)


def stage_project_c(nc, S, G, a_up_d, scr_d, w_out):
    with ExitStack() as ctx:
        a = make_alloc(nc, ctx)
        stage = [a.sb(f"pc_stage{s}", [P, 3, TC]) for s in range(2)]
        flat = [s[:].rearrange("p a b -> p (a b)") for s in stage]
        alow = a.sb("pc_alow", [16, TP])
        a_up = a.sb("pc_a_up", [16, P])
        xg = a.sb("pc_gate", [P, TP])
        ab = a.sb("pc_gate_abs", [P, TP])
        bsum = a.sb("pc_decay_sum", [P, T])
        eq = a.sb("pc_exp_q", [P, 3, TC])
        ek = a.sb("pc_exp_k", [P, 3, TC])
        eqf, ekf = (e[:].rearrange("p a b -> p (a b)") for e in (eq, ek))
        gt = a.sb("pc_group_sum", [P, 17])
        par = a.sb("pc_bias", [P, 1])
        mid = a.sb("pc_mid", [P, 8])

        sem = S.a.sem
        cleared = sem("pc_cleared")
        alow_ready = sem("pc_alow_ready")
        a_up_in = sem("pc_a_up_in")
        lg_done = sem("pc_log_gate_done")
        lg_read = sem("pc_log_gate_read")
        act_chain = sem("pc_act_chain")
        soft_ready = sem("pc_softplus_ready")
        par_ready = sem("pc_bias_ready")
        dve_chain = sem("pc_dve_chain")
        cent_ready = sem("pc_centred_ready")
        exps_ready = sem("pc_exps_ready")
        qk_ready = sem("pc_qk_ready")
        v_ready = sem("pc_v_ready")
        r_ready = sem("pc_r_ready")
        sigmoid_ready = sem("pc_sigmoid_ready")
        spilled = [sem(f"pc_spilled{s}") for s in range(2)]

        def n_slot(d):
            return (C_V0 + d) % 2

        def seqs(buf):
            return buf[:, NP_TOK:T].rearrange("p (s t) -> p s t", t=SLEN)

        def chunked(buf):
            return buf[:, 0:8 * P].rearrange("p (c t) -> p c t", t=P)

        with nc.Block() as block:
            @block.sync
            def _(sp):
                def spill(ready, m, s, head, f):
                    sp.wait_ge(ready, m + 1)
                    dst = scr_d[0:8, bass.ds(head, 1), :, f, :].rearrange("c o p t -> p (o c) t")
                    sp.dma_start(dst, flat[s][:, 0:8 * P].rearrange("p (c t) -> p c t", t=P)).then_inc(spilled[s], 16)
                    sp.dma_start(scr_d[8, bass.ds(head, 1), :, f, 0:LAST].rearrange("o p t -> (o p) t"),
                                 flat[s][:, 8 * P:T]).then_inc(spilled[s], 16)
                G.load(sp, 2, 0)

                def pair(hh, d, first):
                    i = 2 * hh + d
                    n = 2 * i + 1
                    if not first:
                        sp.wait_ge(lg_done, 3 * i)
                    sp.dma_start(a_up[:], a_up_d[:, bass.ds(i, 1), :].rearrange("r o k -> r (o k)")).then_inc(a_up_in, 16)
                    G.load(sp, n + 2, 1)
                    G.load(sp, n + 3, 0)
                    if not first:
                        spill(qk_ready, 2 * i - 1, 0, hh - (d == 0), 3 - d)
                    spill(qk_ready, 2 * i, 1, hh, d)
                pair(0, 0, True)
                pair(0, 1, False)
                with sp.Fori(1, 4) as hh:
                    for d in range(2):
                        pair(hh, d, False)
                spill(qk_ready, 15, 0, 3, 3)

                def two(g, h, d, tail):
                    n = C_V0 + 16 * g + 4 * h + d
                    if not tail:
                        G.load(sp, n + 2, n_slot(d))
                    spill((v_ready, r_ready)[g], 4 * h + d, n_slot(d), h, 4 + 4 * g + d)
                for g in range(2):
                    with sp.Fori(0, 4 - g) as h:
                        w_out.load(sp, h + 4 * g)
                        for d in range(4):
                            two(g, h, d, False)
                w_out.load(sp, 7)
                for d in range(4):
                    two(1, 3, d, d >= 2)
                for s in range(2):
                    sp.wait_ge(spilled[s], 32 * 24)

            @block.scalar
            def _(act):
                act.preload_act_table_set('natural_log_exp_and_others')
                act.wait_ge(G.gemm_done, 1)
                for t in range(3):
                    ins = act.activation(alow[:, t * TC:(t + 1) * TC], G.ps[0:16, t, 0:TC], ACT.Copy)
                ins.then_inc(alow_ready, 1)
                G.split_hi(act, 2, 0, 1)

                def pair(i, first):
                    n = 2 * i + 1
                    link = linker(act, act_chain, i)
                    act.wait_ge(par_ready, i + 1)
                    for t in range(3):
                        act.wait_ge(lg_done, 3 * i + t + 1)
                        act.activation(ab[:, t * TC:(t + 1) * TC], G.ps[:, 6 + t % 2, 0:TC], ACT.Abs, bias=par[:])
                        act.activation(xg[:, t * TC:(t + 1) * TC], G.ps[:, 6 + t % 2, 0:TC], ACT.Identity, bias=par[:]
                                       ).then_inc(lg_read, 1)
                    act.wait_ge(lg_read, 3 * i + 3)
                    link(act.activation(ab[:], ab[:], ACT.Exp, scale=-1.0))
                    act.activation(ab[:], ab[:], ACT.Ln, bias=1.0).then_inc(soft_ready, 1)
                    G.split_hi(act, n + 2, 1, i + 1)
                    act.wait_ge(cent_ready, i + 1)
                    if not first:
                        act.wait_ge(qk_ready, 2 * i)
                    act.activation(eqf[:, 0:T], bsum[:], ACT.Exp, scale=1.0 / 16)
                    act.activation(S.gf[:, bass.ds(i, 1), :].rearrange("p o g -> p (o g)"), gt[:], ACT.Exp, scale=1.0 / 16)
                    act.activation(ekf[:, 0:T], bsum[:], ACT.Exp, scale=-1.0 / 16).then_inc(exps_ready, 1)
                    G.split_hi(act, n + 3, 0, i + 2)
                pair(0, True)
                pair(1, False)
                with act.Fori(1, 4) as hh:
                    for d in range(2):
                        pair(2 * hh + d, False)
                act.preload_act_table_set('sigmoid_and_others')

                def tile(g, h, d, tail):
                    s = n_slot(d)
                    n = C_V0 + 16 * g + 4 * h + d
                    act.wait_ge(G.gemm_done, n + 1)
                    act.wait_ge(spilled[s], 32 * (8 + 8 * g + 2 * h + d // 2))
                    if g == 0:
                        act.activation(stage[s][:], G.bank(s), ACT.Copy).then_inc(v_ready, 1)
                        act.wait_ge(v_ready, 4 * h + d + 1)
                        act.sem_inc(G.psum_free[s], 1)
                    else:
                        act.activation(stage[s][:], G.bank(s), ACT.Sigmoid).then_inc(sigmoid_ready, 1)
                    if not tail:
                        G.split_hi(act, n + 2, s, (C_V0 + 16 * g + d) // 2 + 1 + 2 * h)
                for g in range(2):
                    with act.Fori(0, 4 - g) as h:
                        for d in range(4):
                            tile(g, h, d, False)
                for d in range(4):
                    tile(1, 3, d, d >= 2)

            @block.vector
            def _(dve):
                dve.memset(eqf[:, T:TP], 0.0).then_inc(cleared, 1)
                dve.memset(ekf[:, T:TP], 0.0).then_inc(cleared, 1)
                dve.wait_ge(cleared, 2)
                dve.wait_ge(alow_ready, 1)
                dve.sem_inc(G.psum_free[0], 1)
                G.split_lo(dve, 2, 0)
                dve.tensor_copy(par[:], S.vecs[:, V_ALPHAB:V_ALPHAB + 1]).then_inc(par_ready, 1)
                K = 5

                def pair(i, first):
                    n = 2 * i + 1
                    link = linker(dve, dve_chain, K * i)
                    dve.wait_ge(soft_ready, i + 1)
                    link(dve.scalar_tensor_tensor(out=xg[:, 0:T], in0=xg[:, 0:T], scalar=0.0, in1=ab[:, 0:T],
                                                  op0=ALU.min, op1=ALU.subtract))
                    if not first:
                        dve.wait_ge(exps_ready, i)
                    link(dve.tensor_tensor_scan(bsum[:], S.reset[:], xg[:, 0:T], 0.0, ALU.mult, ALU.add))
                    link(dve.tensor_tensor(gt[:, 0:8], chunked(bsum)[:, :, P - 1], chunked(bsum)[:, :, P // 2 - 1], ALU.subtract))
                    link(dve.tensor_tensor(gt[:, 0:7], gt[:, 0:7], chunked(bsum)[:, 1:8, P // 2 - 1], ALU.add))
                    dve.tensor_copy(gt[:, 8:9], bsum[:, NP_TOK - 1:NP_TOK])
                    dve.tensor_copy(gt[:, 9:17], seqs(bsum)[:, :, SLEN - 1])
                    link(dve.tensor_copy(mid[:], chunked(bsum)[:, :, P // 2 - 1]))
                    assert link.count() == K
                    dve.tensor_tensor(chunked(bsum), chunked(bsum), mid[:].unsqueeze(2).to_broadcast([P, 8, P]), ALU.subtract
                                      ).then_inc(cent_ready, 1)
                    dve.tensor_copy(par[:], S.vecs[:, bass.ds(V_ALPHAB + 1 + i, 1)]).then_inc(par_ready, 1)
                    G.split_lo(dve, n + 2, 1)
                    dve.wait_ge(exps_ready, i + 1)
                    if not first:
                        dve.wait_ge(spilled[1], 32 * i)
                    dve.scalar_tensor_tensor(out=stage[1][:], in0=G.bank(1), scalar=DK ** -0.5, in1=eq[:],
                                             op0=ALU.mult, op1=ALU.mult).then_inc(qk_ready, 1)
                    dve.wait_ge(qk_ready, 2 * i + 1)
                    dve.sem_inc(G.psum_free[1], 1)
                    dve.wait_ge(G.gemm_done, n + 2)
                    if not first:
                        dve.wait_ge(spilled[0], 32 * i)
                    dve.tensor_tensor(stage[0][:], G.bank(0), ek[:], ALU.mult).then_inc(qk_ready, 1)
                    dve.wait_ge(qk_ready, 2 * i + 2)
                    dve.sem_inc(G.psum_free[0], 1)
                    G.split_lo(dve, n + 3, 0)

                pair(0, True)
                pair(1, False)
                with dve.Fori(1, 4) as hh:
                    for d in range(2):
                        pair(2 * hh + d, False)

                def tile(g, h, d, tail):
                    s = n_slot(d)
                    n = C_V0 + 16 * g + 4 * h + d
                    if g == 1:
                        dve.wait_ge(sigmoid_ready, 4 * h + d + 1)
                        dve.scalar_tensor_tensor(out=stage[s][:], in0=G.bank(s), scalar=S.vecs[:, bass.ds(V_GNORM + 4 * h + d, 1)],
                                                 in1=stage[s][:], op0=ALU.mult, op1=ALU.mult).then_inc(r_ready, 1)
                        dve.wait_ge(r_ready, 4 * h + d + 1)
                        dve.sem_inc(G.psum_free[s], 1)
                    if not tail:
                        G.split_lo(dve, n + 2, s)
                for g in range(2):
                    with dve.Fori(0, 4 - g) as h:
                        for d in range(4):
                            tile(g, h, d, False)
                for d in range(4):
                    tile(1, 3, d, d >= 2)

            @block.tensor
            def _(pe):
                def gate_round(i, t):
                    def go():
                        if t == 0:
                            pe.wait_ge(alow_ready, 1)
                            pe.wait_ge(a_up_in, 16 * i + 16)
                            if not (isinstance(i, int) and i == 0):
                                pe.wait_ge(lg_read, 3 * i)
                        if t == 2:
                            pe.wait_ge(lg_read, 3 * i + 1)
                        pe.matmul(G.ps[:, 6 + t % 2, 0:TC], a_up[:], alow[:, t * TC:(t + 1) * TC], start=True, stop=True
                                  ).then_inc(lg_done, 1)
                    return go

                def pair(i):
                    G.products(pe, 2 * i + 1, 1, i, {1: gate_round(i, 0), 2: gate_round(i, 1), 3: gate_round(i, 2)})
                    G.products(pe, 2 * i + 2, 0, i + 1, {})
                pair(0)
                pair(1)
                with pe.Fori(1, 4) as hh:
                    for d in range(2):
                        pair(2 * hh + d)
                with pe.Fori(0, 8) as h:
                    for d in range(4):
                        G.products(pe, C_V0 + 4 * h + d, n_slot(d), (C_V0 + d) // 2 + 2 * h, {})


def stage_mix_c(nc, S, scr_d, w_early, post_d, x_d, y_d, s0_d, out_sp, out_ss):
    with ExitStack() as ctx:
        a = make_alloc(nc, ctx)
        sem = S.a.sem
        O = OutProjection(S, a, "mc", w_early, None, list(range(16)), 1, x_d, y_d)
        hin = [a.sb(f"mc_hin{s}", [P, CF, P]) for s in range(2)]
        cst = a.sb("mc_state", [P, H, 2, GV])
        vv = [a.sb(f"mc_v{s}", [P, GV]) for s in range(2)]
        kk = [a.sb(f"mc_k{s}", [P, 256]) for s in range(2)]
        sc = [a.sb(f"mc_scores{s}", [P, P]) for s in range(2)]
        sc8 = a.sb("mc_scores_last", [LAST, LAST])
        gn = a.sb("mc_normed", [P, GV])
        mp = a.sb("mc_mix_plain", [P, GV])
        sm = a.sb("mc_small", [P, 4])
        gfc = a.sb("mc_factors", [P, 8])
        kw8 = a.sb("mc_group_keys", [LAST, 2, 256])
        qm = [a.sb(f"mc_q_masked{i}", [P, 2, 480]) for i in range(2)]
        cs = [a.sb(f"mc_sample_state{r}", [P, 2, GV]) for r in range(CRING - 2)]
        cs += [t[:, 0:2 * GV].rearrange("p (d v) -> p d v", d=2) for t in (O.xres, O.yb)]
        ps = a.ps("mc_ps", [P, 8, 512])

        hin_in = [sem(f"mc_hin_in{s}") for s in range(2)]
        r_in = [sem(f"mc_r_in{s}") for s in range(2)]
        init_done = sem("mc_init_done")
        turned = sem("mc_turned")
        v_ready = sem("mc_v_ready")
        sc_ready = sem("mc_scores_ready")
        b_done = sem("mc_products_done")
        added = sem("mc_state_added")
        gfc_ready = sem("mc_factors_ready")
        state_ready = sem("mc_state_ready")
        sq_chain = sem("mc_square_chain")
        gn_ready = sem("mc_normed_ready")
        c_done = sem("mc_head_turned")
        mp_ready = sem("mc_mix_plain_ready")
        mhi_ready = sem("mc_mix_hi_ready")
        mix_ready = sem("mc_mix_ready")
        qm_ready = sem("mc_q_masked_ready")
        s_in = [sem(f"mc_sample_in{r}") for r in range(CRING)]
        s_out = [sem(f"mc_sample_out{r}") for r in range(CRING)]
        upd_done = sem("mc_update_done")
        s_added = sem("mc_sample_added")
        s_ready = sem("mc_sample_ready")
        p_stored = sem("mc_prompt_state_stored")
        pool_chain = sem("mc_pool_chain")
        kw8_ready = sem("mc_group_keys_ready")

        def v_bank(h, rows):
            return 2 if rows == P else 3 - h % 2

        def o_bank(h, rows):
            return 3 if rows == P else 3 - h % 2

        with nc.Block() as block:
            @block.sync
            def _(sp):
                def load_head(n, c, h, rows, first=False):
                    piece = scr_d[bass.ds(c, 1), h, :, :, 0:rows].rearrange("o p f t -> (o p) f t")
                    if not first:
                        sp.wait_ge(b_done, n - 1)
                    sp.dma_start(hin[h % 2][:, 0:8, 0:rows], piece[:, 0:8, :]).then_inc(hin_in[h % 2], 16)
                    if not first:
                        sp.wait_ge(mp_ready, n - 1)
                    sp.dma_start(hin[h % 2][:, 8:12, 0:rows], piece[:, 8:12, :]).then_inc(r_in[h % 2], 16)
                load_head(0, 0, 0, P, True)
                load_head(1, 0, 1, P, True)
                O.load_post(sp, post_d)
                O.load_x(sp, 0, P, True)
                load_head(2, 0, 2, P)
                load_head(3, 0, 3, P)
                with sp.Fori(1, 8) as c:
                    for h in range(H):
                        load_head(4 * c + h, c, h, P)
                    O.store_y(sp, c - 1, P)
                    O.load_x(sp, c, P, False)
                load_head(32, 8, 0, LAST)
                load_head(33, 8, 1, LAST)

                def load_state(m):
                    r = m % CRING
                    if m >= CRING:
                        sp.wait_ge(s_out[r], 16 * (m // CRING))
                    sp.dma_start(cs[r][:], s0_d[m % NSEQ, m // NSEQ]).then_inc(s_in[r], 16)

                def store_state(m):
                    r = m % CRING
                    sp.wait_ge(s_ready, m + 1)
                    sp.dma_start(out_ss[m % NSEQ, m // NSEQ], cs[r][:]).then_inc(s_out[r], 16)
                for m in range(CRING - 2):
                    load_state(m)
                O.store_y(sp, 7, P)
                load_state(CRING - 2)
                sp.wait_ge(O.y_stored, 16 * NC)
                load_state(CRING - 1)
                for h in range(H):
                    for b in range(NSEQ):
                        m = h * NSEQ + b
                        store_state(m)
                        if m + CRING < H * NSEQ:
                            load_state(m + CRING)
                        if h in (1, 2) and b == 3:
                            load_head(33 + h, 8, 1 + h, LAST)
                    sp.wait_ge(state_ready, 32 + h + 1)
                    sp.dma_start(out_sp[h], cst[:, h, :, :]).then_inc(p_stored, 16)
                sp.wait_ge(s_out[CRING - 2], 16 * len(range(CRING - 2, H * NSEQ, CRING)))
                O.load_x(sp, 8, LAST, False)
                O.store_y(sp, 8, LAST)
                sp.wait_ge(O.y_stored, 16 * NC + 16)
                sp.wait_ge(p_stored, 16 * H)
                for r in range(CRING):
                    sp.wait_ge(s_out[r], 16 * len(range(r, H * NSEQ, CRING)))

            @block.tensor
            def _(pe):
                def part_a(n, c, h, rows):
                    s = h % 2
                    pe.wait_ge(hin_in[s], 16 * (2 * c + h // 2) + 16)
                    t = hin[s]
                    for d in range(2):
                        pe.transpose(ps[0:rows, 0, P + d * P:P + (d + 1) * P], t[:, 2 + d, 0:rows], S.ident[:])
                    for d in range(4):
                        pe.transpose(ps[0:rows, v_bank(h, rows), d * P:(d + 1) * P], t[:, 4 + d, 0:rows], S.ident[:])
                    for d in range(2):
                        ins = pe.matmul(ps[0:rows, 0, 0:rows], t[:, 2 + d, 0:rows], t[:, d, 0:rows], start=(d == 0), stop=(d == 1))
                    ins.then_inc(turned, 1)

                def part_b(n, h):
                    s = h % 2
                    pe.wait_ge(gn_ready, n)
                    pe.wait_ge(state_ready, n)
                    for d in range(2):
                        pe.matmul(ps[:, 3, :], hin[s][:, d, :], cst[:, h, d, :], start=(d == 0), stop=False)
                    pe.wait_ge(v_ready, n + 1)
                    pe.wait_ge(sc_ready, n + 1)
                    pe.matmul(ps[:, 3, :], sc[s][:], vv[s][:], start=False, stop=True)
                    for d in range(2):
                        ins = pe.matmul(ps[:, 4 + d, :], kk[s][:, d * P:(d + 1) * P], vv[s][:], start=True, stop=True)
                    ins.then_inc(b_done, 1)

                def part_c(n, rows):
                    pe.wait_ge(gn_ready, n + 1)
                    pe.wait_ge(mp_ready, n)
                    for d in range(4):
                        ins = pe.transpose(ps[:, 1, d * rows:(d + 1) * rows], gn[0:rows, d * P:(d + 1) * P], S.ident[0:rows, 0:rows])
                    ins.then_inc(c_done, 1)

                def out(c, h, new_w=False):
                    if h == 0:
                        pe.wait_ge(O.out_read, c)
                    pe.wait_ge(mix_ready, 4 * c + h + 1)
                    for e in range(4 * h, 4 * h + 4):
                        O.products(pe, ps, e, e == 0, e == 15, new_w)

                def chunk(c, first, last):
                    for h in range(H):
                        n = 4 * c + h
                        if not (last and h == 3):
                            part_a(n + 1, c + (h == 3), (h + 1) % H, P)
                        if not (first and h == 0):
                            out(c - (h == 0), (h - 1) % H, first)
                        part_c(n, P)
                        if not (last and h == 3):
                            part_b(n + 1, (h + 1) % H)
                pe.wait_ge(init_done, 1)
                part_a(0, 0, 0, P)
                part_b(0, 0)
                chunk(0, True, False)
                pe.wait_ge(O.w_ready, 16)
                with pe.Fori(1, 7) as c:
                    chunk(c, False, False)
                chunk(7, False, True)
                part_a(32, 8, 0, LAST)
                out(7, 3)
                for h in range(H):
                    n, s = 32 + h, h % 2
                    if h == 0:
                        pe.wait_ge(state_ready, n)
                    pe.wait_ge(qm_ready, h + 1)
                    pe.wait_ge(v_ready, n + 1)
                    for g in range(NG):
                        m = h * NSEQ + g - 1
                        r = m % CRING
                        if g:
                            pe.wait_ge(s_in[r], 16 * (m // CRING) + 16)
                        for d in range(2):
                            st = cst[:, h, d, :] if g == 0 else cs[r][:, d, :]
                            pe.matmul(ps[0:LAST, o_bank(h, LAST), :], qm[s][:, d, g * LAST:(g + 1) * LAST], st,
                                      start=(g == 0 and d == 0), stop=False)
                        u = h * NG + g
                        if u >= 2:
                            pe.wait_ge(s_added, u - 1)
                        if u == 1:
                            pe.wait_ge(O.out_read, 8)
                        pe.wait_ge(kw8_ready, u + 1)
                        for d in range(2):
                            ins = pe.matmul(ps[:, 4 + 2 * (u % 2) + d, :], kw8[:, u % 2, d * P:(d + 1) * P],
                                            vv[s][0:LAST, :], start=True, stop=True)
                        ins.then_inc(upd_done, 1)
                        if h and g == 2:
                            part_c(n - 1, LAST)
                    pe.wait_ge(sc_ready, n + 1)
                    pe.matmul(ps[0:LAST, o_bank(h, LAST), :], sc8[:], vv[s][0:LAST, :], start=False, stop=True).then_inc(b_done, 1)
                    if h < 3:
                        part_a(n + 1, 8, h + 1, LAST)
                part_c(35, LAST)
                pe.wait_ge(s_added, H * NG)
                for h in range(H):
                    out(8, h)

            @block.scalar
            def _(act):
                act.preload_act_table_set('natural_log_exp_and_others')

                def part_a(n, s, rows, first=False, v_in=2):
                    act.wait_ge(turned, n + 1)
                    if not first:
                        act.wait_ge(b_done, n - 1)
                    act.activation(vv[s][0:rows, :], ps[0:rows, v_in, :], ACT.Copy).then_inc(v_ready, 1)

                def norm(n, rows, o_in=3):
                    act.wait_ge(b_done, n + 1)
                    act.activation(gn[0:rows, :], ps[0:rows, o_in, :], ACT.Square, accum_out=sm[0:rows, 0:1]).then_inc(sq_chain, 1)
                    act.wait_ge(sq_chain, 3 * n + 1)
                    act.activation(sm[0:rows, 1:2], sm[0:rows, 0:1], ACT.Ln, scale=1.0 / GV, bias=S.eps[0:rows, :]).then_inc(sq_chain, 1)
                    act.wait_ge(sq_chain, 3 * n + 2)
                    act.activation(sm[0:rows, 2:3], sm[0:rows, 1:2], ACT.Exp, scale=-0.5).then_inc(sq_chain, 1)
                    act.wait_ge(sq_chain, 3 * n + 3)
                    act.activation(gn[0:rows, :], ps[0:rows, o_in, :], ACT.Copy, scale=sm[0:rows, 2:3]).then_inc(gn_ready, 1)

                def part_m(n, c, h, rows):
                    act.wait_ge(mp_ready, n + 1)
                    act.wait_ge(O.out_done, c)
                    act.activation(O.m_hi[:, 4 * h:4 * h + 4, 0:rows], mp[:, 0:4 * rows].rearrange("p (d t) -> p d t", d=4), ACT.Copy
                                   ).then_inc(mhi_ready, 1)

                def chunk(c, first, last):
                    for h in range(H):
                        n = 4 * c + h
                        norm(n, P)
                        if not (last and h == 3):
                            part_a(n + 1, (h + 1) % 2, P, first and h == 0)
                        if first:
                            O.split_w_hi(act, h)
                        if h == 0 and not first:
                            O.post_act(act, ps, c - 1, P)
                        part_m(n, c, h, P)
                part_a(0, 0, P, True)
                chunk(0, True, False)
                with act.Fori(1, 7) as c:
                    chunk(c, False, False)
                chunk(7, False, True)
                part_a(32, 0, LAST, v_in=v_bank(0, LAST))
                O.post_act(act, ps, 7, P)
                for h in range(H):
                    n = 32 + h
                    for g in range(1, NG):
                        m = h * NSEQ + g - 1
                        act.wait_ge(s_added, h * NG + g + 1)
                        for d in range(2):
                            ins = act.activation(cs[m % CRING][:, d, :], cs[m % CRING][:, d, :], ACT.Copy,
                                                 scale=S.gf[:, 2 * h + d, 8 + g:9 + g])
                        ins.then_inc(s_ready, 1)
                        if h and g == 3:
                            part_m(n - 1, 8, h - 1, LAST)
                    if h < 3:
                        part_a(n + 1, (h + 1) % 2, LAST, v_in=v_bank(h + 1, LAST))
                    norm(n, LAST, o_bank(h, LAST))
                part_m(35, 8, 3, LAST)
                act.wait_ge(s_out[CRING - 1], 16 * len(range(CRING - 1, H * NSEQ, CRING)))
                O.post_act(act, ps, 8, LAST)

            @block.vector
            def _(dve):
                dve.memset(sc[0][:], 0.0)
                dve.memset(sc[1][:], 0.0)
                dve.memset(sc8[:], 0.0)
                dve.memset(cst[:], 0.0).then_inc(init_done, 1)

                def part_a(n, s, rows, first=False):
                    dve.wait_ge(turned, n + 1)
                    if not first:
                        dve.wait_ge(b_done, n - 1)
                    dve.tensor_copy(kk[s][0:rows, :], ps[0:rows, 0, P:P + 256])
                    dst, mask = (sc[s], S.mask_one) if rows == P else (sc8, S.mask_one8)
                    dve.copy_predicated(dst[:], mask[:].bitcast(mybir.dt.uint32), ps[0:rows, 0, 0:rows]).then_inc(sc_ready, 1)

                def add_state(dst, bank):
                    for d in range(2):
                        ins = dve.tensor_tensor(dst[:, d, :], ps[:, bank + d, :], dst[:, d, :], ALU.add)
                    return ins

                def part_m(n, c, h, s, rows):
                    dve.wait_ge(c_done, n + 1)
                    dve.wait_ge(r_in[s], 16 * (2 * c + h // 2) + 16)
                    dve.wait_ge(mix_ready, n)
                    dve.tensor_tensor(mp[:, 0:4 * rows].rearrange("p (d t) -> p d t", d=4),
                                      ps[:, 1, 0:4 * rows].rearrange("p (d t) -> p d t", d=4), hin[s][:, 8:12, 0:rows],
                                      ALU.mult).then_inc(mp_ready, 1)

                def chunk(c, first, last):
                    for h in range(H):
                        n = 4 * c + h
                        dve.wait_ge(b_done, n + 1)
                        add_state(cst[:, h, :, :], 4).then_inc(added, 1)
                        if not (last and h == 3):
                            part_a(n + 1, (h + 1) % 2, P, first and h == 0)
                        if first:
                            O.split_w_lo(dve, h)
                        part_m(n, c, h, h % 2, P)
                        if h == 0 and not first:
                            O.post_dve(dve, ps, c - 1, P)
                part_a(0, 0, P, True)
                chunk(0, True, False)
                with dve.Fori(1, 7) as c:
                    chunk(c, False, False)
                chunk(7, False, True)

                def group_keys(u, g):
                    if u >= 2:
                        dve.wait_ge(upd_done, u - 1)
                    mask = S.tail_mask[:] if g == 0 else S.seq_mask[:, g - 1:g]
                    dve.tensor_scalar(kw8[:, u % 2, :], ps[0:LAST, 0, P:P + 256], mask, None, ALU.mult).then_inc(kw8_ready, 1)
                part_a(32, 0, LAST)
                group_keys(0, 0)
                group_keys(1, 1)
                O.post_dve(dve, ps, 7, P)
                for h in range(H):
                    n, s = 32 + h, h % 2
                    for g in range(NG + 1):
                        u = h * NG + g
                        if g < NG and u >= 2:
                            group_keys(u, g)
                        if g:
                            u -= 1
                            dve.wait_ge(upd_done, u + 1)
                            dst = cst[:, h, :, :] if g == 1 else cs[(h * NSEQ + g - 2) % CRING]
                            add_state(dst, 4 + 2 * (u % 2)).then_inc(s_added, 1)
                        if h and g == 4:
                            part_m(n - 1, 8, h - 1, 1 - s, LAST)
                    if h < 3:
                        part_a(n + 1, 1 - s, LAST)
                part_m(35, 8, 3, 1, LAST)
                O.post_dve(dve, ps, 8, LAST)

            @block.gpsimd
            def _(pool):
                link = linker(pool, pool_chain)
                for i in range(2):
                    link(pool.memset(qm[i][:], 0.0))

                def take_factors(c):
                    if not (isinstance(c, int) and c == 0):
                        pool.wait_ge(state_ready, 4 * c)
                    pool.tensor_copy(gfc[:], S.gf[:, :, bass.ds(c, 1)].rearrange("p t o -> p (t o)")).then_inc(gfc_ready, 1)
                    pool.wait_ge(gfc_ready, c + 1)

                def scale_state(h):
                    for d in range(2):
                        factor = gfc[:, 2 * h + d:2 * h + d + 1].to_broadcast([P, GV])
                        ins = pool.tensor_tensor(cst[:, h, d, :], cst[:, h, d, :], factor, ALU.mult)
                    ins.then_inc(state_ready, 1)

                def lo(n, h, rows):
                    pool.wait_ge(mhi_ready, n + 1)
                    tiles = slice(4 * h, 4 * h + 4)
                    pool.tensor_tensor(O.m_lo[:, tiles, 0:rows], mp[:, 0:4 * rows].rearrange("p (d t) -> p d t", d=4),
                                       O.m_hi[:, tiles, 0:rows].bitcast(F32), ALU.subtract).then_inc(mix_ready, 1)

                def chunk(c, first):
                    take_factors(c)
                    for h in range(H):
                        n = 4 * c + h
                        pool.wait_ge(added, n + 1)
                        scale_state(h)
                        lo(n, h, P)
                        if h == 0 and not first:
                            O.post_pool(pool, c - 1, P)
                chunk(0, True)
                with pool.Fori(1, 8) as c:
                    chunk(c, False)
                take_factors(8)

                def masked_q(h):
                    pool.wait_ge(hin_in[h % 2], 16 * (16 + h // 2) + 16)
                    if h >= 2:
                        pool.wait_ge(upd_done, NG * (h - 1))
                    for d in range(2):
                        q = hin[h % 2][:, d, :]
                        pool.tensor_copy(qm[h % 2][:, d, 0:TAIL], q[:, 0:TAIL])
                        ins = pool.tensor_copy(qm[h % 2][:, d, 64:480].rearrange("p (s r) -> p s r", r=LAST + SLEN)[:, :, 0:SLEN],
                                               q[:, TAIL:LAST].rearrange("p (s t) -> p s t", t=SLEN))
                    ins.then_inc(qm_ready, 1)
                masked_q(0)
                O.post_pool(pool, 7, P)
                masked_q(1)
                for h in range(H):
                    pool.wait_ge(s_added, NG * h + 1)
                    scale_state(h)
                    lo(32 + h, h, LAST)
                    if h < 2:
                        masked_q(h + 2)
                O.post_pool(pool, 8, LAST)


CRING = 5


def build_program(nc, io):
    with ExitStack() as ctx:
        S = Names()
        S.a = make_alloc(nc, ctx)
        sb = S.a.sb
        S.vecs = sb("vecs", [P, NVEC])
        S.derived = sb("derived", [P, 2, 8])
        S.eps = sb("eps", [P, 1])
        S.tiny = sb("tiny", [P, 1])
        S.ident = sb("ident", [P, P])
        S.sel = sb("sel", [H, H, P])
        S.mask_add = sb("mask_add", [P, P])
        S.mask_one = sb("mask_one", [P, P])
        S.mask_add8 = sb("mask_add8", [LAST, LAST])
        S.mask_one8 = sb("mask_one8", [LAST, LAST])
        S.seq_mask = sb("seq_mask", [LAST, NSEQ])
        S.tail_mask = sb("tail_mask", [LAST, 1])
        stage_constants(nc, S, io["vecs"])
        scr_a = nc.dram_tensor("scr_a", [NC, H, P, AF, P], F32, kind="Internal").ap()
        scr_l = nc.dram_tensor("scr_l", [NC, P, 8, P], F32, kind="Internal").ap()
        with ExitStack() as actx:
            la = make_alloc(nc, actx)
            S.wc = la.sb("wc", [P, H, 17])
            S.tok = la.sb("tok", [P, NC, 3, H])
            S.rrow = la.sb("rrow", [H, T])
            raw_rows = ExitStack()
            w_early = OutWeights(S, make_alloc(nc, raw_rows), "wout_a_early", io["w_oa"], 8, 8)
            with ExitStack() as xctx:
                xa = make_alloc(nc, xctx)
                S.reset = xa.sb("a_reset", [P, T])
                S.XT_hi = xa.sb("a_XT_hi", [P, KT, TP], F32R)
                S.XT_lo = xa.sb("a_XT_lo", [P, KT, TP], F32R)
                G = Projection(S, xa, "pa", io["w_a"])
                stage_norm(nc, S, G, "na", io["x"], V_PRE_A)
                stage_project_a(nc, S, G, io["lru_w"], io["conv0"], io["h0"], scr_a, scr_l, io["m0"],
                                io["conv_p"], io["conv_s"], io["h_p"], io["h_s"], io["m_out"], w_early)
            scr_y = nc.dram_tensor("scr_y", [T, D], F32, kind="Internal").ap()
            w_late = OutWeights(S, make_alloc(nc, raw_rows), "wout_a_late", io["w_oa"], 0, 8)
            raw_rows.close()
            stage_mix_a(nc, S, scr_a, scr_l, w_early, w_late, io["post"], io["x"], scr_y, io["c0"], io["c_p"], io["c_s"])
        clear_semaphores(nc, S.a)
        with ExitStack() as cctx:
            lc = make_alloc(nc, cctx)
            S.gf = lc.sb("gf", [P, 8, 17])
            scr_c = nc.dram_tensor("scr_c", [NC, H, P, CF, P], F32, kind="Internal").ap()
            raw_rows = ExitStack()
            w_out = OutWeights(S, make_alloc(nc, raw_rows), "wout_c", io["w_oc"], 0, 16)
            with ExitStack() as xctx:
                xa = make_alloc(nc, xctx)
                S.reset = xa.sb("c_reset", [P, T])
                S.XT_hi = xa.sb("c_XT_hi", [P, KT, TP], F32R)
                S.XT_lo = xa.sb("c_XT_lo", [P, KT, TP], F32R)
                G = Projection(S, xa, "pc", io["w_c"])
                stage_norm(nc, S, G, "nc", scr_y, V_PRE_C)
                stage_project_c(nc, S, G, io["a_up"], scr_c, w_out)
            raw_rows.close()
            stage_mix_c(nc, S, scr_c, w_out, io["post"], scr_y, io["y"], io["s0"], io["s_p"], io["s_s"])


def _features(v, n):
    return v.reshape(n, P).T


def _tiles(w, columns):
    import numpy as np
    wz = np.concatenate([w, np.zeros((w.shape[0], 1), w.dtype)], axis=1)
    t = wz[:, columns].reshape(KT, P, -1, P)
    return t.transpose(2, 1, 0, 3)


def lay_out(i):
    import numpy as np
    r = np.arange
    none = -np.ones(P, np.int64)
    gates = none.copy()
    gates[0:4], gates[32:36] = r(4096, 4100), r(4100, 4104)
    cols = [gates]
    for t in range(8):
        cols += [5128 + P * t + r(P), 6152 + P * t + r(P)]
    cols += [r(0, 4096), r(4104, 5128)]
    alow = none.copy()
    alow[0:16] = r(6144, 6160)
    ccols = [alow]
    for t in range(8):
        ccols += [P * t + r(P), 1024 + P * t + r(P)]
    ccols += [r(2048, 6144)]
    vecs = [_features(i["pre_norm_a"][0], 8), _features(i["pre_norm_c"][0], 8)]
    vecs += [_features(i["conv_w"][0, j], 8) for j in range(4)]
    vecs += [_features(i[k][0], n) for k, n in (("conv_b", 8), ("lru_b_a", 8), ("lru_b_x", 8), ("lru_lambda", 8),
                                                ("mlstm_norm", 8), ("gla_norm", 16), ("gla_alpha_b", 8))]
    gb = np.zeros((P, 1), np.float32)
    gb[0:4, 0], gb[32:36, 0] = i["mlstm_b_i"][0], i["mlstm_b_f"][0]
    vecs.append(gb)
    c = i["state_mlstm_C"][0].transpose(0, 1, 3, 2)
    caug = np.concatenate([c, i["state_mlstm_n"][0][..., None]], axis=-1)
    return {
        "x": np.concatenate([i["meta_tokens"], i["x_prompt"][0], i["x_sample"].reshape(-1, D)], axis=0),
        "vecs": np.concatenate(vecs, axis=1),
        "w_a": _tiles(i["w_in_a"][0], np.concatenate(cols)),
        "w_c": _tiles(i["w_in_c"][0], np.concatenate(ccols)),
        "lru_w": np.stack([i["lru_w_a"][0], i["lru_w_x"][0]], axis=2),
        "conv0": i["state_rglru_conv"][0].reshape(NSEQ, 3, 8, P).transpose(3, 2, 0, 1),
        "h0": i["state_rglru_h"][0].reshape(NSEQ, 8, P).transpose(2, 1, 0),
        "m0": i["state_mlstm_m"][0].T,
        "c0": caug.reshape(NSEQ, H, 2, P, MV).transpose(0, 1, 3, 2, 4),
        "s0": i["state_gla_S"][0].reshape(NSEQ, H, 2, P, GV).transpose(0, 1, 3, 2, 4),
        "w_oa": i["w_out_a"][0].reshape(16, P, D).transpose(1, 0, 2),
        "w_oc": i["w_out_c"][0].reshape(16, P, D).transpose(1, 0, 2),
        "post": np.stack([np.broadcast_to(i["post_norm_a"][0], (P, D)), np.broadcast_to(i["post_norm_c"][0], (P, D))], axis=1),
        "a_up": i["gla_alpha_up"][0].reshape(16, 8, P),
    }


OUTS = {
    "y": (T, D), "conv_p": (P, 8, 3), "conv_s": (P, 8, NSEQ, 3), "h_p": (P, 8), "h_s": (P, 8, NSEQ), "m_out": (H, 9),
    "c_p": (H, P, 2, MV), "c_s": (NSEQ, H, P, 2, MV), "s_p": (H, P, 2, GV), "s_s": (NSEQ, H, P, 2, GV),
}


def take_out(o):
    import numpy as np
    y = o["y"]

    def c_state(c):
        c = np.moveaxis(c, -2, -3)
        c = c.reshape(c.shape[:-3] + (DK, MV))
        return np.ascontiguousarray(np.swapaxes(c[..., 0:DK], -1, -2)), np.ascontiguousarray(c[..., DK])

    def s_state(c):
        c = np.moveaxis(c, -2, -3)
        return c.reshape(c.shape[:-3] + (DK, GV))
    pc, pn = c_state(o["c_p"])
    sc, sn = c_state(o["c_s"])
    con = np.ascontiguousarray
    return (
        con(y[16:NP_TOK][None]), con(y[NP_TOK:].reshape(NSEQ, SLEN, D)),
        pc[None, None], pn[None, None], con(o["m_out"][:, 0][None, None]),
        con(o["h_p"].T.reshape(1, 1, D)), con(o["conv_p"].transpose(2, 1, 0).reshape(1, 1, 3, D)), con(s_state(o["s_p"])[None, None]),
        sc[None], sn[None], con(o["m_out"][:, 1:].T[None]),
        con(o["h_s"].transpose(2, 1, 0).reshape(1, NSEQ, D)), con(o["conv_s"].transpose(2, 3, 1, 0).reshape(1, NSEQ, 3, D)),
        con(s_state(o["s_s"])[None]),
    )


def kernel(**inputs):
    import numpy as _np
    import concourse.bacc as _bacc
    from concourse.bass_utils import run_bass_kernel_spmd as _run

    nc = _bacc.Bacc("TRN2", target_bir_lowering=False, num_devices=1,
                    dynamic_dma_scratch_size=1024)
    arrays = {k: _np.ascontiguousarray(v) for k, v in lay_out({k: _np.asarray(v) for k, v in inputs.items()}).items()}
    io = {k: nc.dram_tensor("in_" + k, v.shape, F32, kind="ExternalInput").ap() for k, v in arrays.items()}
    for k, shape in OUTS.items():
        io[k] = nc.dram_tensor("out_" + k, shape, F32, kind="ExternalOutput").ap()
    build_program(nc, io)
    r = _run(nc, [{"in_" + k: v for k, v in arrays.items()}], core_ids=[0])
    return take_out({k: r.results[0]["out_" + k] for k in OUTS})
```
